# Optimizing a Trainium2 kernel written in Bass

```python
import math
import jax
import jax.numpy as jnp
from jax import lax
import numpy as np

D_MODEL = 1024
BATCH = 1
SEQ = 512
DEPTH = 1

GRID_W = 64
CTX_LEN = 256
EPS = 1e-6
ROPE_BASE = 10000.0

RET_HEADS = 4
RET_DK = 128
RET_DV = 256
RET_CHUNK = 128
RET_QK_W = RET_HEADS * RET_DK
RET_V_W = RET_HEADS * RET_DV

DIFF_HEADS = 8
DIFF_D = 64
DIFF_QK_W = DIFF_HEADS * 2 * DIFF_D
DIFF_V_W = DIFF_HEADS * 2 * DIFF_D
Q_BLOCK = 128

IN_WIDTHS = (RET_QK_W, RET_QK_W, RET_V_W, RET_V_W, DIFF_QK_W, DIFF_QK_W, DIFF_V_W, D_MODEL, D_MODEL)
IN_COLS = 2 * RET_QK_W + 2 * RET_V_W + 2 * DIFF_QK_W + DIFF_V_W + 2 * D_MODEL

PEER_HEADS = 8
PEER_NKEYS = 128
PEER_EXPERTS = PEER_NKEYS * PEER_NKEYS
PEER_DKEY = 256
PEER_HALF = PEER_DKEY // 2
PEER_TOPK = 16
PEER_TOK_BLOCK = 128

kernel_name = 'hybrid_retention_diffattn_peer_dit_block'

def rmsnorm(x, g):
    xf = x.astype(jnp.float32)
    y = xf * lax.rsqrt(jnp.mean(xf * xf, axis=-1, keepdims=True) + EPS)
    return (y * g.astype(jnp.float32)).astype(x.dtype)

def modulate(h, shift, scale):
    return h * (1 + scale) + shift

def modulation(cvec, w, b):
    m = jax.nn.silu(cvec) @ w + b
    return [t[:, None, :] for t in jnp.split(m, 6, axis=-1)]

def split_cols(p):
    outs, off = [], 0
    for w in IN_WIDTHS:
        outs.append(p[..., off:off + w])
        off += w
    return outs

def rope_1d(x, pos):
    half = x.shape[-1] // 2
    inv = ROPE_BASE ** (-jnp.arange(half, dtype=jnp.float32) / half)
    ang = pos[:, None] * inv[None, :]
    cos = jnp.cos(ang).astype(x.dtype)
    sin = jnp.sin(ang).astype(x.dtype)
    x1, x2 = x[..., :half], x[..., half:]
    return jnp.concatenate([x1 * cos - x2 * sin, x1 * sin + x2 * cos], axis=-1)

def axial_rope(x, row, col):
    h = x.shape[-1] // 2
    return jnp.concatenate([rope_1d(x[..., :h], row), rope_1d(x[..., h:], col)], axis=-1)

def heads(p, h):
    B, T, _ = p.shape
    return p.reshape(B, T, h, -1).transpose(0, 2, 1, 3)

def diff_heads(p):
    B, T, _ = p.shape
    return p.reshape(B, T, DIFF_HEADS, 2, DIFF_D).transpose(0, 2, 3, 1, 4)

def flip_t(t):
    return jnp.flip(t, axis=2)

def decay_logs(log2_decay):
    return jnp.log1p(-jnp.exp2(log2_decay.astype(jnp.float32)))

def retention_scan(q, k, v, log2_decay, s0, include_diag):
    B, H, T, DK = q.shape
    DV = v.shape[-1]
    C = RET_CHUNK
    n = T // C
    log_g = decay_logs(log2_decay)
    idx = jnp.arange(C, dtype=jnp.float32)
    dist = idx[:, None] - idx[None, :]
    mask = dist >= 0 if include_diag else dist > 0
    dmat = jnp.where(mask[None], jnp.exp(log_g[:, None, None] * jnp.where(mask, dist, 0.0)[None]), 0.0)
    q_dec = jnp.exp(log_g[:, None] * (idx + 1.0))[None, :, :, None]
    k_dec = jnp.exp(log_g[:, None] * (C - 1.0 - idx))[None, :, :, None]
    s_dec = jnp.exp(log_g * C)[None, :, None, None]

    def chunks(t):
        return jnp.moveaxis(t.astype(jnp.float32).reshape(B, H, n, C, t.shape[-1]), 2, 0)

    def step(s, inp):
        qi, ki, vi = inp
        att = jnp.einsum('bhid,bhjd->bhij', qi, ki) * dmat
        y = jnp.einsum('bhij,bhjv->bhiv', att, vi) + jnp.einsum('bhid,bhdv->bhiv', qi * q_dec, s)
        s = s_dec * s + jnp.einsum('bhjd,bhjv->bhdv', ki * k_dec, vi)
        return s, y

    s_fin, ys = lax.scan(step, s0, (chunks(q), chunks(k), chunks(v)))
    return jnp.moveaxis(ys, 0, 2).reshape(B, H, T, DV), s_fin

def retention_state(k, v, log2_decay):
    T = k.shape[2]
    log_g = decay_logs(log2_decay)
    w = jnp.exp(log_g[:, None] * (T - 1.0 - jnp.arange(T, dtype=jnp.float32)))
    return jnp.einsum('bhtd,bhtv->bhdv', k.astype(jnp.float32) * w[None, :, :, None], v.astype(jnp.float32))

def bidir_retention(q, k, v, dec_f, dec_b, s_f, s_b):
    y_f, sf_fin = retention_scan(q, k, v, dec_f, s_f, True)
    y_b, sb_fin = retention_scan(flip_t(q), flip_t(k), flip_t(v), dec_b, s_b, False)
    return y_f + flip_t(y_b), sf_fin, sb_fin

def retention_out(y, g_pre, gn_g, w_br, dtype):
    B, H, T, DV = y.shape
    mu = jnp.mean(y, axis=-1, keepdims=True)
    var = jnp.var(y, axis=-1, keepdims=True)
    yn = ((y - mu) * lax.rsqrt(var + EPS)).transpose(0, 2, 1, 3).reshape(B, T, H * DV)
    yn = (yn * gn_g.astype(jnp.float32)).astype(dtype)
    return (jax.nn.silu(g_pre) * yn) @ w_br

def diff_lambda_value(lp, lam_init):
    lp = lp.astype(jnp.float32)
    return jnp.exp(jnp.sum(lp[0] * lp[1])) - jnp.exp(jnp.sum(lp[2] * lp[3])) + lam_init

def diff_attention(q, k, v, lam):
    s = jnp.einsum('bhaqd,bhakd->bhaqk', q, k).astype(jnp.float32) * (DIFF_D ** -0.5)
    p = jax.nn.softmax(s, axis=-1)
    a = p[:, :, 0] - lam * p[:, :, 1]
    return jnp.einsum('bhqk,bhkv->bhqv', a, v.astype(jnp.float32))

def diff_attention_blocks(q, k, v, lam):
    B, H, _, T, d = q.shape
    nb = T // Q_BLOCK
    qb = jnp.moveaxis(q.reshape(B, H, 2, nb, Q_BLOCK, d), 3, 0)
    o = lax.map(lambda qi: diff_attention(qi, k, v, lam), qb)
    return jnp.moveaxis(o, 0, 2).reshape(B, H, T, v.shape[-1])

def diff_out(o, gn_g, lam_init, w_br, dtype):
    B, H, T, DV = o.shape
    on = o * lax.rsqrt(jnp.mean(o * o, axis=-1, keepdims=True) + EPS) * (1.0 - lam_init)
    on = on.transpose(0, 2, 1, 3).reshape(B, T, H * DV) * gn_g.astype(jnp.float32)
    return on.astype(dtype) @ w_br

def peer_ffn(h, w_q, sub_keys, u_tab, v_tab):
    B, T, D = h.shape
    nb = (B * T) // PEER_TOK_BLOCK
    hb = h.reshape(nb, PEER_TOK_BLOCK, D)
    E = PEER_HEADS * PEER_TOPK

    def block(xb):
        q = (xb @ w_q).reshape(PEER_TOK_BLOCK, PEER_HEADS, 2, PEER_HALF)
        sc = jnp.einsum('thad,hakd->thak', q, sub_keys).astype(jnp.float32)
        s_top, i_top = lax.top_k(sc, PEER_TOPK)
        cand_s = (s_top[:, :, 0, :, None] + s_top[:, :, 1, None, :]).reshape(PEER_TOK_BLOCK, PEER_HEADS, PEER_TOPK * PEER_TOPK)
        cand_i = (i_top[:, :, 0, :, None] * PEER_NKEYS + i_top[:, :, 1, None, :]).reshape(PEER_TOK_BLOCK, PEER_HEADS, PEER_TOPK * PEER_TOPK)
        s_fin, pos = lax.top_k(cand_s, PEER_TOPK)
        idx = jnp.take_along_axis(cand_i, pos, axis=-1).reshape(PEER_TOK_BLOCK, E)
        g = jax.nn.softmax(s_fin, axis=-1).reshape(PEER_TOK_BLOCK, E)
        act = jax.nn.gelu(jnp.einsum('td,ted->te', xb, u_tab[idx]).astype(jnp.float32), approximate=False)
        return jnp.einsum('te,ted->td', (g * act).astype(xb.dtype), v_tab[idx])

    return lax.map(block, hb).reshape(B, T, D)

def setup_inputs(seed: int = 0) -> dict:
    key = jax.random.key(seed)
    ks = jax.random.split(key, 23)
    f32 = jnp.float32

    def nrm(k, shape, s):
        return jax.random.normal(k, shape, f32) * s

    def gain(k, shape):
        return 1.0 + 0.05 * jax.random.normal(k, shape, f32)

    decay_base = -5.0 - jnp.arange(RET_HEADS, dtype=f32)
    return {
        'x': nrm(ks[0], (BATCH, SEQ, D_MODEL), 1.0),
        'c': nrm(ks[1], (BATCH, D_MODEL), 1.0),
        'ctx': nrm(ks[2], (BATCH, CTX_LEN, D_MODEL), 1.0),
        'c_ctx': nrm(ks[3], (D_MODEL,), 1.0),
        'w_mod': nrm(ks[4], (DEPTH, D_MODEL, 6 * D_MODEL), 0.5 * D_MODEL ** -0.5),
        'b_mod': nrm(ks[5], (DEPTH, 6 * D_MODEL), 0.02),
        'pre_mix_g': gain(ks[6], (DEPTH, D_MODEL)),
        'post_mix_g': gain(ks[7], (DEPTH, D_MODEL)),
        'pre_ffn_g': gain(ks[8], (DEPTH, D_MODEL)),
        'post_ffn_g': gain(ks[9], (DEPTH, D_MODEL)),
        'w_in': nrm(ks[10], (DEPTH, D_MODEL, IN_COLS), D_MODEL ** -0.5),
        'ret_decay_fwd': decay_base[None] + nrm(ks[11], (DEPTH, RET_HEADS), 0.1),
        'ret_decay_bwd': decay_base[None] + nrm(ks[12], (DEPTH, RET_HEADS), 0.1),
        'ret_gn_g': gain(ks[13], (DEPTH, RET_V_W)),
        'diff_lambda': nrm(ks[14], (DEPTH, 4, DIFF_D), 0.1),
        'diff_gn_g': gain(ks[15], (DEPTH, DIFF_V_W)),
        'w_br_ret': nrm(ks[16], (DEPTH, RET_V_W, D_MODEL), RET_V_W ** -0.5),
        'w_br_diff': nrm(ks[17], (DEPTH, DIFF_V_W, D_MODEL), DIFF_V_W ** -0.5),
        'w_out': nrm(ks[18], (DEPTH, D_MODEL, D_MODEL), D_MODEL ** -0.5),
        'peer_w_q': nrm(ks[19], (DEPTH, D_MODEL, PEER_HEADS * PEER_DKEY), D_MODEL ** -0.5),
        'peer_sub_keys': nrm(ks[20], (DEPTH, PEER_HEADS, 2, PEER_NKEYS, PEER_HALF), PEER_HALF ** -0.5),
        'peer_u': nrm(ks[21], (DEPTH, PEER_EXPERTS, D_MODEL), D_MODEL ** -0.5),
        'peer_v': nrm(ks[22], (DEPTH, PEER_EXPERTS, D_MODEL), D_MODEL ** -0.5),
    }

def reference(x, c, ctx, c_ctx, w_mod, b_mod, pre_mix_g, post_mix_g, pre_ffn_g, post_ffn_g,
              w_in, ret_decay_fwd, ret_decay_bwd, ret_gn_g, diff_lambda, diff_gn_g,
              w_br_ret, w_br_diff, w_out, peer_w_q, peer_sub_keys, peer_u, peer_v):
    B, n_lat, _ = x.shape
    rows = n_lat // GRID_W
    row = jnp.repeat(jnp.arange(rows, dtype=jnp.float32), GRID_W)
    col = jnp.tile(jnp.arange(GRID_W, dtype=jnp.float32), rows)
    q_scale = RET_DK ** -0.5
    xc = ctx
    for l in range(DEPTH):
        last = l == DEPTH - 1
        lam_init = 0.8 - 0.6 * math.exp(-0.3 * l)
        lam = diff_lambda_value(diff_lambda[l], lam_init)
        sh_a, sc_a, ga_a, sh_f, sc_f, ga_f = modulation(c, w_mod[l], b_mod[l])
        csh_a, csc_a, cga_a, csh_f, csc_f, cga_f = modulation(c_ctx[None], w_mod[l], b_mod[l])

        u = modulate(rmsnorm(x, pre_mix_g[l]), sh_a, sc_a)
        uc = modulate(rmsnorm(xc, pre_mix_g[l]), csh_a, csc_a)
        rq, rk, rv, rg, dq, dk, dv, gr, gd = split_cols(u @ w_in[l])
        rq_c, rk_c, rv_c, rg_c, dq_c, dk_c, dv_c, gr_c, gd_c = split_cols(uc @ w_in[l])

        qr = axial_rope(heads(rq, RET_HEADS), row, col) * q_scale
        kr = axial_rope(heads(rk, RET_HEADS), row, col)
        vr = heads(rv, RET_HEADS)
        kr_c = heads(rk_c, RET_HEADS)
        vr_c = heads(rv_c, RET_HEADS)
        if last:
            s_f = retention_state(kr_c, vr_c, ret_decay_fwd[l])
            s_b = retention_state(flip_t(kr_c), flip_t(vr_c), ret_decay_bwd[l])
        else:
            zero = jnp.zeros((B, RET_HEADS, RET_DK, RET_DV), jnp.float32)
            qr_c = heads(rq_c, RET_HEADS) * q_scale
            yr_c, s_f, s_b = bidir_retention(qr_c, kr_c, vr_c, ret_decay_fwd[l], ret_decay_bwd[l], zero, zero)
        yr, _, _ = bidir_retention(qr, kr, vr, ret_decay_fwd[l], ret_decay_bwd[l], s_f, s_b)
        p_ret = retention_out(yr, rg, ret_gn_g[l], w_br_ret[l], x.dtype)

        qd = axial_rope(diff_heads(dq), row, col)
        kd = axial_rope(diff_heads(dk), row, col)
        vd = heads(dv, DIFF_HEADS)
        kd_c = diff_heads(dk_c)
        vd_c = heads(dv_c, DIFF_HEADS)
        k_all = jnp.concatenate([kd, kd_c], axis=3)
        v_all = jnp.concatenate([vd, vd_c], axis=2)
        p_diff = diff_out(diff_attention_blocks(qd, k_all, v_all, lam), diff_gn_g[l], lam_init, w_br_diff[l], x.dtype)

        mix = (jax.nn.sigmoid(gr) * p_ret + jax.nn.sigmoid(gd) * p_diff) @ w_out[l]
        x = x + ga_a * rmsnorm(mix, post_mix_g[l])
        if not last:
            p_ret_c = retention_out(yr_c, rg_c, ret_gn_g[l], w_br_ret[l], xc.dtype)
            p_diff_c = diff_out(diff_attention(diff_heads(dq_c), kd_c, vd_c, lam), diff_gn_g[l], lam_init, w_br_diff[l], xc.dtype)
            mix_c = (jax.nn.sigmoid(gr_c) * p_ret_c + jax.nn.sigmoid(gd_c) * p_diff_c) @ w_out[l]
            xc = xc + cga_a * rmsnorm(mix_c, post_mix_g[l])

        f = modulate(rmsnorm(x, pre_ffn_g[l]), sh_f, sc_f)
        x = x + ga_f * rmsnorm(peer_ffn(f, peer_w_q[l], peer_sub_keys[l], peer_u[l], peer_v[l]), post_ffn_g[l])
        if not last:
            fc = modulate(rmsnorm(xc, pre_ffn_g[l]), csh_f, csc_f)
            xc = xc + cga_f * rmsnorm(peer_ffn(fc, peer_w_q[l], peer_sub_keys[l], peer_u[l], peer_v[l]), post_ffn_g[l])
    return x


_drawn_inputs = setup_inputs


def setup_inputs(seed=0):
    import zlib

    import numpy as np

    out = dict(_drawn_inputs(seed))
    spreads = {}
    factors = {'post_ffn_g': 3.795}
    for name, (base, spread) in spreads.items():
        noise = np.random.default_rng([zlib.crc32(name.encode()), seed]).standard_normal(out[name].shape)
        drawn = base * np.exp(spread * noise) if base else spread * noise
        out[name] = jnp.asarray(drawn.astype(out[name].dtype))
    for name, factor in factors.items():
        out[name] = (out[name] * factor).astype(out[name].dtype)
    return out
```

```python
import math
from contextlib import ExitStack

import numpy as np

import concourse.bass as bass
from concourse import mybir

F32 = mybir.dt.float32
U32 = mybir.dt.uint32
ACT = mybir.ActivationFunctionType
ALU = mybir.AluOpType
AX = mybir.AxisListType

P = 128
D = 1024
KT = D // P
T = 512
TC = 256
TA = T + TC
NT = T // P
NTA = TA // P
GRID_W = 64
EPS = 1e-6
LAM_INIT = 0.8 - 0.6 * math.exp(0.0)

RH, RDK, RDV = 4, 128, 256
DH, DD = 8, 64
RQ0, RK0 = 0, RH * RDK
RV0 = RK0 + RH * RDK
RG0 = RV0 + RH * RDV
DQ0 = RG0 + RH * RDV
DK0 = DQ0 + DH * 2 * DD
DV0 = DK0 + DH * 2 * DD
GR0 = DV0 + DH * 2 * DD

PH, PK, TOPK = 8, 128, 16
PDK = 256
USLOTS = VSLOTS = 8
NDIAG = 4
V_CREDIT = 32

LAG_W = (NT - 1) * P
M1W = 2 * NT * P - P
M2W = T + TC - P
WCOL = 896
ROPE_W = 384
NEG = -3.0e38

B_MOD, PRE_MIX, POST_MIX, PRE_FFN, POST_FFN, RET_GN, DIFF_GN, NROWS = 0, 48, 56, 64, 72, 80, 88, 96


FILL = ((("p", 0), ("p", 1), ("t", 0)), (("p", 2), ("t", 1)),
        (("p", 3), ("t", 2), ("p", 4), ("t", 3)), (("p", 5), ("t", 4)))


def shape_constants():
    p = np.arange(P, dtype=np.float32)[:, None]
    d1 = np.arange(M1W, dtype=np.float32)[None, :] - LAG_W - p
    d2 = np.arange(M2W, dtype=np.float32)[None, :] - (TC - P) - p
    dist = np.concatenate([np.maximum(d1, 0), np.maximum(-d1, 0), d2 + TC, T - d2], axis=1)
    small = np.concatenate([np.eye(P, dtype=np.float32), np.tile(np.arange(16, dtype=np.float32), (P, 1))], axis=1)
    tok = np.arange(T)
    pos = np.stack([tok // GRID_W, tok % GRID_W], axis=1).astype(np.float32)

    def table(half):
        inv = np.power(np.float32(10000.0), -(np.arange(half, dtype=np.float32) / np.float32(half))).astype(np.float32)
        ang = (pos[:, :, None] * inv).astype(np.float32)
        cos, sin = np.cos(ang), np.sin(ang)
        both = np.stack([cos, cos], axis=2).reshape(T, 4 * half)
        return [both, (-sin).reshape(T, 2 * half), sin.reshape(T, 2 * half)]

    rope = np.concatenate(table(RDK // 4) + table(DD // 4), axis=1)
    return small.astype(np.float32), dist.astype(np.float32), rope.astype(np.float32)


def build(nc, x, ctx, c_pair, w_mod, rows, w_in, decays, lam, w_br_ret, w_br_diff, w_out,
          w_q, keys, peer_u, peer_v, small, dist, rope, out, debug=None):
    es = ExitStack()

    def sb(name, width, dt=F32):
        return es.enter_context(nc.sbuf_tensor(name, [P, width], dt))

    ps = es.enter_context(nc.psum_tensor("ps", [P, 8, 512], F32))
    wring = sb("wring", 2 * KT * WCOL)
    region_y = sb("region_ab", 2 * NT * D)
    region_o = sb("region_o", NT * D)
    region_z = sb("region_z", NT * D)
    region_u = sb("region_u", KT * TA)
    work = sb("work", 8 * D)
    tables = sb("tables", 2 * M1W + 3 * M2W + M1W)
    rope_t = sb("rope_t", NT * ROPE_W)
    small_t = sb("small_t", P + 16)
    vT = sb("vT", NROWS)
    stat = sb("stat", 672)
    ones = sb("ones", P)

    W = [wring[:, i * KT * WCOL:(i + 1) * KT * WCOL].rearrange("p (k n) -> p k n", k=KT) for i in range(2)]
    ident, iota16 = small_t[:, 0:P], small_t[:, P:P + 16]
    uT = region_u[:, :].rearrange("p (k t) -> p k t", k=KT)
    mT = fT = region_u[:, 0:KT * T].rearrange("p (k t) -> p k t", k=KT)
    y_sb = region_y[:, 0:NT * D].rearrange("p (t n) -> p t n", t=NT)
    sg_sb = region_y[:, NT * D:].rearrange("p (t n) -> p t n", t=NT)
    onT = region_y[:, NT * D:].rearrange("p (k t) -> p k t", k=KT)
    x_in = region_y[:, 0:NTA * D].rearrange("p (t n) -> p t n", t=NTA)
    m_sb = y_sb
    x_again = sg_sb
    o_sb = region_o[:, :].rearrange("p (t n) -> p t n", t=NT)
    x1 = o_sb
    zT = region_z[:, :].rearrange("p (k t) -> p k t", k=KT)
    f_sb = region_z[:, :].rearrange("p (t n) -> p t n", t=NT)
    gate = work[:, :].rearrange("p (n t c) -> p n t c", n=4, t=NT)
    uslot = work[:, :].rearrange("p (s n) -> p s n", s=USLOTS)
    vslot = region_y[:, :].rearrange("p (s n) -> p s n", s=VSLOTS)
    d_pos, d_neg = tables[:, 0:M1W], tables[:, M1W:2 * M1W]
    c_fwd, c_bwd = tables[:, 2 * M1W:2 * M1W + M2W], tables[:, 2 * M1W + M2W:2 * M1W + 2 * M2W]
    mask1 = tables[:, 2 * M1W + 2 * M2W:3 * M1W + 2 * M2W]
    mask2 = tables[:, 3 * M1W + 2 * M2W:3 * M1W + 3 * M2W]
    row_gf, row_ga, row_af, row_bf = (tables[:, i * D:(i + 1) * D] for i in range(4))
    ropes = rope_t[:, :].rearrange("p (t n) -> p t n", t=NT)

    at = [0]

    def piece(region, n, dt=None):
        a = region[:, at[0]:at[0] + n]
        at[0] += n
        return a if dt is None else a.bitcast(dt)

    at[0] = 0
    qT, kT = piece(work, T), piece(work, TA)
    v_sb = piece(work, NTA * RDV).rearrange("p (t n) -> p t n", t=NTA)
    rot = piece(work, 512).rearrange("p (b n) -> p b n", b=2)
    t1 = piece(work, 512).rearrange("p (b n) -> p b n", b=2)
    t2 = piece(work, 512).rearrange("p (b n) -> p b n", b=2)
    shared = at[0]
    aT = piece(work, NTA * T).rearrange("p (j n) -> p j n", j=NTA)
    eg = piece(work, 2 * RDV).rearrange("p (b n) -> p b n", b=2)
    at[0] = shared
    prob = piece(work, 4 * TA).rearrange("p (b a n) -> p b a n", b=2, a=2)
    dT = piece(work, TA)
    assert at[0] <= 8 * D
    at[0] = 0
    qTd = [qT, piece(region_z, T)]
    kTd = [kT, piece(region_z, TA)]
    v_d = [v_sb[:, :, 0:P], piece(region_z, NTA * P).rearrange("p (t n) -> p t n", t=NTA)]
    at[0] = 0
    cin = piece(stat, 2 * KT)
    csig = piece(stat, 2 * KT)
    csil = piece(stat, 2 * KT).rearrange("p (k j) -> p k j", j=2)
    eps_t = piece(stat, 1)
    ss, rms, rstd = piece(stat, 8), piece(stat, 8), piece(stat, 8)
    modv = piece(stat, 32).rearrange("p (k j) -> p k j", j=2)
    scaleA = piece(stat, 2 * KT).rearrange("p (k j) -> p k j", j=2)
    dec, dec_e, dec_y, dec_l, dec_r = (piece(stat, 2 * RH) for _ in range(5))
    lsum, lexp, nlam = piece(stat, 2), piece(stat, 2), piece(stat, 1)
    bn6 = piece(stat, RH * NT * 6)
    mv = piece(stat, RH * NT * 2)
    rmx, nbias, rsum, rinv, cfac = (piece(stat, 4) for _ in range(5))
    colv = piece(stat, 4 * KT).rearrange("p (v k) -> p v k", v=4)
    ssq, rmsq, rq = (piece(stat, 2 * NT * DH) for _ in range(3))
    assert at[0] <= 672, at[0]
    rowsT = work[:, 0:P]
    lamb = work[:, P:P + 256]
    lamp = work[:, P + 256:P + 384]
    row_diag = tables[:, 4 * D:4 * D + 512].rearrange("p (b n) -> p b n", b=4)
    square_u = region_y[:, NTA * D:].rearrange("p (b n) -> p b n", b=2)
    peer_t = wring[:, 7680:10240]
    at[0] = 0
    top_v = piece(peer_t, 32).rearrange("p (a n) -> p a n", a=2)
    top_i = piece(peer_t, 32, U32).rearrange("p (a n) -> p a n", a=2)
    top_f = piece(peer_t, 32).rearrange("p (a n) -> p a n", a=2)
    left = piece(peer_t, 256).rearrange("p (a n) -> p a n", a=2)
    cand = piece(peer_t, 256)
    cand2 = piece(peer_t, 256)
    fin_v = piece(peer_t, 16)
    pos = piece(peer_t, 16, U32)
    ab_i = piece(peer_t, 32, U32).rearrange("p (a n) -> p a n", a=2)
    ab_f = piece(peer_t, 32)
    hot = piece(peer_t, 512)
    ij = piece(peer_t, 32).rearrange("p (a n) -> p a n", a=2)
    idxs = piece(peer_t, NT * 16, U32).rearrange("p (t n) -> p t n", t=NT)
    logit = piece(peer_t, NT * 16).rearrange("p (t n) -> p t n", t=NT)
    dots = piece(peer_t, 32).rearrange("p (b n) -> p b n", b=2)
    gel = piece(peer_t, 32).rearrange("p (b n) -> p b n", b=2)
    soft = piece(peer_t, 32).rearrange("p (b n) -> p b n", b=2)
    ssum, sinv = piece(peer_t, 2), piece(peer_t, 2)
    wgt = piece(peer_t, 32).rearrange("p (b n) -> p b n", b=2)
    diag = piece(peer_t, NDIAG * P).rearrange("p (b n) -> p b n", b=NDIAG)
    assert at[0] <= 2560, at[0]
    wq_t = wring[:, 0:KT * PDK].rearrange("p (k n) -> p k n", k=KT)
    keys_t = wring[:, 2048:2048 + 256].rearrange("p (a n) -> p a n", a=2)
    keysT = wring[:, 2304:2304 + 256].rearrange("p (a n) -> p a n", a=2)
    pqT = wring[:, 2560:2560 + 1024].rearrange("p (a n) -> p a n", a=2)
    acc = wring[:, 3584:3584 + NT * D].rearrange("p (t n) -> p t n", t=NT)
    square_b = rope_t[:, 0:D]
    modps = ps[:, 5, 416:512].rearrange("p (c j) -> p c j", j=2)

    made = {}

    def s(name):
        if name not in made:
            made[name] = es.enter_context(nc.semaphore(name))
        return made[name]

    stood = {}

    def stand(eng, name):
        eng.sem_inc(s("stood_" + name), 1)

    w_in_v = w_in.rearrange("(k p) n -> p k n", p=P)
    w_mod_v = w_mod.rearrange("(p k) n -> p k n", k=KT)
    br_v = [w.rearrange("(k p) n -> p k n", p=P) for w in (w_br_ret, w_br_diff, w_out)]
    w_q_v = w_q.rearrange("(k p) n -> p k n", p=P)
    x_v = x.rearrange("(t p) n -> p t n", p=P)
    ctx_v = ctx.rearrange("(t p) n -> p t n", p=P)
    out_v = out.rearrange("(t p) n -> p t n", p=P)
    C1 = 512

    block = es.enter_context(nc.Block())

    @block.sync
    def _(sp):
        def load(dst, src, name):
            return sp.dma_start(dst, src).then_inc(s(name), 16)

        load(cin, c_pair.rearrange("(p k) j -> p (k j)", k=KT), "ld_c")
        load(small_t[:, :], small, "ld_small")
        load(rowsT[0:NROWS, :], rows, "ld_rows")
        for b in range(2):
            load(W[b][:, :, 0:C1], w_mod_v[:, :, b * C1:(b + 1) * C1], f"w_mod1_{b}")
        load(x_in[:, 0:NT, :], x_v, "ld_x")
        load(x_in[:, NT:NTA, :], ctx_v, "ld_ctx")
        load(dec, decays.partition_broadcast(P), "ld_dec")
        load(lamb, lam.partition_broadcast(P), "ld_lam")
        for b in range(2):
            sp.wait_ge(s("mod1_used"), b + 1)
            load(W[b][:, :, 0:C1], w_mod_v[:, :, (2 + b) * C1:(3 + b) * C1], f"w_mod1_{b}")
        load(rope_t[:, :].rearrange("p (t n) -> p t n", t=NT), rope.rearrange("(t p) n -> p t n", p=P), "ld_rope")
        load(tables[:, 0:2 * M1W + 2 * M2W], dist, "ld_dist")

        def ret_load(h, b):
            for dst, base, width in ((0, RQ0, RDK), (RDK, RK0, RDK), (2 * RDK, RV0, RDV), (2 * RDK + RDV, RG0, RDV)):
                load(W[b][:, :, dst:dst + width], w_in_v[:, :, bass.ds(h * width + base, width)], f"ret_w_{b}")

        def diff_load(h, b):
            for j, base in enumerate((DQ0, DK0, DV0)):
                load(W[b][:, :, j * P:(j + 1) * P], w_in_v[:, :, bass.ds(h * P + base, P)], f"diff_w_{b}")
            load(W[b][:, :, 3 * P:3 * P + C1], w_mod_v[:, :, bass.ds(h * C1 + 4 * C1, C1)], f"diff_w_{b}")

        for b in range(2):
            sp.wait_ge(s("mod1_used"), 3 + b)
            ret_load(b, b)
        with sp.Fori(1, RH // 2) as i:
            for b in range(2):
                sp.wait_ge(s("r_proj"), 20 * i + 10 * b - 10)
                ret_load(2 * i + b, b)
        for b in range(2):
            sp.wait_ge(s("r_proj"), 10 * (RH - 1 + b))
            diff_load(b, b)
        with sp.Fori(1, DH // 2) as i:
            for b in range(2):
                sp.wait_ge(s("diff_w_used"), 2 * i + b - 1)
                diff_load(2 * i + b, b)
        for n in range(4):
            b = n % 2
            if n < 2:
                sp.wait_ge(s("diff_w_used"), DH - 1 + b)
            else:
                sp.wait_ge(s("g_proj"), 4 * (b + 1))
            load(W[b][:, :, 0:C1], w_in_v[:, :, n * C1 + GR0:(n + 1) * C1 + GR0], f"gate_w_{b}")
        for n in range(2):
            for b in range(2):
                if n == 0:
                    sp.wait_ge(s("g_proj"), 4 * (3 + b))
                else:
                    sp.wait_ge(s("br_proj"), 4 * (b + 1))
                load(W[b][:, :, 0:C1], br_v[b][:, :, n * C1:(n + 1) * C1], f"br_w_{b}")
        for b in range(2):
            sp.wait_ge(s("br_proj"), 8 + 4 * (b + 1))
            load(W[b][:, :, 0:C1], br_v[2][:, :, b * C1:(b + 1) * C1], f"out_w_{b}")
        load(x_again, x_v, "ld_x2")
        sp.wait_ge(s("mix"), 2 * NT)
        load(wq_t, w_q_v[:, :, 0:PDK], "ld_wq")
        load(keys_t, keys[0].rearrange("a k d -> k a d"), "ld_wq")
        with sp.Fori(0, PH - 1) as h:
            sp.wait_ge(s("q_proj"), 2 * h + 2)
            load(wq_t, w_q_v[:, :, bass.ds(h * PDK + PDK, PDK)], "ld_wq")
            load(keys_t, keys[bass.ds(h + 1, 1)].rearrange("o a k d -> k (o a) d"), "ld_wq")
        for t in range(NT):
            sp.wait_ge(s("y_ready"), t + 1)
            load(out_v[:, t, :], acc[:, t, :], "stored")
        sp.wait_ge(s("stored"), NT * 16)

    @block.tensor
    def _(pe):
        def product(out_ap, lhs, rhs, n=KT):
            for k in range(n):
                last = pe.matmul(out_ap, lhs(k), rhs(k), start=(k == 0), stop=(k == n - 1))
            return last

        pe.wait_ge(s("csil_ready"), 1)
        with pe.Fori(0, 2) as i:
            for b in range(2):
                pe.wait_ge(s(f"w_mod1_{b}"), 16 * i + 16)
                for j in range(4):
                    last = product(modps[:, bass.ds((2 * i + b) * 4 + j, 1), :].rearrange("p c j -> p (c j)"),
                                   lambda k: W[b][:, k, j * P:(j + 1) * P], lambda k: csil[:, k, :])
                last.then_inc(s("mod1_used"), 1)
        pe.wait_ge(s("ld_rows"), 16)
        pe.wait_ge(s("ld_small"), 16)
        pe.transpose(ps[:, 4, 0:NROWS], rowsT[0:NROWS, :], small_t[0:NROWS, 0:NROWS]).then_inc(s("rows_turned"), 1)
        for t in range(NTA):
            pe.wait_ge(s("xn_ready"), t + 1)
            if t >= 2:
                pe.wait_ge(s("ut_act"), t - 1)
                pe.wait_ge(s("ut_dve"), t - 1)
            for k in range(KT):
                last = pe.transpose(ps[:, 2 * (t % 2) + k // 4, (k % 4) * P:(k % 4 + 1) * P],
                                    x_in[:, t, k * P:(k + 1) * P], ident)
            last.then_inc(s("x_turned"), 1)

        pe.wait_ge(s("ut_act"), NTA)
        pe.wait_ge(s("ut_dve"), NTA)
        with pe.Fori(0, RH // 2) as i:
            for b in range(2):
                h = 2 * i + b

                def turn(t):
                    pe.wait_ge(s("r_took"), 10 * h + t + 3)
                    pe.wait_ge(s("r_tfree"), 6 * h + t + 1)
                    if t == 1:
                        pe.wait_ge(s("r_yfree"), NT * h + 2)
                    if t < NT:
                        pe.transpose(ps[:, 4 - t % 2, 0:P], rot[:, t % 2, 0:P], ident)
                    pe.transpose(ps[:, 4 - t % 2, P:2 * P], rot[:, t % 2, P:2 * P], ident).then_inc(s("r_turned"), 1)

                for u in range(NTA + NT):
                    if u == 0:
                        pe.wait_ge(s(f"ret_w_{b}"), 64 * i + 64)
                    if 2 <= u < NTA + 2:
                        pe.wait_ge(s("r_vcopied"), 6 * h + u - 1)
                    pe.wait_ge(s("r_took"), 10 * h + u + 1)
                    t = u % NTA
                    lo, hi = ((0, 512) if u < NT else (P, 512)) if u < NTA else (512, 768)
                    product(ps[:, 6 + u % 2, 0:hi - lo], lambda k: uT[:, k, t * P:(t + 1) * P],
                            lambda k: W[b][:, k, lo:hi]).then_inc(s("r_proj"), 1)
                    if 1 <= u <= NTA:
                        turn(u - 1)
                pe.wait_ge(s("r_tfree"), 6 * h + NTA + 2)
                for j in range(NTA):
                    pe.wait_ge(s("r_masked"), 6 * h + j + 1)
                    mm = pe.matmul(ps[:, j % 3, :], kT[:, j * P:(j + 1) * P], qT[:, :], start=True, stop=True)
                    mm.then_inc(s("r_score"), 1)
                for t in range(NT):
                    if t == 0:
                        pe.wait_ge(s("r_masked"), 6 * h + NTA + 3)
                    pe.wait_ge(s("r_yfree"), NT * h + t + 1)
                    product(ps[:, 3 + 2 * (t % 2), 0:RDV], lambda j: aT[:, j, t * P:(t + 1) * P],
                            lambda j: v_sb[:, j, :], NTA).then_inc(s("r_y"), 1)

        def project(h, b, t):
            pe.wait_ge(s("d_tfree"), 6 * h + t + 1)
            lo = 0 if t < NT else P
            product(ps[:, 6 + t % 2, lo:3 * P], lambda k: uT[:, k, t * P:(t + 1) * P],
                    lambda k: W[b][:, k, lo:3 * P]).then_inc(s("d_proj"), 1)

        def turn_d(h, t):
            pe.wait_ge(s("d_took"), 6 * h + t + 1)
            pe.wait_ge(s("d_vcopied"), 6 * h + t + 1)
            for a in range(0 if t < NT else 1, 2):
                last = pe.transpose(ps[:, 6 + t % 2, a * P:(a + 1) * P], rot[:, t % 2, a * P:(a + 1) * P], ident)
            last.then_inc(s("d_turned"), 1)

        def mod(h, b, j):
            return product(modps[:, bass.ds(h * 4 + 16 + j, 1), :].rearrange("p c j -> p (c j)"),
                           lambda k: W[b][:, k, 3 * P + j * P:3 * P + (j + 1) * P], lambda k: csil[:, k, :])

        def scores(h, b, t):
            for a in range(2):
                pe.wait_ge(s("d_exp"), 2 * (NT * h + t) + a + 1)
                for lo, hi in ((0, 512), (512, TA)):
                    mm = pe.matmul(ps[:, 2 * a + lo // 512, 0:hi - lo], qTd[b][a * DD:(a + 1) * DD, t * P:(t + 1) * P],
                                   kTd[b][a * DD:(a + 1) * DD, lo:hi], start=True, stop=True)
                mm.then_inc(s("d_score"), 1)

        def first_scores(h, b):
            pe.wait_ge(s("d_tfree"), 6 * h + NTA + 2)
            scores(h, b, 0)

        def head(h, b, weights):
            for t in range(NT):
                if weights is not None:
                    if t == 0:
                        pe.wait_ge(*weights)
                    for kind, u in FILL[t]:
                        if kind == "p":
                            project(h + 1, 1 - b, u)
                        else:
                            turn_d(h + 1, u)
                pe.wait_ge(s("d_ofree"), NT * h + t + 1)
                if weights is not None:
                    last = mod(h + 1, 1 - b, t)
                    if t == NT - 1:
                        last.then_inc(s("diff_w_used"), 1)
                pe.wait_ge(s("d_comb"), NT * h + t + 1)
                for j in range(NTA):
                    mm = pe.transpose(ps[:, 4 + j // 4, (j % 4) * P:(j % 4 + 1) * P],
                                      prob[:, t % 2, 0, j * P:(j + 1) * P], ident)
                mm.then_inc(s("d_aturned"), 1)
                if t + 1 < NT:
                    scores(h, b, t + 1)
                elif weights is not None:
                    turn_d(h + 1, NTA - 1)
                pe.wait_ge(s("d_acopied"), NT * h + t + 1)
                product(ps[:, 5, 256:384], lambda j: dT[:, j * P:(j + 1) * P],
                        lambda j: v_d[b][:, j, :], NTA).then_inc(s("d_o"), 1)
            if weights is not None:
                first_scores(h + 1, 1 - b)

        pe.wait_ge(s("r_took"), 10 * RH + 2)
        pe.wait_ge(s("diff_w_0"), 64)
        for step in FILL:
            for kind, u in step:
                project(0, 0, u) if kind == "p" else turn_d(0, u)
        pe.wait_ge(s("d_ofree"), 1)
        for j in range(4):
            last = mod(0, 0, j)
        last.then_inc(s("diff_w_used"), 1)
        turn_d(0, NTA - 1)
        first_scores(0, 0)
        with pe.Fori(0, DH // 2 - 1) as i:
            head(2 * i, 0, (s("diff_w_1"), 64 * i + 64))
            head(2 * i + 1, 1, (s("diff_w_0"), 64 * i + 128))
        head(DH - 2, 0, (s("diff_w_1"), 32 * DH))
        head(DH - 1, 1, None)

        with pe.Fori(0, 2) as i:
            for b in range(2):
                pe.wait_ge(s(f"gate_w_{b}"), 16 * i + 16)
                for t in range(NT):
                    pe.wait_ge(s("g_free"), 4 * (2 * i + b) + t + 1)
                    last = product(ps[:, t, :], lambda k: uT[:, k, t * P:(t + 1) * P], lambda k: W[b][:, k, 0:C1])
                    last.then_inc(s("g_proj"), 1)
        for v in range(4):
            for half in range(2):
                n = 2 * v + half
                if n >= 2:
                    pe.wait_ge(s("row_copied"), n - 1)
                for k in range(4):
                    pe.wait_ge(s("diag8"), 4 * n + k + 1)
                    pe.matmul(ps[:, 6 + n % 2, k * P:(k + 1) * P], ones[:, :], row_diag[:, k, :],
                              start=True, stop=True).then_inc(s("row_mm"), 1)
        for n in range(2 * NT):
            t, src = n % NT, (y_sb if n < NT else o_sb)
            pe.wait_ge(s("branch_normed"), n + 1)
            if n >= 2:
                pe.wait_ge(s("branch_copied"), n - 1)
            elif n == 1:
                pe.wait_ge(s("row_copied"), 8)
            if n == 0:
                pe.wait_ge(s("g_free"), 16 + 2)
            bank = 6 * (n % 2)
            for k in range(KT):
                last = pe.transpose(ps[:, bank + k // 4, (k % 4) * P:(k % 4 + 1) * P], src[:, t, k * P:(k + 1) * P], ident)
            last.then_inc(s("branch_turned"), 1)
        pe.wait_ge(s("branch_copied"), 2 * NT)
        pe.wait_ge(s("g_free"), 16 + 4)
        with pe.Fori(0, 2) as n:
            for b in range(2):
                pe.wait_ge(s(f"br_w_{b}"), 16 * n + 16)
                src = zT if b == 0 else onT
                for t in range(NT):
                    pe.wait_ge(s("br_free"), 8 * n + 4 * b + t + 1)
                    product(ps[:, 4 * b + t, :], lambda k: src[:, k, t * P:(t + 1) * P],
                            lambda k: W[b][:, k, 0:C1]).then_inc(s("br_proj"), 1)
        for t in range(NT):
            pe.wait_ge(s("m_ready"), NT + t + 1)
            if t >= 2:
                pe.wait_ge(s("m_copied"), t - 1)
            for k in range(KT):
                last = pe.transpose(ps[:, 2 * (t % 2) + k // 4, (k % 4) * P:(k % 4 + 1) * P], m_sb[:, t, k * P:(k + 1) * P], ident)
            last.then_inc(s("m_turned"), 1)
        for b in range(2):
            pe.wait_ge(s(f"out_w_{b}"), 16)

        def turn_f(t):
            pe.wait_ge(s("f_ready"), t + 1)
            if t >= 2:
                pe.wait_ge(s("f_copied"), t - 1)
            for k in range(KT):
                last = pe.transpose(ps[:, 2 * (t % 2) + k // 4, (k % 4) * P:(k % 4 + 1) * P], f_sb[:, t, k * P:(k + 1) * P], ident)
            last.then_inc(s("f_turned"), 1)

        for t in range(NT):
            pe.wait_ge(s("m_copied"), t + 1)
            if t >= 2:
                pe.wait_ge(s("mix_out"), 2 * (t - 1))
            for n in range(2):
                product(ps[:, 4 + 2 * (t % 2) + n, :], lambda k: mT[:, k, t * P:(t + 1) * P],
                        lambda k: W[n][:, k, 0:C1]).then_inc(s("mix"), 1)
        for t in range(NT):
            turn_f(t)

        def queries(h):
            pe.wait_ge(s("ld_wq"), 32 * h + 32)
            for a in range(2):
                last = pe.transpose(ps[:, 4, a * P:(a + 1) * P], keys_t[:, a, :], ident)
            last.then_inc(s("keys_turned"), 1)
            for a in range(2):
                if a == 1:
                    pe.wait_ge(s("q_copied"), 2 * h + 1)
                product(ps[:, 5, :], lambda k: wq_t[:, k, a * P:(a + 1) * P], lambda k: fT[:, k, :]).then_inc(s("q_proj"), 1)
            for a in range(2):
                pe.wait_ge(s("q_copied"), 2 * h + a + 1)
                if a == 0:
                    pe.wait_ge(s("keys_copied"), h + 1)
                for t in range(NT):
                    last = pe.matmul(ps[:, 6 + a, t * P:(t + 1) * P], pqT[:, a, t * P:(t + 1) * P], keysT[:, a, :],
                                     start=True, stop=True)
                last.then_inc(s("scored"), 1)

        def weighted_sum(h, t):
            n = NT * h + t
            pe.wait_ge(s("acc_added"), n + 1)
            for e in range(TOPK):
                pe.wait_ge(s(f"v_in_{e % VSLOTS}"), 32 * n + 16 * (e // VSLOTS) + 16)
                pe.wait_ge(s("diag_ready"), TOPK * n + e + 1)
                for half in range(2):
                    last = pe.matmul(ps[:, 2 * (t % 2) + half, :], diag[:, e % NDIAG, :],
                                     vslot[:, e % VSLOTS, half * 512:(half + 1) * 512],
                                     start=(e == 0), stop=(e == TOPK - 1))
                last.then_inc(s("v_used"), 1)

        pe.sem_inc(s("v_used"), V_CREDIT)
        pe.wait_ge(s("f_copied"), NT)
        queries(0)
        with pe.Fori(0, PH - 1) as h:
            for t in range(NT):
                weighted_sum(h, t)
                if t == 0:
                    pe.wait_ge(s("topk_done"), NT * h + NT)
                    queries(h + 1)
        for t in range(NT):
            weighted_sum(PH - 1, t)

    @block.scalar
    def _(act):
        def do(out_ap, in_ap, func=ACT.Copy, **kw):
            return act.activation(out_ap, in_ap, func, **kw)

        act.wait_ge(s("ld_c"), 16)
        do(csig, cin, ACT.Sigmoid).then_inc(s("csig"), 1)
        act.wait_ge(s("eps_set"), 1)
        for t in range(NTA):
            if t in (0, NT):
                act.wait_ge(s("ld_x" if t == 0 else "ld_ctx"), 16)
            if t >= 2:
                act.drain()
            do(square_u[:, t % 2, :], x_in[:, t, :], ACT.Square, accum_out=ss[:, t:t + 1])
        act.drain()
        do(rms[:, 0:NTA], ss[:, 0:NTA], ACT.Sqrt, scale=1.0 / D, bias=eps_t).then_inc(s("x_rms"), 1)
        act.wait_ge(s("ld_dec"), 16)
        do(dec_e, dec, ACT.Exp, scale=math.log(2.0)).then_inc(s("dec_e"), 1)
        act.wait_ge(s("lam_sums"), 1)
        do(lexp, lsum, ACT.Exp).then_inc(s("lam_exp"), 1)
        act.wait_ge(s("dec_y"), 1)
        do(dec_l, dec_y, ACT.Ln).then_inc(s("dec_ln"), 1)
        act.wait_ge(s("mod_ready"), 1)
        for t in range(NTA):
            act.wait_ge(s("x_turned"), t + 1)
            j = 0 if t < NT else 1
            for k in range(4):
                last = do(uT[:, k, t * P:(t + 1) * P], ps[:, 2 * (t % 2), k * P:(k + 1) * P], ACT.Identity,
                          scale=scaleA[:, k, j:j + 1], bias=modv[:, k, j:j + 1])
            last.then_inc(s("ut_act"), 1)

        act.sem_inc(s("r_tfree"), 2)
        act.sem_inc(s("r_yfree"), 2)
        act.wait_ge(s("ld_dist"), 16)
        act.wait_ge(s("dec_ready"), 1)
        with act.Fori(0, RH // 2) as i:
            for b in range(2):
                h = 2 * i + b
                act.wait_ge(s("r_dist"), h + 1)
                do(mask1, mask1, ACT.Exp).then_inc(s("r_mask"), 1)
                do(mask2, mask2, ACT.Exp).then_inc(s("r_mask"), 1)
                do(aT[:, 0:2, :].rearrange("p a n -> p (a n)")[:, 0:M2W],
                   aT[:, 0:2, :].rearrange("p a n -> p (a n)")[:, 0:M2W], ACT.Exp).then_inc(s("r_mask"), 1)

                def copy_t(t):
                    act.wait_ge(s("r_turned"), 6 * h + t + 1)
                    if t < NT:
                        do(qT[:, t * P:(t + 1) * P], ps[:, 4 - t % 2, 0:P], scale=RDK ** -0.5)
                    last = do(kT[:, t * P:(t + 1) * P], ps[:, 4 - t % 2, P:2 * P])
                    last.then_inc(s("r_tfree"), 1)

                for u in range(NTA + NT):
                    act.wait_ge(s("r_proj"), 10 * h + u + 1)
                    if u < NTA:
                        act.wait_ge(s("r_took"), 10 * h + u + 3)
                        lo = 2 * RDK if u < NT else RDK
                        do(v_sb[:, u, :], ps[:, 6 + u % 2, lo:lo + RDV]).then_inc(s("r_vcopied"), 1)
                    else:
                        if u >= NTA + 2:
                            act.wait_ge(s("r_took"), 10 * h + u + 1)
                        do(eg[:, u % 2, :], ps[:, 6 + u % 2, 0:RDV], ACT.Exp, scale=-1.0).then_inc(s("r_eg"), 1)
                    if 1 <= u <= NTA:
                        copy_t(u - 1)
                for t in range(NT):
                    act.wait_ge(s("r_ystat"), NT * h + t + 1)
                    stand(act, "act")
                    do(y_sb[:, t, bass.ds(h * RDV, RDV)], ps[:, 3 + 2 * (t % 2), 0:RDV]).then_inc(s("r_yfree"), 1)

        act.sem_inc(s("d_tfree"), 2)
        act.sem_inc(s("d_exp"), 2)
        act.sem_inc(s("d_ofree"), 1)

        def copy_v(h, b, u):
            act.wait_ge(s("d_took"), 6 * h + u + 1)
            do(v_d[b][:, u, :], ps[:, 6 + u % 2, 2 * P:3 * P]).then_inc(s("d_vcopied"), 1)

        def copy_qk(h, b, t):
            act.wait_ge(s("d_turned"), 6 * h + t + 1)
            if t < NT:
                do(qTd[b][:, t * P:(t + 1) * P], ps[:, 6 + t % 2, 0:P])
            do(kTd[b][:, t * P:(t + 1) * P], ps[:, 6 + t % 2, P:2 * P]).then_inc(s("d_tfree"), 1)

        def fill(h, b, step):
            for kind, u in FILL[step]:
                if kind == "t":
                    copy_qk(h, b, u)
                else:
                    copy_v(h, b, u)

        def exps(h, t):
            for a in range(2):
                act.wait_ge(s("d_max"), 2 * (NT * h + t) + a + 1)
                table = ps[:, 2 * a:2 * a + 2, :].rearrange("p b n -> p (b n)")[:, 0:TA]
                do(prob[:, t % 2, a, :], table, ACT.Exp, scale=DD ** -0.5,
                   bias=nbias[:, 2 * (t % 2) + a:2 * (t % 2) + a + 1],
                   accum_out=rsum[:, 2 * (t % 2) + a:2 * (t % 2) + a + 1]).then_inc(s("d_exp"), 1)

        def head(h, b, ahead):
            exps(h, 0)
            for t in range(NT):
                if ahead:
                    fill(h + 1, 1 - b, t)
                act.wait_ge(s("d_aturned"), NT * h + t + 1)
                do(dT[:, :], ps[:, 4:6, :].rearrange("p b n -> p (b n)")[:, 0:TA]).then_inc(s("d_acopied"), 1)
                if t + 1 < NT:
                    exps(h, t + 1)
                elif ahead:
                    copy_qk(h + 1, 1 - b, NTA - 1)
                act.wait_ge(s("d_o"), NT * h + t + 1)
                stand(act, "act")
                do(o_sb[:, t, bass.ds(h * P, P)], ps[:, 5, 256:384], scale=rinv[:, 2 * (t % 2):2 * (t % 2) + 1])\
                    .then_inc(s("d_ofree"), 1)

        for step in range(NT):
            fill(0, 0, step)
        copy_qk(0, 0, NTA - 1)
        with act.Fori(0, DH // 2 - 1) as i:
            for b in range(2):
                head(2 * i + b, b, True)
        head(DH - 2, 0, True)
        head(DH - 1, 1, False)

        act.sem_inc(s("g_free"), 4)
        act.wait_ge(s("q_sq"), 1)
        do(rmsq[:, 0:16], mv.rearrange("p (n j) -> p n j", j=2)[:, :, 1], ACT.Sqrt, bias=eps_t).then_inc(s("br_rms"), 1)
        do(rmsq[:, 16:48], ssq[:, 16:48], ACT.Sqrt, scale=1.0 / P, bias=eps_t).then_inc(s("br_rms"), 1)
        with act.Fori(0, 2) as i:
            for b in range(2):
                for t in range(NT):
                    act.wait_ge(s("g_proj"), 4 * (2 * i + b) + t + 1)
                    stand(act, "act")
                    do(gate[:, bass.ds(2 * i + b, 1), t, :].rearrange("p o c -> p (o c)"), ps[:, t, :], ACT.Sigmoid)\
                        .then_inc(s("g_free"), 1)
        for n in range(8):
            act.wait_ge(s("row_mm"), 4 * n + 4)
            dst = (row_gf, row_ga, row_af, row_bf)[n // 2]
            do(dst[:, (n % 2) * 512:(n % 2 + 1) * 512], ps[:, 6 + n % 2, :]).then_inc(s("row_copied"), 1)
        for t in range(NT):
            act.wait_ge(s("m_turned"), t + 1)
            do(mT[:, :, t * P:(t + 1) * P], ps[:, 2 * (t % 2):2 * (t % 2) + 2, :].rearrange("p b (k n) -> p (b k) n", n=P))\
                .then_inc(s("m_copied"), 1)
        for t in range(NT):
            act.wait_ge(s("mix_out"), 2 * t + 2)
            if t:
                act.drain()
            do(square_b, x1[:, t, :], ACT.Square, accum_out=ss[:, t:t + 1])
            act.drain()
            do(rms[:, t:t + 1], ss[:, t:t + 1], ACT.Sqrt, scale=1.0 / D, bias=eps_t).then_inc(s("mix_rms"), 1)
            act.wait_ge(s("x1_ready"), t + 1)
            do(square_b, x1[:, t, :], ACT.Square, accum_out=ss[:, 4 + t:5 + t])
            act.drain()
            do(rms[:, 4 + t:5 + t], ss[:, 4 + t:5 + t], ACT.Sqrt, scale=1.0 / D, bias=eps_t).then_inc(s("x1_rms"), 1)
        for t in range(NT):
            act.wait_ge(s("f_turned"), t + 1)
            do(fT[:, :, t * P:(t + 1) * P], ps[:, 2 * (t % 2):2 * (t % 2) + 2, :].rearrange("p b (k n) -> p (b k) n", n=P))\
                .then_inc(s("f_copied"), 1)

        def copies(h):
            act.wait_ge(s("keys_turned"), h + 1)
            do(keysT, ps[:, 4, 0:256].rearrange("p (a n) -> p a n", a=2)).then_inc(s("keys_copied"), 1)
            for a in range(2):
                act.wait_ge(s("q_proj"), 2 * h + a + 1)
                do(pqT[:, a, :], ps[:, 5, :]).then_inc(s("q_copied"), 1)

        def unit(h, t):
            n, b = NT * h + t, t % 2
            act.wait_ge(s("u_used"), TOPK * n + TOPK + USLOTS)
            do(soft[:, b, :], logit[:, t, :], ACT.Exp, accum_out=ssum[:, b:b + 1])
            do(gel[:, b, :], dots[:, b, :], ACT.Gelu)
            act.drain()
            act.sem_inc(s("gelu_done"), 1)
            act.wait_ge(s("w_ready"), n + 1)
            for e in range(TOPK):
                act.wait_ge(s("v_used"), TOPK * n + e + 1 - NDIAG + V_CREDIT)
                do(diag[:, e % NDIAG, :], ident, scale=wgt[:, b, e:e + 1]).then_inc(s("diag_ready"), 1)

        copies(0)
        with act.Fori(0, PH - 1) as h:
            for t in range(NT):
                unit(h, t)
                if t == 0:
                    copies(h + 1)
        for t in range(NT):
            unit(PH - 1, t)
        for t in range(NT):
            act.wait_ge(s("acc_final"), t + 1)
            if t >= 1:
                act.drain()
            do(square_b, acc[:, t, :], ACT.Square, accum_out=ss[:, t:t + 1])
            act.drain()
            do(rms[:, t:t + 1], ss[:, t:t + 1], ACT.Sqrt, scale=1.0 / D, bias=eps_t).then_inc(s("y_rms"), 1)

    @block.vector
    def _(dve):
        tt, ts, stt, cp = dve.tensor_tensor, dve.tensor_scalar, dve.scalar_tensor_tensor, dve.tensor_copy

        dve.memset(eps_t, EPS).then_inc(s("eps_set"), 1)
        dve.memset(ones[:, :], 1.0)
        dve.wait_ge(s("csig"), 1)
        tt(csil, cin.rearrange("p (k j) -> p k j", j=2), csig.rearrange("p (k j) -> p k j", j=2), ALU.mult)\
            .then_inc(s("csil_ready"), 1)
        dve.wait_ge(s("ld_lam"), 16)
        lam4 = lamb.rearrange("p (a b n) -> p a b n", a=2, b=2)
        tt(lamp.rearrange("p (a n) -> p a n", a=2), lam4[:, :, 0, :], lam4[:, :, 1, :], ALU.mult)
        dve.drain()
        dve.tensor_reduce(lsum, lamp.rearrange("p (a n) -> p a n", a=2), AX.X, ALU.add).then_inc(s("lam_sums"), 1)
        dve.wait_ge(s("x_rms"), 1)
        dve.reciprocal(rstd[:, 0:NTA], rms[:, 0:NTA])
        dve.drain()
        for t in range(NTA):
            ts(x_in[:, t, :], x_in[:, t, :], rstd[:, t:t + 1], None, ALU.mult).then_inc(s("xn_ready"), 1)
        dve.wait_ge(s("dec_e"), 1)
        ts(dec_y, dec_e, -1.0, 1.0, ALU.mult, ALU.add).then_inc(s("dec_y"), 1)
        dve.drain()
        ts(dec_r, dec_y, -1.0, 1.0, ALU.mult, ALU.add)
        dve.drain()
        ts(dec_r, dec_r, 1e-30, None, ALU.max)
        dve.drain()
        dve.reciprocal(dec_r, dec_r)
        dve.drain()
        tt(dec_r, dec_r, dec_e, ALU.mult)
        dve.drain()
        dve.wait_ge(s("dec_ln"), 1)
        tt(dec_l, dec_l, dec_r, ALU.mult).then_inc(s("dec_ready"), 1)
        dve.wait_ge(s("lam_exp"), 1)
        tt(nlam, lexp[:, 1:2], lexp[:, 0:1], ALU.subtract)
        dve.drain()
        ts(nlam, nlam, -LAM_INIT, None, ALU.add)
        dve.wait_ge(s("rows_turned"), 1)
        cp(vT[:, :], ps[:, 4, 0:NROWS])
        dve.drain()
        dve.wait_ge(s("mod1_used"), 4)
        tt(modv, modps[:, 0:16, :], vT[:, B_MOD:B_MOD + 16].unsqueeze(2).to_broadcast([P, 16, 2]), ALU.add)
        dve.drain()
        stt(scaleA, modv[:, 8:16, :], 1.0, vT[:, PRE_MIX:PRE_MIX + 8].unsqueeze(2).to_broadcast([P, 8, 2]),
            ALU.add, ALU.mult).then_inc(s("mod_ready"), 1)
        ts(vT[:, DIFF_GN:DIFF_GN + 8], vT[:, DIFF_GN:DIFF_GN + 8], 1.0 - LAM_INIT, None, ALU.mult)
        dve.drain()
        for t in range(NTA):
            dve.wait_ge(s("x_turned"), t + 1)
            j = 0 if t < NT else 1
            for k in range(4, KT):
                last = ts(uT[:, k, t * P:(t + 1) * P], ps[:, 2 * (t % 2) + 1, (k - 4) * P:(k - 3) * P],
                          scaleA[:, k, j:j + 1], modv[:, k, j:j + 1], ALU.mult, ALU.add)
            last.then_inc(s("ut_dve"), 1)

        def rotate(t, src, groups, half, table):
            w = 4 * half
            cos = ropes[:, t, table:table + w].unsqueeze(1).to_broadcast([P, groups, w])
            g = src.rearrange("p (g n) -> p g n", g=groups)
            sin = [ropes[:, t, table + w + i * 2 * half:table + w + (i + 1) * 2 * half]
                   .rearrange("p (x n) -> p x n", x=2).unsqueeze(1).to_broadcast([P, groups, 2, half]) for i in range(2)]
            src5 = src.rearrange("p (g x f n) -> p g x f n", g=groups, x=2, f=2)
            dst5 = t2[:, t % 2, :].rearrange("p (g x f n) -> p g x f n", g=groups, x=2, f=2)
            tt(t1[:, t % 2, :].rearrange("p (g n) -> p g n", g=groups), g, cos, ALU.mult)
            tt(dst5[:, :, :, 0, :], src5[:, :, :, 1, :], sin[0], ALU.mult)
            tt(dst5[:, :, :, 1, :], src5[:, :, :, 0, :], sin[1], ALU.mult)
            dve.drain()
            return tt(rot[:, t % 2, :], t1[:, t % 2, :], t2[:, t % 2, :], ALU.add)

        dve.sem_inc(s("r_took"), 2)
        dve.sem_inc(s("r_masked"), 3)
        dve.wait_ge(s("ld_rope"), 16)
        dve.wait_ge(s("ld_dist"), 16)
        with dve.Fori(0, RH // 2) as i:
            for b in range(2):
                h = 2 * i + b
                lf, lb = dec_l[:, bass.ds(h, 1)], dec_l[:, bass.ds(h + RH, 1)]
                back = aT[:, 0:2, :].rearrange("p a n -> p (a n)")[:, 0:M2W]
                dve.drain()
                ts(mask1, d_neg, lb, None, ALU.mult)
                ts(mask2, c_fwd, lf, None, ALU.mult)
                ts(back, c_bwd, lb, None, ALU.mult)
                dve.drain()
                stt(mask1, d_pos, lf, mask1, ALU.mult, ALU.add).then_inc(s("r_dist"), 1)
                for u in range(NTA + NT):
                    t = u % NTA
                    bank = ps[:, 6 + u % 2, :]
                    if u < NTA:
                        dve.drain()
                        dve.wait_ge(s("r_proj"), 10 * h + u + 1)
                        if u < NT:
                            rotate(t, bank[:, 0:2 * RDK], 2, RDK // 4, 0).then_inc(s("r_took"), 1)
                        else:
                            cp(rot[:, t % 2, P:2 * P], bank[:, 0:P]).then_inc(s("r_took"), 1)
                    else:
                        dve.wait_ge(s("r_eg"), NT * h + t + 1)
                        e = eg[:, u % 2, :]
                        ts(e, e, 1.0, None, ALU.add)
                        dve.drain()
                        dve.reciprocal(e, e)
                        dve.drain()
                        tt(sg_sb[:, t, bass.ds(h * RDV, RDV)], bank[:, 0:RDV], e, ALU.mult).then_inc(s("r_took"), 1)
                dve.wait_ge(s("r_mask"), 3 * h + 3)
                tt(mask2, mask2, back, ALU.add)
                dve.drain()
                for j in range(NTA):
                    dve.wait_ge(s("r_score"), 6 * h + j + 1)
                    m = mask1[:, (NT - 1 - j) * P:(NT - 1 - j) * P + T] if j < NT else \
                        mask2[:, (NTA - 1 - j) * P:(NTA - 1 - j) * P + T]
                    tt(aT[:, j, :], ps[:, j % 3, :], m, ALU.mult).then_inc(s("r_masked"), 1)
                for t in range(NT):
                    dve.wait_ge(s("r_y"), NT * h + t + 1)
                    stand(dve, "dve")
                    dve.bn_stats(bn6[:, bass.ds((h * NT + t) * 6, 6)], ps[:, 3 + 2 * (t % 2), 0:RDV]).then_inc(s("r_ystat"), 1)

        def take(h, t):
            bank = ps[:, 6 + t % 2, :]
            dve.drain()
            dve.wait_ge(s("d_proj"), 6 * h + t + 1)
            if t < NT:
                rotate(t, bank[:, 0:2 * P], 4, DD // 4, 256).then_inc(s("d_took"), 1)
            else:
                cp(rot[:, t % 2, P:2 * P], bank[:, P:2 * P]).then_inc(s("d_took"), 1)

        def fill_d(h, step):
            for kind, u in FILL[step]:
                if kind == "p":
                    take(h, u)

        def head_d(h, ahead):
            for t in range(NT):
                for a in range(2):
                    q = 2 * (t % 2) + a
                    dve.wait_ge(s("d_score"), 2 * (NT * h + t) + a + 1)
                    dve.tensor_reduce(rmx[:, q:q + 1], ps[:, 2 * a:2 * a + 2, :].rearrange("p b n -> p (b n)")[:, 0:TA],
                                      AX.X, ALU.max)
                    dve.drain()
                    ts(nbias[:, q:q + 1], rmx[:, q:q + 1], -(DD ** -0.5), None, ALU.mult).then_inc(s("d_max"), 1)
                dve.wait_ge(s("d_exp"), 2 * (NT * h + t) + 4)
                q = 2 * (t % 2)
                dve.reciprocal(rinv[:, q:q + 2], rsum[:, q:q + 2])
                dve.drain()
                stt(cfac[:, 0:1], rsum[:, q:q + 1], rinv[:, q + 1:q + 2], nlam, ALU.mult, ALU.mult)
                dve.drain()
                stt(prob[:, t % 2, 0, :], prob[:, t % 2, 1, :], cfac[:, 0:1], prob[:, t % 2, 0, :], ALU.mult, ALU.add)\
                    .then_inc(s("d_comb"), 1)
                if ahead:
                    fill_d(h + 1, t)

        for step in range(NT):
            fill_d(0, step)
        with dve.Fori(0, DH // 2 - 1) as i:
            for b in range(2):
                head_d(2 * i + b, True)
        head_d(DH - 2, True)
        head_d(DH - 1, False)

        for n in range(RH * NT):
            dve.bn_aggr(mv[:, 2 * n:2 * n + 2], bn6[:, 6 * n:6 * n + 6])
        sqr = tables[:, 0:2 * D].rearrange("p (b n) -> p b n", b=2)
        dve.wait_ge(s("d_ofree"), NT * DH + 1)
        for t in range(NT):
            tt(sqr[:, t % 2, :], o_sb[:, t, :], o_sb[:, t, :], ALU.mult)
            dve.drain()
            dve.tensor_reduce(ssq[:, 16 + t * DH:16 + (t + 1) * DH], sqr[:, t % 2, :].rearrange("p (h n) -> p h n", n=P), AX.X, ALU.add)
        dve.drain()
        dve.sem_inc(s("q_sq"), 1)
        vbias = vT[:, B_MOD + 16:B_MOD + 48]
        mod2 = modps[:, 16:48, 0]
        for v, (col, gain) in enumerate(((24, POST_FFN), (0, POST_MIX), (16, PRE_FFN), (8, None))):
            tt(colv[:, v, :], mod2[:, col:col + 8], vbias[:, col:col + 8], ALU.add)
            dve.drain()
            if gain is not None:
                stt(colv[:, v, :], colv[:, v, :], 1.0 if v == 2 else 0.0, vT[:, gain:gain + 8], ALU.add, ALU.mult)
                dve.drain()
        dve.wait_ge(s("br_rms"), 2)
        dve.reciprocal(rq[:, 0:48], rmsq[:, 0:48])
        dve.drain()
        mv3 = mv.rearrange("p (h t j) -> p h t j", h=RH, t=NT)
        rq_r = rq[:, 0:16].rearrange("p (h t) -> p h t", h=RH)
        for t in range(NT):
            y3 = y_sb[:, t, :].rearrange("p (h n) -> p h n", h=RH)
            tt(y3, y3, mv3[:, :, t, 0:1].to_broadcast([P, RH, RDV]), ALU.subtract)
            dve.drain()
            tt(y3, y3, rq_r[:, :, t:t + 1].to_broadcast([P, RH, RDV]), ALU.mult)
            dve.drain()
            tt(y_sb[:, t, :], y_sb[:, t, :], sg_sb[:, t, :], ALU.mult).then_inc(s("branch_normed"), 1)
        for t in range(NT):
            o3 = o_sb[:, t, :].rearrange("p (h n) -> p h n", h=DH)
            tt(o3, o3, rq[:, 16 + t * DH:16 + (t + 1) * DH].unsqueeze(2).to_broadcast([P, DH, P]), ALU.mult)\
                .then_inc(s("branch_normed"), 1)
        for n in range(32):
            if n >= 4:
                dve.wait_ge(s("row_mm"), n - 3)
            k = n % 4
            ts(row_diag[:, k, :], ident, colv[:, n // 8, n % 8:n % 8 + 1], None, ALU.mult).then_inc(s("diag8"), 1)
        dve.wait_ge(s("branch_normed"), 2 * NT)
        for n in range(2 * NT):
            t, dst, gain = n % NT, (zT if n < NT else onT), (RET_GN if n < NT else DIFF_GN)
            dve.wait_ge(s("branch_turned"), n + 1)
            bank = 6 * (n % 2)
            tt(dst[:, :, t * P:(t + 1) * P], ps[:, bank:bank + 2, :].rearrange("p b (k n) -> p (b k) n", n=P),
               vT[:, gain:gain + 8].unsqueeze(2).to_broadcast([P, KT, P]), ALU.mult).then_inc(s("branch_copied"), 1)
        dve.sem_inc(s("br_free"), 8)
        dve.wait_ge(s("g_free"), 16 + 4)
        with dve.Fori(0, 2) as n:
            for b in range(2):
                for t in range(NT):
                    dve.wait_ge(s("br_proj"), 8 * n + 4 * b + t + 1)
                    g = gate[:, bass.ds(n + 2 * b, 1), t, :].rearrange("p o c -> p (o c)")
                    tt(g, ps[:, 4 * b + t, :], g, ALU.mult).then_inc(s("br_free"), 1)
                    if b == 1:
                        g0 = gate[:, bass.ds(n, 1), t, :].rearrange("p o c -> p (o c)")
                        dve.wait_ge(s("br_free"), 8 * n + 4 * b + t + 9)
                        tt(m_sb[:, t, bass.ds(n * 512, 512)], g0, g, ALU.add).then_inc(s("m_ready"), 1)
        dve.wait_ge(s("row_copied"), 8)
        dve.wait_ge(s("ld_x2"), 16)
        for t in range(NT):
            for n in range(2):
                dve.wait_ge(s("mix"), 2 * t + n + 1)
                cp(x1[:, t, n * 512:(n + 1) * 512], ps[:, 4 + 2 * (t % 2) + n, :]).then_inc(s("mix_out"), 1)
            dve.wait_ge(s("mix_rms"), t + 1)
            dve.reciprocal(rstd[:, t:t + 1], rms[:, t:t + 1])
            dve.drain()
            stt(x1[:, t, :], x1[:, t, :], rstd[:, t:t + 1], row_ga, ALU.mult, ALU.mult)
            dve.drain()
            tt(x1[:, t, :], x1[:, t, :], x_again[:, t, :], ALU.add).then_inc(s("x1_ready"), 1)
            dve.wait_ge(s("x1_rms"), t + 1)
            dve.reciprocal(rstd[:, 4 + t:5 + t], rms[:, 4 + t:5 + t])
            dve.drain()
            stt(f_sb[:, t, :], x1[:, t, :], rstd[:, 4 + t:5 + t], row_af, ALU.mult, ALU.mult)
            dve.drain()
            tt(f_sb[:, t, :], f_sb[:, t, :], row_bf, ALU.add).then_inc(s("f_ready"), 1)

        def topk(h, t, first=False):
            m = NT * h + t
            dve.drain()
            if t == 0:
                for a in range(2):
                    dve.wait_ge(s("scored"), 2 * h + a + 1)
            if not first:
                dve.wait_ge(s("v_used"), TOPK * (m - 3) + V_CREDIT)
            stand(dve, "dve")
            sc = [ps[:, 6 + a, t * P:(t + 1) * P] for a in range(2)]
            for a in range(2):
                dve.max(top_v[:, a, 0:8], sc[a])
            dve.drain()
            for a in range(2):
                dve.max_index(top_i[:, a, 0:8], top_v[:, a, 0:8], sc[a])
                dve.match_replace(left[:, a, :], top_v[:, a, 0:8], sc[a], NEG)
            dve.drain()
            for a in range(2):
                dve.max(top_v[:, a, 8:16], left[:, a, :])
            dve.drain()
            for a in range(2):
                dve.max_index(top_i[:, a, 8:16], top_v[:, a, 8:16], left[:, a, :])
            tt(cand.rearrange("p (i j) -> p i j", i=TOPK), top_v[:, 0, :].unsqueeze(2).to_broadcast([P, TOPK, TOPK]),
               top_v[:, 1, :].unsqueeze(1).to_broadcast([P, TOPK, TOPK]), ALU.add)
            dve.drain()
            dve.sem_inc(s("topk_done"), 1)
            cp(top_f, top_i)
            dve.max(fin_v[:, 0:8], cand)
            dve.drain()
            dve.max_index(pos[:, 0:8], fin_v[:, 0:8], cand)
            dve.match_replace(cand2, fin_v[:, 0:8], cand, NEG)
            dve.drain()
            dve.max(fin_v[:, 8:16], cand2)
            dve.drain()
            dve.max_index(pos[:, 8:16], fin_v[:, 8:16], cand2)
            ts(logit[:, t, :], fin_v, fin_v[:, 0:1], None, ALU.subtract)
            dve.drain()
            ts(ab_i[:, 0, :], pos, 4, None, ALU.logical_shift_right)
            ts(ab_i[:, 1, :], pos, 15, None, ALU.bitwise_and)
            dve.drain()
            cp(ab_f, ab_i.rearrange("p a n -> p (a n)"))
            dve.drain()
            hot3 = hot.rearrange("p (m j) -> p m j", j=TOPK)
            hot4 = hot.rearrange("p (a m j) -> p a m j", a=2, j=TOPK)
            tt(hot3, ab_f.unsqueeze(2).to_broadcast([P, 32, TOPK]), iota16.unsqueeze(1).to_broadcast([P, 32, TOPK]), ALU.is_equal)
            dve.drain()
            tt(hot4, hot4, top_f.unsqueeze(2).to_broadcast([P, 2, TOPK, TOPK]), ALU.mult)
            dve.drain()
            dve.tensor_reduce(ij.rearrange("p a n -> p (a n)"), hot3, AX.X, ALU.add)
            dve.drain()
            stt(idxs[:, t, :], ij[:, 0, :], float(PK), ij[:, 1, :], ALU.mult, ALU.add).then_inc(s("idx_ready"), 1)

        def unit(h, t, ahead=True):
            n, b = NT * h + t, t % 2
            dve.drain()
            for e in range(TOPK):
                dve.wait_ge(s(f"u_in_{e % USLOTS}"), 32 * n + 16 * (e // USLOTS) + 16)
                dve.tensor_tensor_reduce(uslot[:, e % USLOTS, :], uslot[:, e % USLOTS, :], f_sb[:, t, :], 1.0, 0.0,
                                         ALU.mult, ALU.add, dots[:, b, e:e + 1]).then_inc(s("u_used"), 1)
            if ahead:
                topk(h + (t + 2) // NT, (t + 2) % NT)
            dve.wait_ge(s("v_used"), TOPK * (n - 1) + V_CREDIT)
            accumulate(t + 2)
            dve.wait_ge(s("gelu_done"), n + 1)
            dve.reciprocal(sinv[:, b:b + 1], ssum[:, b:b + 1])
            dve.drain()
            stt(wgt[:, b, :], gel[:, b, :], sinv[:, b:b + 1], soft[:, b, :], ALU.mult, ALU.mult).then_inc(s("w_ready"), 1)

        def accumulate(t):
            a3 = acc[:, t % NT, :].rearrange("p (b n) -> p b n", b=2)
            return tt(a3, a3, ps[:, 2 * (t % 2):2 * (t % 2) + 2, :], ALU.add).then_inc(s("acc_added"), 1)

        dve.sem_inc(s("u_used"), USLOTS)
        dve.wait_ge(s("mix"), 2 * NT)
        dve.memset(wring[:, 3584:3584 + NT * D], 0.0)
        dve.wait_ge(s("f_copied"), NT)
        dve.memset(ps[:, 0:4, :], 0.0)
        topk(0, 0, first=True)
        topk(0, 1, first=True)
        with dve.Fori(0, PH - 1) as h:
            for t in range(NT):
                unit(h, t)
        for t in range(NT):
            unit(PH - 1, t, ahead=t < 2)
        for t in range(2):
            dve.wait_ge(s("v_used"), TOPK * (NT * PH - 1 + t) + V_CREDIT)
            accumulate(t + 2)
        dve.drain()
        dve.sem_inc(s("acc_final"), NT)
        for t in range(NT):
            dve.wait_ge(s("y_rms"), t + 1)
            dve.reciprocal(rstd[:, t:t + 1], rms[:, t:t + 1])
            dve.drain()
            stt(acc[:, t, :], acc[:, t, :], rstd[:, t:t + 1], row_gf, ALU.mult, ALU.mult)
            dve.drain()
            tt(acc[:, t, :], acc[:, t, :], x1[:, t, :], ALU.add).then_inc(s("y_ready"), 1)

    @block.gpsimd
    def _(pool):
        def rows_of(table, dst, n, t, half, kind, need):
            for k in range(USLOTS):
                e = half * USLOTS + k
                pool.wait_ge(s(kind + "_used"), TOPK * n + e + 1 + need)
                stand(pool, "pool")
                pool.indirect_dma_start(out=dst[:, k, :], out_offset=None, in_=table,
                                        in_offset=bass.IndirectOffsetOnAxis(ap=idxs[:, t, e:e + 1], axis=0))\
                    .then_inc(s(f"{kind}_in_{k}"), 16)

        def u_rows(n, t, half):
            if half == 0:
                pool.wait_ge(s("idx_ready"), n + 1)
                stand(pool, "pool")
            rows_of(peer_u[:, :], uslot, n, t, half, "u", 0)

        def v_rows(n, t, half):
            rows_of(peer_v[:, :], vslot, n, t, half, "v", V_CREDIT - VSLOTS)

        for half in range(2):
            u_rows(0, 0, half)
        with pool.Fori(0, PH - 1) as h:
            for t in range(NT):
                for half in range(2):
                    u_rows(NT * h + t + 1, (t + 1) % NT, half)
                    v_rows(NT * h + t, t, half)
        for t in range(NT):
            n = NT * (PH - 1) + t
            for half in range(2):
                if t + 1 < NT:
                    u_rows(n + 1, t + 1, half)
                v_rows(n, t, half)

    es.close()


def kernel(**inputs):
    import concourse.bacc as bacc
    from concourse.bass_utils import run_bass_kernel_spmd

    nc = bacc.Bacc("TRN2", target_bir_lowering=False, num_devices=1)
    a = {k: np.asarray(v) for k, v in inputs.items()}
    small, dist, rope = shape_constants()
    blocks = [a[k][0].reshape(-1, P) for k in ("b_mod", "pre_mix_g", "post_mix_g", "pre_ffn_g", "post_ffn_g",
                                               "ret_gn_g", "diff_gn_g")]
    given = {
        "x": a["x"][0], "ctx": a["ctx"][0], "c_pair": np.stack([a["c"][0], a["c_ctx"]], axis=-1),
        "w_mod": a["w_mod"][0], "rows": np.concatenate(blocks, axis=0), "w_in": a["w_in"][0],
        "decays": np.concatenate([a["ret_decay_fwd"][0], a["ret_decay_bwd"][0]]),
        "lam": a["diff_lambda"][0].reshape(-1), "w_br_ret": a["w_br_ret"][0], "w_br_diff": a["w_br_diff"][0],
        "w_out": a["w_out"][0], "w_q": a["peer_w_q"][0], "keys": a["peer_sub_keys"][0],
        "peer_u": a["peer_u"][0], "peer_v": a["peer_v"][0], "small": small, "dist": dist, "rope": rope,
    }
    arrays, args = {}, {}
    for name, value in given.items():
        arrays["in_" + name] = np.ascontiguousarray(value)
        args[name] = nc.dram_tensor("in_" + name, value.shape, mybir.dt.from_np(value.dtype), kind="ExternalInput").ap()
    out = nc.dram_tensor("out_y", (T, D), F32, kind="ExternalOutput").ap()
    build(nc, out=out, **args)
    result = run_bass_kernel_spmd(nc, [arrays], core_ids=[0])
    return result.results[0]["out_y"].reshape(1, T, D)
```

```python
import math
from contextlib import ExitStack

import numpy as np

import concourse.bass as bass
from concourse import mybir

F32 = mybir.dt.float32
F32R = mybir.dt.float32r
U32 = mybir.dt.uint32
ACT = mybir.ActivationFunctionType
ALU = mybir.AluOpType
AX = mybir.AxisListType

P = 128
D = 1024
KT = D // P
T = 512
TC = 256
TA = T + TC
NT = T // P
NTA = TA // P
GRID_W = 64
EPS = 1e-6
LAM_INIT = 0.8 - 0.6 * math.exp(0.0)

RH, RDK, RDV = 4, 128, 256
DH, DD = 8, 64
RQ0, RK0 = 0, RH * RDK
RV0 = RK0 + RH * RDK
RG0 = RV0 + RH * RDV
DQ0 = RG0 + RH * RDV
DK0 = DQ0 + DH * 2 * DD
DV0 = DK0 + DH * 2 * DD
GR0 = DV0 + DH * 2 * DD

PH, PK, TOPK = 8, 128, 16
PDK = 256
USLOTS = VSLOTS = 8
NDIAG = 4
V_CREDIT = 32

LAG_W = (NT - 1) * P
M1W = 2 * NT * P - P
M2W = T + TC - P
G1 = 256
ROPE_W = 384
NEG = -3.0e38

B_MOD, PRE_MIX, POST_MIX, PRE_FFN, POST_FFN, RET_GN, DIFF_GN, NROWS = 0, 48, 56, 64, 72, 80, 88, 96


FILL = ((("p", 0), ("p", 1), ("t", 0)), (("p", 2), ("t", 1), ("m", 0)),
        (("p", 3), ("t", 2), ("p", 4), ("t", 3)), (("t", 4), ("p", 5), ("m", 1)))


def shape_constants():
    p = np.arange(P, dtype=np.float32)[:, None]
    d1 = np.arange(M1W, dtype=np.float32)[None, :] - LAG_W - p
    d2 = np.arange(M2W, dtype=np.float32)[None, :] - (TC - P) - p
    dist = np.concatenate([np.maximum(d1, 0), np.maximum(-d1, 0), d2 + TC, T - d2], axis=1)
    small = np.concatenate([np.eye(P, dtype=np.float32), np.tile(np.arange(16, dtype=np.float32), (P, 1))], axis=1)
    tok = np.arange(T)
    pos = np.stack([tok // GRID_W, tok % GRID_W], axis=1).astype(np.float32)

    def table(half):
        inv = np.power(np.float32(10000.0), -(np.arange(half, dtype=np.float32) / np.float32(half))).astype(np.float32)
        ang = (pos[:, :, None] * inv).astype(np.float32)
        cos, sin = np.cos(ang), np.sin(ang)
        both = np.stack([cos, cos], axis=2).reshape(T, 4 * half)
        return [both, (-sin).reshape(T, 2 * half), sin.reshape(T, 2 * half)]

    rope = np.concatenate(table(RDK // 4) + table(DD // 4), axis=1)
    return small.astype(np.float32), dist.astype(np.float32), rope.astype(np.float32)


def build(nc, x, ctx, c_pair, w_mod, rows, w_in, decays, lam, w_br_ret, w_br_diff, w_out,
          w_q, keys, peer_u, peer_v, small, dist, rope, out, debug=None):
    es = ExitStack()

    place = {}

    def sb(name, width, dt=F32):
        t = es.enter_context(nc.sbuf_tensor(name, [P, width], dt))
        place[name] = nc.sbuf_base - 4 * width
        return t

    def half_of(name, region, first, width):
        return nc.alloc_sbuf_tensor_at(name, [P, width], F32R, offset=place[region] + 4 * first)

    ps = es.enter_context(nc.psum_tensor("ps", [P, 8, 512], F32))
    wring = sb("wring", 14336)
    region_y = sb("region_ab", 2 * NT * D)
    region_o = sb("region_o", NT * D)
    region_z = sb("region_z", NT * D)
    region_u = sb("region_u", KT * TA)
    work = sb("work", 8 * D)
    tables = sb("tables", 2 * M1W + 3 * M2W + M1W)
    rope_t = sb("rope_t", NT * ROPE_W)
    small_t = sb("small_t", P + 16)
    vT = sb("vT", NROWS)
    stat = sb("stat", 672)
    ones = sb("ones", P)

    def ks(ap, k=KT):
        return ap.rearrange("p (k n) -> p k n", k=k)

    UW = KT * TA
    u_raw = ks(wring[:, 0:UW])
    u_lo, u_hi = ks(half_of("u_lo", "wring", 0, UW)[:, :]), ks(half_of("u_hi", "region_u", 0, UW)[:, :])
    GW = KT * G1
    slots = []
    for n, (region, name, first) in enumerate(((wring, "wring", UW), (wring, "wring", UW + 2 * GW), (region_o, "region_o", 0))):
        slots.append((ks(region[:, first:first + GW]), ks(half_of(f"w_lo_{n}", name, first, GW)[:, :]),
                      ks(half_of(f"w_hi_{n}", name, first + GW, GW)[:, :])))
    gate_raw = [ks(region_z[:, b * GW:(b + 1) * GW]) for b in range(2)]
    DW, DHALF = KT * 3 * P, KT // 2 * 3 * P
    d_raw = [ks(wring[:, UW:UW + DW]), ks(tables[:, 0:DW])]
    d_lo = [ks(half_of("d_lo_0", "wring", UW, DW)[:, :]), ks(half_of("d_lo_1", "tables", 0, DW)[:, :])]
    d_hi_0 = half_of("d_hi_0", "wring", UW + DW, DW)
    d_hi = [[ks(d_hi_0[:, j * DHALF:(j + 1) * DHALF], KT // 2) for j in range(2)],
            [ks(half_of("d_hi_1a", "tables", DW, DHALF)[:, :], KT // 2),
             ks(half_of("d_hi_1b", "region_z", 0, DHALF)[:, :], KT // 2)]]
    mod_w = ks(region_z[:, DHALF:DHALF + GW])
    mod_row = region_z[0:2, DHALF + GW:DHALF + GW + 512]
    WC = [r[:, 0:KT * 512].rearrange("p (k n) -> p k n", k=KT)
          for r in (wring[:, UW:UW + KT * 512], wring[:, UW + KT * 512:], region_z, region_u)]
    ident, iota16 = small_t[:, 0:P], small_t[:, P:P + 16]
    mT = fT = region_u[:, 0:KT * T].rearrange("p (k t) -> p k t", k=KT)
    y_sb = region_y[:, 0:NT * D].rearrange("p (t n) -> p t n", t=NT)
    sg_sb = region_y[:, NT * D:].rearrange("p (t n) -> p t n", t=NT)
    onT = region_y[:, NT * D:].rearrange("p (k t) -> p k t", k=KT)
    x_in = region_y[:, 0:NTA * D].rearrange("p (t n) -> p t n", t=NTA)
    m_sb = y_sb
    o_sb = region_o[:, :].rearrange("p (t n) -> p t n", t=NT)
    x1 = o_sb
    zT = region_z[:, :].rearrange("p (k t) -> p k t", k=KT)
    f_sb = region_z[:, :].rearrange("p (t n) -> p t n", t=NT)
    gate = work[:, :].rearrange("p (n t c) -> p n t c", n=4, t=NT)
    uslot = work[:, :].rearrange("p (s n) -> p s n", s=USLOTS)
    vslot = region_y[:, :].rearrange("p (s n) -> p s n", s=VSLOTS)
    d_pos, d_neg = tables[:, 0:M1W], tables[:, M1W:2 * M1W]
    c_fwd, c_bwd = tables[:, 2 * M1W:2 * M1W + M2W], tables[:, 2 * M1W + M2W:2 * M1W + 2 * M2W]
    mask1 = tables[:, 2 * M1W + 2 * M2W:3 * M1W + 2 * M2W]
    mask2 = tables[:, 3 * M1W + 2 * M2W:3 * M1W + 3 * M2W]
    row_gf, row_ga, row_af, row_bf = (tables[:, i * D:(i + 1) * D] for i in range(4))
    ropes = rope_t[:, :].rearrange("p (t n) -> p t n", t=NT)

    at = [0]

    def piece(region, n, dt=None):
        a = region[:, at[0]:at[0] + n]
        at[0] += n
        return a if dt is None else a.bitcast(dt)

    at[0] = 0
    qT, kT = piece(work, T), piece(work, TA)
    v_sb = piece(work, NTA * RDV).rearrange("p (t n) -> p t n", t=NTA)
    rot = piece(work, 512).rearrange("p (b n) -> p b n", b=2)
    t1 = piece(work, 512).rearrange("p (b n) -> p b n", b=2)
    t2 = piece(work, 512).rearrange("p (b n) -> p b n", b=2)
    shared = at[0]
    aT = piece(work, NTA * T).rearrange("p (j n) -> p j n", j=NTA)
    eg = piece(work, 2 * RDV).rearrange("p (b n) -> p b n", b=2)
    at[0] = shared
    prob = piece(work, 4 * TA).rearrange("p (b a n) -> p b a n", b=2, a=2)
    dT = piece(work, TA)
    assert at[0] <= 8 * D
    at[0] = 0
    second = wring[:, UW + 2 * DW:]
    qTd = [qT, piece(second, T)]
    kTd = [kT, piece(second, TA)]
    v_d = [v_sb[:, :, 0:P], piece(second, NTA * P).rearrange("p (t n) -> p t n", t=NTA)]
    mod_row1 = work[0:2, 2048:4096]
    at[0] = 0
    cin = piece(stat, 2 * KT)
    csig = piece(stat, 2 * KT)
    csil = piece(stat, 2 * KT).rearrange("p (k j) -> p k j", j=2)
    eps_t = piece(stat, 1)
    ss, rms, rstd = piece(stat, 8), piece(stat, 8), piece(stat, 8)
    modv = piece(stat, 32).rearrange("p (k j) -> p k j", j=2)
    scaleA = piece(stat, 2 * KT).rearrange("p (k j) -> p k j", j=2)
    dec, dec_e, dec_y, dec_l, dec_r = (piece(stat, 2 * RH) for _ in range(5))
    lsum, lexp, nlam = piece(stat, 2), piece(stat, 2), piece(stat, 1)
    bn6 = piece(stat, RH * NT * 6)
    mv = piece(stat, RH * NT * 2)
    rmx, nbias, rsum, rinv, cfac = (piece(stat, 4) for _ in range(5))
    colv = piece(stat, 4 * KT).rearrange("p (v k) -> p v k", v=4)
    ssq, rmsq, rq = (piece(stat, 2 * NT * DH) for _ in range(3))
    assert at[0] <= 672, at[0]
    rowsT = work[:, 0:P]
    lamb = work[:, P:P + 256]
    lamp = work[:, P + 256:P + 384]
    row_diag = tables[:, 4 * D:4 * D + 512].rearrange("p (b n) -> p b n", b=4)
    square_u = region_y[:, NTA * D:].rearrange("p (b n) -> p b n", b=2)
    beside = [wring[:, 0:UW // 2], wring[:, UW // 2:UW]]
    peer_t = beside[0][:, 0:2560]
    at[0] = 0
    top_v = piece(peer_t, 32).rearrange("p (a n) -> p a n", a=2)
    top_i = piece(peer_t, 32, U32).rearrange("p (a n) -> p a n", a=2)
    top_f = piece(peer_t, 32).rearrange("p (a n) -> p a n", a=2)
    left = piece(peer_t, 256).rearrange("p (a n) -> p a n", a=2)
    cand = piece(peer_t, 256)
    cand2 = piece(peer_t, 256)
    fin_v = piece(peer_t, 16)
    pos = piece(peer_t, 16, U32)
    ab_i = piece(peer_t, 32, U32).rearrange("p (a n) -> p a n", a=2)
    ab_f = piece(peer_t, 32)
    hot = piece(peer_t, 512)
    ij = piece(peer_t, 32).rearrange("p (a n) -> p a n", a=2)
    idxs = piece(peer_t, NT * 16, U32).rearrange("p (t n) -> p t n", t=NT)
    logit = piece(peer_t, NT * 16).rearrange("p (t n) -> p t n", t=NT)
    dots = piece(peer_t, 32).rearrange("p (b n) -> p b n", b=2)
    gel = piece(peer_t, 32).rearrange("p (b n) -> p b n", b=2)
    soft = piece(peer_t, 32).rearrange("p (b n) -> p b n", b=2)
    ssum, sinv = piece(peer_t, 2), piece(peer_t, 2)
    wgt = piece(peer_t, 32).rearrange("p (b n) -> p b n", b=2)
    diag = piece(peer_t, NDIAG * P).rearrange("p (b n) -> p b n", b=NDIAG)
    assert at[0] <= 2560, at[0]
    keys_t = beside[0][:, 2560:2816].rearrange("p (a n) -> p a n", a=2)
    keysT = beside[0][:, 2816:3072].rearrange("p (a n) -> p a n", a=2)
    wq_t = beside[1][:, 0:KT * PDK].rearrange("p (k n) -> p k n", k=KT)
    pqT = beside[1][:, KT * PDK:KT * PDK + 1024].rearrange("p (a n) -> p a n", a=2)
    acc = wring[:, UW:UW + NT * D].rearrange("p (t n) -> p t n", t=NT)
    square_b = rope_t[:, 0:D]
    modps = ps[:, 5, 416:512].rearrange("p (c j) -> p c j", j=2)

    made = {}

    def s(name):
        if name not in made:
            made[name] = es.enter_context(nc.semaphore(name))
        return made[name]

    stood = {}

    def stand(eng, name):
        eng.sem_inc(s("stood_" + name), 1)

    w_in_v = w_in.rearrange("(k p) n -> p k n", p=P)
    w_mod_v = w_mod.rearrange("(p k) n -> p k n", k=KT)
    br_v = [w.rearrange("(k p) n -> p k n", p=P) for w in (w_br_ret, w_br_diff, w_out)]
    w_q_v = w_q.rearrange("(k p) n -> p k n", p=P)
    x_v = x.rearrange("(t p) n -> p t n", p=P)
    ctx_v = ctx.rearrange("(t p) n -> p t n", p=P)
    out_v = out.rearrange("(t p) n -> p t n", p=P)
    C1 = 512

    block = es.enter_context(nc.Block())

    @block.sync
    def _(sp):
        def load(dst, src, name):
            return sp.dma_start(dst, src).then_inc(s(name), 16)

        load(cin, c_pair.rearrange("(p k) j -> p (k j)", k=KT), "ld_c")
        load(small_t[:, :], small, "ld_small")
        load(rowsT[0:NROWS, :], rows, "ld_rows")
        load(x_in[:, 0:NT, :], x_v, "ld_x")
        load(x_in[:, NT:NTA, :], ctx_v, "ld_ctx")
        load(dec, decays.partition_broadcast(P), "ld_dec")
        load(lamb, lam.partition_broadcast(P), "ld_lam")
        for n in range(4):
            load(WC[n], w_mod_v[:, :, n * C1:(n + 1) * C1], f"w_mod1_{n}")

        def ret_load(h, j):
            for dst, base, width in (((0, RQ0, RDK), (RDK, RK0, RDK)), ((0, RV0, RDV),), ((0, RG0, RDV),))[j]:
                load(slots[j][0][:, :, dst:dst + width], w_in_v[:, :, bass.ds(h * width + base, width)], f"ret_w_{j}")

        def diff_load(h, b):
            for j, base in enumerate((DQ0, DK0, DV0)):
                load(d_raw[b][:, :, j * P:(j + 1) * P], w_in_v[:, :, bass.ds(h * P + base, P)], f"diff_w_{b}")

        def mod_load(h, j):
            load(mod_w, w_mod_v[:, :, bass.ds(h * C1 + 4 * C1 + j * G1, G1)], "mod_w")

        sp.wait_ge(s("mod1_used"), 1)
        ret_load(0, 0)
        sp.wait_ge(s("mod1_used"), 2)
        ret_load(0, 1)
        load(rope_t[:, :].rearrange("p (t n) -> p t n", t=NT), rope.rearrange("(t p) n -> p t n", p=P), "ld_rope")
        load(tables[:, 0:2 * M1W + 2 * M2W], dist, "ld_dist")
        ret_load(0, 2)
        with sp.Fori(1, RH) as h:
            sp.wait_ge(s("r_proj"), 10 * h - 4)
            ret_load(h, 0)
            ret_load(h, 1)
            sp.wait_ge(s("r_proj"), 10 * h)
            ret_load(h, 2)
        sp.wait_ge(s("r_proj"), 10 * RH - 4)
        diff_load(0, 0)
        mod_load(0, 0)
        sp.wait_ge(s("r_masked"), 6 * RH + 3)
        diff_load(1, 1)
        sp.wait_ge(s("mod_used"), 1)
        mod_load(0, 1)

        def diff_step(h, b, ahead=True):
            sp.wait_ge(s("mod_used"), 2 * h)
            mod_load(h, 0)
            if ahead:
                sp.wait_ge(s("d_proj"), 6 * h)
                diff_load(h + 1, b)
            sp.wait_ge(s("mod_used"), 2 * h + 1)
            mod_load(h, 1)

        with sp.Fori(0, DH // 2 - 1) as i:
            diff_step(2 * i + 1, 0)
            diff_step(2 * i + 2, 1)
        diff_step(DH - 1, 0, ahead=False)
        for n in range(8):
            if n == 0:
                sp.wait_ge(s("mod_used"), 2 * DH)
            elif n == 1:
                sp.wait_ge(s("d_aturned"), NT * (DH - 1) + 1)
            else:
                sp.wait_ge(s("gate_split"), n - 1)
            load(gate_raw[n % 2], w_in_v[:, :, n * G1 + GR0:(n + 1) * G1 + GR0], f"gate_w_{n % 2}")
        for n in range(2):
            for b in range(2):
                if n == 0:
                    sp.wait_ge(s("g_proj"), 4 * (7 + b))
                else:
                    sp.wait_ge(s("br_proj"), 4 * (b + 1))
                load(WC[b], br_v[b][:, :, n * C1:(n + 1) * C1], f"br_w_{b}")
        load(wq_t, w_q_v[:, :, 0:PDK], "ld_wq")
        load(keys_t, keys[0].rearrange("a k d -> k a d"), "ld_wq")
        for b in range(2):
            sp.wait_ge(s("br_proj"), 8 + 4 * (b + 1))
            load(WC[b], br_v[2][:, :, b * C1:(b + 1) * C1], f"out_w_{b}")
        load(x1, x_v, "ld_x2")
        with sp.Fori(0, PH - 1) as h:
            sp.wait_ge(s("q_proj"), 2 * h + 2 * NT)
            load(wq_t, w_q_v[:, :, bass.ds(h * PDK + PDK, PDK)], "ld_wq")
            load(keys_t, keys[bass.ds(h + 1, 1)].rearrange("o a k d -> k (o a) d"), "ld_wq")
        for t in range(NT):
            sp.wait_ge(s("y_ready"), t + 1)
            load(out_v[:, t, :], acc[:, t, :], "stored")
        sp.wait_ge(s("stored"), NT * 16)

    @block.tensor
    def _(pe):
        def product(out_ap, lhs, rhs, n=KT):
            for k in range(n):
                last = pe.matmul(out_ap, lhs(k), rhs(k), start=(k == 0), stop=(k == n - 1))
            return last

        def product3(out_ap, t, hi, lo):
            tile = slice(t * P, (t + 1) * P)
            for k in range(KT):
                pe.matmul(out_ap, u_hi[:, k, tile], hi(k), start=(k == 0), stop=False)
                pe.matmul(out_ap, u_hi[:, k, tile], lo(k), start=False, stop=False)
                last = pe.matmul(out_ap, u_lo[:, k, tile], hi(k), start=False, stop=(k == KT - 1))
            return last

        def slot_product(out_ap, t, n):
            return product3(out_ap, t, lambda k: slots[n][2][:, k, :], lambda k: slots[n][1][:, k, :])

        pe.wait_ge(s("csil_ready"), 1)
        pe.wait_ge(s("ld_small"), 16)

        def turn_mod1(n):
            pe.wait_ge(s("mod1_row"), n + 1)
            for j in range(4):
                last = pe.transpose(modps[:, n * 4 + j, :], mod_row1[:, (4 * n + j) * P:(4 * n + j + 1) * P], ident[0:2, 0:2])
            last.then_inc(s("mod1_turned"), 1)

        for n in range(4):
            pe.wait_ge(s(f"w_mod1_{n}"), 16)
            product(ps[0:2, n, :], lambda k: csil[:, k, :], lambda k: WC[n][:, k, :]).then_inc(s("mod1_used"), 1)
            if n >= 1:
                turn_mod1(n - 1)
        turn_mod1(3)
        pe.wait_ge(s("ld_rows"), 16)
        pe.transpose(ps[:, 4, 0:NROWS], rowsT[0:NROWS, :], small_t[0:NROWS, 0:NROWS]).then_inc(s("rows_turned"), 1)
        for t in range(NTA):
            pe.wait_ge(s("xn_ready"), t + 1)
            if t >= 2:
                pe.wait_ge(s("ut_act"), t - 1)
                pe.wait_ge(s("ut_dve"), t - 1)
            for k in range(KT):
                last = pe.transpose(ps[:, 2 * (t % 2) + k // 4, (k % 4) * P:(k % 4 + 1) * P],
                                    x_in[:, t, k * P:(k + 1) * P], ident)
            last.then_inc(s("x_turned"), 1)

        pe.wait_ge(s("ut_split"), NTA)
        with pe.Fori(0, RH // 2) as i:
            for b in range(2):
                h = 2 * i + b

                def turn(t):
                    pe.wait_ge(s("r_took"), 10 * h + t + 3)
                    pe.wait_ge(s("r_tfree"), 6 * h + t + 1)
                    if t == 1:
                        pe.wait_ge(s("r_yfree"), NT * h + 2)
                    if t < NT:
                        pe.transpose(ps[:, 4 - t % 2, 0:P], rot[:, t % 2, 0:P], ident)
                    pe.transpose(ps[:, 4 - t % 2, P:2 * P], rot[:, t % 2, P:2 * P], ident).then_inc(s("r_turned"), 1)

                for u in range(NTA + NT):
                    if u == 0:
                        pe.wait_ge(s("ret_split"), 3 * h + 2)
                    elif u == NTA:
                        pe.wait_ge(s("ret_split"), 3 * h + 3)
                    if 2 <= u < NTA + 2:
                        pe.wait_ge(s("r_vcopied"), 6 * h + u - 1)
                    pe.wait_ge(s("r_took"), 10 * h + u + 1)
                    t = u % NTA
                    if u < NTA:
                        slot_product(ps[:, 6 + u % 2, 0:G1], t, 0)
                    slot_product(ps[:, 6 + u % 2, G1:2 * G1], t, 1 if u < NTA else 2).then_inc(s("r_proj"), 1)
                    if 1 <= u <= NTA:
                        turn(u - 1)
                pe.wait_ge(s("r_tfree"), 6 * h + NTA + 2)
                for j in range(NTA):
                    pe.wait_ge(s("r_masked"), 6 * h + j + 1)
                    mm = pe.matmul(ps[:, j % 3, :], kT[:, j * P:(j + 1) * P], qT[:, :], start=True, stop=True)
                    mm.then_inc(s("r_score"), 1)
                for t in range(NT):
                    if t == 0:
                        pe.wait_ge(s("r_masked"), 6 * h + NTA + 3)
                    pe.wait_ge(s("r_yfree"), NT * h + t + 1)
                    product(ps[:, 3 + 2 * (t % 2), 0:RDV], lambda j: aT[:, j, t * P:(t + 1) * P],
                            lambda j: v_sb[:, j, :], NTA).then_inc(s("r_y"), 1)

        def project(h, b, t):
            pe.wait_ge(s("d_tfree"), 6 * h + t + 1)
            if t in (0, 3):
                pe.wait_ge(s("d_row"), 2 * h + 1 + (1 if t else 0))
            lo = 0 if t < NT else P
            product3(ps[:, 6 + t % 2, lo:3 * P], t, lambda k: d_hi[b][k // 4][:, k % 4, lo:3 * P],
                     lambda k: d_lo[b][:, k, lo:3 * P]).then_inc(s("d_proj"), 1)

        def turn_d(h, t):
            pe.wait_ge(s("d_took"), 6 * h + t + 1)
            pe.wait_ge(s("d_vcopied"), 6 * h + t + 1)
            for a in range(0 if t < NT else 1, 2):
                last = pe.transpose(ps[:, 6 + t % 2, a * P:(a + 1) * P], rot[:, t % 2, a * P:(a + 1) * P], ident)
            last.then_inc(s("d_turned"), 1)

        def mod(h, u):
            pe.wait_ge(s("mod_w"), 32 * h + 16 * u + 16)
            pe.wait_ge(s("d_tfree"), 6 * h + 3 * u + 4)
            product(ps[0:2, 7 - u, 0:G1], lambda k: csil[:, k, :], lambda k: mod_w[:, k, :])\
                .then_inc(s("mod_used"), 1)

        def turn_mod(h):
            pe.wait_ge(s("d_row"), 2 * h + 3)
            for j in range(4):
                pe.matmul(modps[:, bass.ds(h * 4 + 16 + j, 1), :].rearrange("p c j -> p (c j)"),
                          mod_row[:, j * P:(j + 1) * P], ident[0:2, 0:2], start=True, stop=True)

        def fill(h, b, step):
            for kind, u in FILL[step]:
                if kind == "p":
                    project(h, b, u)
                elif kind == "t":
                    turn_d(h, u)
                else:
                    mod(h, u)

        def scores(h, b, t):
            for a in range(2):
                pe.wait_ge(s("d_exp"), 2 * (NT * h + t) + a + 1)
                for lo, hi in ((0, 512), (512, TA)):
                    mm = pe.matmul(ps[:, 2 * a + lo // 512, 0:hi - lo], qTd[b][a * DD:(a + 1) * DD, t * P:(t + 1) * P],
                                   kTd[b][a * DD:(a + 1) * DD, lo:hi], start=True, stop=True)
                mm.then_inc(s("d_score"), 1)

        def first_scores(h, b):
            pe.wait_ge(s("d_tfree"), 6 * h + NTA + 2)
            scores(h, b, 0)

        def head(h, b, ahead):
            for t in range(NT):
                if ahead:
                    if t == 0:
                        pe.wait_ge(s("diff_split"), h + 2)
                    fill(h + 1, 1 - b, t)
                pe.wait_ge(s("d_ofree"), NT * h + t + 1)
                if t == 0:
                    turn_mod(h)
                pe.wait_ge(s("d_comb"), NT * h + t + 1)
                for j in range(NTA):
                    mm = pe.transpose(ps[:, 4 + j // 4, (j % 4) * P:(j % 4 + 1) * P],
                                      prob[:, t % 2, 0, j * P:(j + 1) * P], ident)
                mm.then_inc(s("d_aturned"), 1)
                if t + 1 < NT:
                    scores(h, b, t + 1)
                elif ahead:
                    turn_d(h + 1, NTA - 1)
                pe.wait_ge(s("d_acopied"), NT * h + t + 1)
                product(ps[:, 5, 256:384], lambda j: dT[:, j * P:(j + 1) * P],
                        lambda j: v_d[b][:, j, :], NTA).then_inc(s("d_o"), 1)
            if ahead:
                first_scores(h + 1, 1 - b)

        pe.wait_ge(s("r_took"), 10 * RH + 2)
        pe.wait_ge(s("diff_split"), 1)
        for step in range(NT):
            fill(0, 0, step)
        turn_d(0, NTA - 1)
        first_scores(0, 0)
        with pe.Fori(0, DH // 2 - 1) as i:
            head(2 * i, 0, True)
            head(2 * i + 1, 1, True)
        head(DH - 2, 0, True)
        head(DH - 1, 1, False)

        def gate_piece(n, b, between=None):
            pe.wait_ge(s("gate_split"), n + 1)
            for t in range(NT):
                pe.wait_ge(s("g_free"), 4 * n + t + 1)
                slot_product(ps[:, t, 0:G1], t, b).then_inc(s("g_proj"), 1)
                if between is not None:
                    between(2 * t)
                    between(2 * t + 1)

        def row_half(n):
            if n >= 2:
                pe.wait_ge(s("row_copied"), n - 1)
            for k in range(4):
                pe.wait_ge(s("diag8"), 4 * n + k + 1)
                pe.matmul(ps[:, 6 + n % 2, k * P:(k + 1) * P], ones[:, :], row_diag[:, k, :],
                          start=True, stop=True).then_inc(s("row_mm"), 1)

        def turn_branch(n):
            t, src = n % NT, (y_sb if n < NT else o_sb)
            pe.wait_ge(s("branch_normed"), n + 1)
            if n >= 2:
                pe.wait_ge(s("branch_copied"), n - 1)
            elif n == 1:
                pe.wait_ge(s("row_copied"), 8)
            for k in range(KT):
                last = pe.transpose(ps[:, 4 + 2 * (n % 2) + k // 4, (k % 4) * P:(k % 4 + 1) * P],
                                    src[:, t, k * P:(k + 1) * P], ident)
            last.then_inc(s("branch_turned"), 1)

        with pe.Fori(0, 3) as i:
            for b in range(2):
                gate_piece(2 * i + b, b)
        gate_piece(6, 0, row_half)
        gate_piece(7, 1, turn_branch)
        pe.wait_ge(s("branch_copied"), 2 * NT)
        pe.wait_ge(s("g_free"), 32 + 4)
        with pe.Fori(0, 2) as n:
            for b in range(2):
                pe.wait_ge(s(f"br_w_{b}"), 16 * n + 16)
                src = zT if b == 0 else onT
                for t in range(NT):
                    pe.wait_ge(s("br_free"), 8 * n + 4 * b + t + 1)
                    product(ps[:, 4 * b + t, :], lambda k: src[:, k, t * P:(t + 1) * P],
                            lambda k: WC[b][:, k, :]).then_inc(s("br_proj"), 1)
        for t in range(NT):
            pe.wait_ge(s("m_ready"), NT + t + 1)
            if t >= 2:
                pe.wait_ge(s("m_copied"), t - 1)
            for k in range(KT):
                last = pe.transpose(ps[:, 2 * (t % 2) + k // 4, (k % 4) * P:(k % 4 + 1) * P], m_sb[:, t, k * P:(k + 1) * P], ident)
            last.then_inc(s("m_turned"), 1)
        for b in range(2):
            pe.wait_ge(s(f"out_w_{b}"), 16)

        def keys_of(h, bank):
            pe.wait_ge(s("ld_wq"), 32 * h + 32)
            for a in range(2):
                last = pe.transpose(ps[:, bank, a * P:(a + 1) * P], keys_t[:, a, :], ident)
            last.then_inc(s("keys_turned"), 1)

        def queries_of_tile(t):
            pe.wait_ge(s("f_ready"), t + 1)
            for k in range(KT):
                last = pe.transpose(ps[:, k // 4, (k % 4) * P:(k % 4 + 1) * P], f_sb[:, t, k * P:(k + 1) * P], ident)
            last.then_inc(s("f_turned"), 1)
            pe.wait_ge(s("f_copied"), t + 1)
            if t == 0:
                pe.wait_ge(s("keys_copied"), 1)
            for a in range(2):
                product(ps[:, 2 + a, 0:P], lambda k: wq_t[:, k, a * P:(a + 1) * P],
                        lambda k: fT[:, k, t * P:(t + 1) * P]).then_inc(s("q_proj"), 1)
            if t in (1, 2):
                pe.wait_ge(s("topk_done"), t)
            for a in range(2):
                pe.wait_ge(s("q_copied"), 2 * t + a + 1)
                last = pe.matmul(ps[:, 6 + a, t * P:(t + 1) * P], pqT[:, a, t * P:(t + 1) * P], keysT[:, a, :],
                                 start=True, stop=True)
            last.then_inc(s("scored"), 1)

        pe.wait_ge(s("m_copied"), NT)
        pe.sem_inc(s("v_used"), V_CREDIT)
        keys_of(0, 6)
        for t in range(NT):
            pe.wait_ge(s("m_copied"), t + 1)
            for n in range(2):
                if t >= 1:
                    pe.wait_ge(s("mix_out"), 2 * (t - 1) + n + 1)
                product(ps[:, 4 + n, :], lambda k: mT[:, k, t * P:(t + 1) * P],
                        lambda k: WC[n][:, k, :]).then_inc(s("mix"), 1)
            if t >= 1:
                queries_of_tile(t - 1)
        queries_of_tile(NT - 1)

        def queries(h):
            keys_of(h, 4)
            for a in range(2):
                if a == 1:
                    pe.wait_ge(s("q_copied"), 2 * (h + NT - 1) + 1)
                product(ps[:, 5, :], lambda k: wq_t[:, k, a * P:(a + 1) * P], lambda k: fT[:, k, :]).then_inc(s("q_proj"), 1)
            for a in range(2):
                pe.wait_ge(s("q_copied"), 2 * (h + NT - 1) + a + 1)
                if a == 0:
                    pe.wait_ge(s("keys_copied"), h + 1)
                for t in range(NT):
                    last = pe.matmul(ps[:, 6 + a, t * P:(t + 1) * P], pqT[:, a, t * P:(t + 1) * P], keysT[:, a, :],
                                     start=True, stop=True)
            last.then_inc(s("scored"), 1)

        def weighted_sum(h, t):
            n = NT * h + t
            pe.wait_ge(s("acc_added"), n + 1)
            for e in range(TOPK):
                pe.wait_ge(s(f"v_in_{e % VSLOTS}"), 32 * n + 16 * (e // VSLOTS) + 16)
                pe.wait_ge(s("diag_ready"), TOPK * n + e + 1)
                for half in range(2):
                    last = pe.matmul(ps[:, 2 * (t % 2) + half, :], diag[:, e % NDIAG, :],
                                     vslot[:, e % VSLOTS, half * 512:(half + 1) * 512],
                                     start=(e == 0), stop=(e == TOPK - 1))
                last.then_inc(s("v_used"), 1)

        pe.wait_ge(s("mix_out"), 2 * NT)
        with pe.Fori(0, PH - 1) as h:
            for t in range(NT):
                weighted_sum(h, t)
                if t == 0:
                    pe.wait_ge(s("topk_done"), NT * h + NT)
                    queries(h + 1)
        for t in range(NT):
            weighted_sum(PH - 1, t)

    @block.scalar
    def _(act):
        def do(out_ap, in_ap, func=ACT.Copy, **kw):
            return act.activation(out_ap, in_ap, func, **kw)

        act.wait_ge(s("ld_c"), 16)
        do(csig, cin, ACT.Sigmoid).then_inc(s("csig"), 1)
        act.wait_ge(s("eps_set"), 1)
        for t in range(NTA):
            if t in (0, NT):
                act.wait_ge(s("ld_x" if t == 0 else "ld_ctx"), 16)
            if t >= 2:
                act.drain()
            do(square_u[:, t % 2, :], x_in[:, t, :], ACT.Square, accum_out=ss[:, t:t + 1])
        act.drain()
        do(rms[:, 0:NTA], ss[:, 0:NTA], ACT.Sqrt, scale=1.0 / D, bias=eps_t).then_inc(s("x_rms"), 1)
        act.wait_ge(s("ld_dec"), 16)
        do(dec_e, dec, ACT.Exp, scale=math.log(2.0)).then_inc(s("dec_e"), 1)
        act.wait_ge(s("lam_sums"), 1)
        do(lexp, lsum, ACT.Exp).then_inc(s("lam_exp"), 1)
        act.wait_ge(s("dec_y"), 1)
        do(dec_l, dec_y, ACT.Ln).then_inc(s("dec_ln"), 1)
        act.wait_ge(s("mod_ready"), 1)
        for t in range(NTA):
            act.wait_ge(s("x_turned"), t + 1)
            j = 0 if t < NT else 1
            for k in range(4):
                last = do(u_raw[:, k, t * P:(t + 1) * P], ps[:, 2 * (t % 2), k * P:(k + 1) * P], ACT.Identity,
                          scale=scaleA[:, k, j:j + 1], bias=modv[:, k, j:j + 1])
            last.then_inc(s("ut_act"), 1)
            act.drain()
            do(u_hi[:, 0:4, t * P:(t + 1) * P], u_raw[:, 0:4, t * P:(t + 1) * P]).then_inc(s("ut_hi"), 1)

        act.sem_inc(s("r_tfree"), 2)
        act.sem_inc(s("r_yfree"), 2)
        act.wait_ge(s("ld_dist"), 16)
        act.wait_ge(s("dec_ready"), 1)
        with act.Fori(0, RH // 2) as i:
            for b in range(2):
                h = 2 * i + b
                act.wait_ge(s("r_dist"), h + 1)
                do(mask1, mask1, ACT.Exp).then_inc(s("r_mask"), 1)
                do(mask2, mask2, ACT.Exp).then_inc(s("r_mask"), 1)
                do(aT[:, 0:2, :].rearrange("p a n -> p (a n)")[:, 0:M2W],
                   aT[:, 0:2, :].rearrange("p a n -> p (a n)")[:, 0:M2W], ACT.Exp).then_inc(s("r_mask"), 1)

                def copy_t(t):
                    act.wait_ge(s("r_turned"), 6 * h + t + 1)
                    if t < NT:
                        do(qT[:, t * P:(t + 1) * P], ps[:, 4 - t % 2, 0:P], scale=RDK ** -0.5)
                    last = do(kT[:, t * P:(t + 1) * P], ps[:, 4 - t % 2, P:2 * P])
                    last.then_inc(s("r_tfree"), 1)

                for u in range(NTA + NT):
                    act.wait_ge(s("r_proj"), 10 * h + u + 1)
                    if u < NTA:
                        act.wait_ge(s("r_took"), 10 * h + u + 3)
                        do(v_sb[:, u, :], ps[:, 6 + u % 2, G1:2 * G1]).then_inc(s("r_vcopied"), 1)
                    else:
                        if u >= NTA + 2:
                            act.wait_ge(s("r_took"), 10 * h + u + 1)
                        do(eg[:, u % 2, :], ps[:, 6 + u % 2, G1:2 * G1], ACT.Exp, scale=-1.0).then_inc(s("r_eg"), 1)
                    if 1 <= u <= NTA:
                        copy_t(u - 1)
                for t in range(NT):
                    act.wait_ge(s("r_ystat"), NT * h + t + 1)
                    stand(act, "act")
                    do(y_sb[:, t, bass.ds(h * RDV, RDV)], ps[:, 3 + 2 * (t % 2), 0:RDV]).then_inc(s("r_yfree"), 1)

        act.sem_inc(s("d_tfree"), 2)
        act.sem_inc(s("d_exp"), 2)
        act.sem_inc(s("d_ofree"), 1)

        def copy_v(h, b, u):
            act.wait_ge(s("d_took"), 6 * h + u + 1)
            do(v_d[b][:, u, :], ps[:, 6 + u % 2, 2 * P:3 * P]).then_inc(s("d_vcopied"), 1)

        def copy_qk(h, b, t):
            act.wait_ge(s("d_turned"), 6 * h + t + 1)
            if t < NT:
                do(qTd[b][:, t * P:(t + 1) * P], ps[:, 6 + t % 2, 0:P])
            do(kTd[b][:, t * P:(t + 1) * P], ps[:, 6 + t % 2, P:2 * P]).then_inc(s("d_tfree"), 1)

        def fill(h, b, step):
            for kind, u in FILL[step]:
                if kind == "t":
                    copy_qk(h, b, u)
                elif kind == "p":
                    copy_v(h, b, u)

        def exps(h, t):
            for a in range(2):
                act.wait_ge(s("d_max"), 2 * (NT * h + t) + a + 1)
                table = ps[:, 2 * a:2 * a + 2, :].rearrange("p b n -> p (b n)")[:, 0:TA]
                do(prob[:, t % 2, a, :], table, ACT.Exp, scale=DD ** -0.5,
                   bias=nbias[:, 2 * (t % 2) + a:2 * (t % 2) + a + 1],
                   accum_out=rsum[:, 2 * (t % 2) + a:2 * (t % 2) + a + 1]).then_inc(s("d_exp"), 1)

        def head(h, b, ahead):
            exps(h, 0)
            for t in range(NT):
                if ahead:
                    fill(h + 1, 1 - b, t)
                act.wait_ge(s("d_aturned"), NT * h + t + 1)
                do(dT[:, :], ps[:, 4:6, :].rearrange("p b n -> p (b n)")[:, 0:TA]).then_inc(s("d_acopied"), 1)
                if t + 1 < NT:
                    exps(h, t + 1)
                elif ahead:
                    copy_qk(h + 1, 1 - b, NTA - 1)
                act.wait_ge(s("d_o"), NT * h + t + 1)
                stand(act, "act")
                do(o_sb[:, t, bass.ds(h * P, P)], ps[:, 5, 256:384], scale=rinv[:, 2 * (t % 2):2 * (t % 2) + 1])\
                    .then_inc(s("d_ofree"), 1)

        for step in range(NT):
            fill(0, 0, step)
        copy_qk(0, 0, NTA - 1)
        with act.Fori(0, DH // 2 - 1) as i:
            for b in range(2):
                head(2 * i + b, b, True)
        head(DH - 2, 0, True)
        head(DH - 1, 1, False)

        act.sem_inc(s("g_free"), 4)
        act.wait_ge(s("q_sq"), 1)
        do(rmsq[:, 0:16], mv.rearrange("p (n j) -> p n j", j=2)[:, :, 1], ACT.Sqrt, bias=eps_t).then_inc(s("br_rms"), 1)
        do(rmsq[:, 16:48], ssq[:, 16:48], ACT.Sqrt, scale=1.0 / P, bias=eps_t).then_inc(s("br_rms"), 1)
        def gate_hi(n, b):
            act.wait_ge(s(f"gate_w_{b}"), 8 * (n - b) + 16)
            stand(act, "act")
            do(slots[b][2], gate_raw[b]).then_inc(s("gate_hi"), 1)

        def sigmoids(n, i, b, between=None):
            for t in range(NT):
                act.wait_ge(s("g_proj"), 4 * n + t + 1)
                stand(act, "act")
                do(gate[:, bass.ds(i, 1), t, b * G1:(b + 1) * G1].rearrange("p o c -> p (o c)"), ps[:, t, 0:G1], ACT.Sigmoid)\
                    .then_inc(s("g_free"), 1)
                if between is not None:
                    between(2 * t)
                    between(2 * t + 1)

        def row_half(n):
            act.wait_ge(s("row_mm"), 4 * n + 4)
            dst = (row_gf, row_ga, row_af, row_bf)[n // 2]
            do(dst[:, (n % 2) * 512:(n % 2 + 1) * 512], ps[:, 6 + n % 2, :]).then_inc(s("row_copied"), 1)

        gate_hi(1, 1)
        with act.Fori(0, 3) as i:
            for b in range(2):
                sigmoids(2 * i + b, i, b)
                gate_hi(2 * i + b + 2, b)
        sigmoids(6, 3, 0, row_half)
        sigmoids(7, 3, 1)
        for t in range(NT):
            act.wait_ge(s("m_turned"), t + 1)
            do(mT[:, :, t * P:(t + 1) * P], ps[:, 2 * (t % 2):2 * (t % 2) + 2, :].rearrange("p b (k n) -> p (b k) n", n=P))\
                .then_inc(s("m_copied"), 1)
        act.wait_ge(s("keys_turned"), 1)
        do(keysT, ps[:, 6, 0:256].rearrange("p (a n) -> p a n", a=2)).then_inc(s("keys_copied"), 1)

        def copy_tile(t):
            act.wait_ge(s("f_turned"), t + 1)
            do(fT[:, :, t * P:(t + 1) * P], ps[:, 0:2, :].rearrange("p b (k n) -> p (b k) n", n=P)).then_inc(s("f_copied"), 1)
            for a in range(2):
                act.wait_ge(s("q_proj"), 2 * t + a + 1)
                do(pqT[:, a, t * P:(t + 1) * P], ps[:, 2 + a, 0:P]).then_inc(s("q_copied"), 1)

        for t in range(NT):
            for n in range(2):
                act.wait_ge(s("mix"), 2 * t + n + 1)
                do(f_sb[:, t, n * 512:(n + 1) * 512], ps[:, 4 + n, :]).then_inc(s("mix_out"), 1)
            act.drain()
            do(square_b, f_sb[:, t, :], ACT.Square, accum_out=ss[:, t:t + 1])
            act.drain()
            do(rms[:, t:t + 1], ss[:, t:t + 1], ACT.Sqrt, scale=1.0 / D, bias=eps_t).then_inc(s("mix_rms"), 1)
            if 1 <= t < NT - 1:
                copy_tile(t - 1)
                act.drain()
            act.wait_ge(s("x1_ready"), t + 1)
            do(square_b, x1[:, t, :], ACT.Square, accum_out=ss[:, 4 + t:5 + t])
            act.drain()
            do(rms[:, 4 + t:5 + t], ss[:, 4 + t:5 + t], ACT.Sqrt, scale=1.0 / D, bias=eps_t).then_inc(s("x1_rms"), 1)
        copy_tile(NT - 2)
        copy_tile(NT - 1)

        def copies(h):
            act.wait_ge(s("keys_turned"), h + 1)
            do(keysT, ps[:, 4, 0:256].rearrange("p (a n) -> p a n", a=2)).then_inc(s("keys_copied"), 1)
            for a in range(2):
                act.wait_ge(s("q_proj"), 2 * (h + NT - 1) + a + 1)
                do(pqT[:, a, :], ps[:, 5, :]).then_inc(s("q_copied"), 1)

        def square_sum(t):
            act.wait_ge(s("acc_added"), NT * PH - 1 + t)
            act.drain()
            do(square_b, acc[:, t, :], ACT.Square, accum_out=ss[:, t:t + 1])
            act.drain()
            do(rms[:, t:t + 1], ss[:, t:t + 1], ACT.Sqrt, scale=1.0 / D, bias=eps_t).then_inc(s("y_rms"), 1)

        def unit(h, t, last=False):
            n, b = NT * h + t, t % 2
            act.wait_ge(s("u_used"), TOPK * n + TOPK + USLOTS)
            do(soft[:, b, :], logit[:, t, :], ACT.Exp, accum_out=ssum[:, b:b + 1])
            do(gel[:, b, :], dots[:, b, :], ACT.Gelu)
            act.drain()
            act.sem_inc(s("gelu_done"), 1)
            act.wait_ge(s("w_ready"), n + 1)
            for e in range(TOPK):
                if last and e == USLOTS:
                    square_sum(0)
                    square_sum(1)
                act.wait_ge(s("v_used"), TOPK * n + e + 1 - NDIAG + V_CREDIT)
                do(diag[:, e % NDIAG, :], ident, scale=wgt[:, b, e:e + 1]).then_inc(s("diag_ready"), 1)

        with act.Fori(0, PH - 1) as h:
            for t in range(NT):
                unit(h, t)
                if t == 0:
                    copies(h + 1)
        for t in range(NT):
            unit(PH - 1, t, last=(t == NT - 1))
        square_sum(2)
        square_sum(3)

    @block.vector
    def _(dve):
        tt, ts, stt, cp = dve.tensor_tensor, dve.tensor_scalar, dve.scalar_tensor_tensor, dve.tensor_copy

        dve.memset(eps_t, EPS).then_inc(s("eps_set"), 1)
        dve.memset(ones[:, :], 1.0)
        dve.wait_ge(s("csig"), 1)
        tt(csil, cin.rearrange("p (k j) -> p k j", j=2), csig.rearrange("p (k j) -> p k j", j=2), ALU.mult)\
            .then_inc(s("csil_ready"), 1)
        dve.wait_ge(s("ld_lam"), 16)
        lam4 = lamb.rearrange("p (a b n) -> p a b n", a=2, b=2)
        tt(lamp.rearrange("p (a n) -> p a n", a=2), lam4[:, :, 0, :], lam4[:, :, 1, :], ALU.mult)
        dve.drain()
        dve.tensor_reduce(lsum, lamp.rearrange("p (a n) -> p a n", a=2), AX.X, ALU.add).then_inc(s("lam_sums"), 1)
        dve.wait_ge(s("x_rms"), 1)
        dve.reciprocal(rstd[:, 0:NTA], rms[:, 0:NTA])
        dve.drain()
        for t in range(NTA):
            ts(x_in[:, t, :], x_in[:, t, :], rstd[:, t:t + 1], None, ALU.mult).then_inc(s("xn_ready"), 1)
        dve.wait_ge(s("dec_e"), 1)
        ts(dec_y, dec_e, -1.0, 1.0, ALU.mult, ALU.add).then_inc(s("dec_y"), 1)
        dve.drain()
        ts(dec_r, dec_y, -1.0, 1.0, ALU.mult, ALU.add)
        dve.drain()
        ts(dec_r, dec_r, 1e-30, None, ALU.max)
        dve.drain()
        dve.reciprocal(dec_r, dec_r)
        dve.drain()
        tt(dec_r, dec_r, dec_e, ALU.mult)
        dve.drain()
        dve.wait_ge(s("dec_ln"), 1)
        tt(dec_l, dec_l, dec_r, ALU.mult).then_inc(s("dec_ready"), 1)
        dve.wait_ge(s("lam_exp"), 1)
        tt(nlam, lexp[:, 1:2], lexp[:, 0:1], ALU.subtract)
        dve.drain()
        ts(nlam, nlam, -LAM_INIT, None, ALU.add)
        for n in range(4):
            dve.wait_ge(s("mod1_used"), n + 1)
            cp(mod_row1[:, n * C1:(n + 1) * C1], ps[0:2, n, :]).then_inc(s("mod1_row"), 1)
        dve.wait_ge(s("rows_turned"), 1)
        cp(vT[:, :], ps[:, 4, 0:NROWS])
        dve.drain()
        dve.wait_ge(s("mod1_turned"), 4)
        tt(modv, modps[:, 0:16, :], vT[:, B_MOD:B_MOD + 16].unsqueeze(2).to_broadcast([P, 16, 2]), ALU.add)
        dve.drain()
        stt(scaleA, modv[:, 8:16, :], 1.0, vT[:, PRE_MIX:PRE_MIX + 8].unsqueeze(2).to_broadcast([P, 8, 2]),
            ALU.add, ALU.mult).then_inc(s("mod_ready"), 1)
        ts(vT[:, DIFF_GN:DIFF_GN + 8], vT[:, DIFF_GN:DIFF_GN + 8], 1.0 - LAM_INIT, None, ALU.mult)
        dve.drain()
        for t in range(NTA):
            dve.wait_ge(s("x_turned"), t + 1)
            j = 0 if t < NT else 1
            for k in range(4, KT):
                last = ts(u_raw[:, k, t * P:(t + 1) * P], ps[:, 2 * (t % 2) + 1, (k - 4) * P:(k - 3) * P],
                          scaleA[:, k, j:j + 1], modv[:, k, j:j + 1], ALU.mult, ALU.add)
            last.then_inc(s("ut_dve"), 1)
            tile = slice(t * P, (t + 1) * P)
            dve.drain()
            cp(u_hi[:, 4:KT, tile], u_raw[:, 4:KT, tile])
            dve.drain()
            dve.wait_ge(s("ut_hi"), t + 1)
            tt(u_lo[:, :, tile], u_raw[:, :, tile], u_hi[:, :, tile].bitcast(F32), ALU.subtract).then_inc(s("ut_split"), 1)

        def rotate(t, src, groups, half, table):
            w = 4 * half
            cos = ropes[:, t, table:table + w].unsqueeze(1).to_broadcast([P, groups, w])
            g = src.rearrange("p (g n) -> p g n", g=groups)
            sin = [ropes[:, t, table + w + i * 2 * half:table + w + (i + 1) * 2 * half]
                   .rearrange("p (x n) -> p x n", x=2).unsqueeze(1).to_broadcast([P, groups, 2, half]) for i in range(2)]
            src5 = src.rearrange("p (g x f n) -> p g x f n", g=groups, x=2, f=2)
            dst5 = t2[:, t % 2, :].rearrange("p (g x f n) -> p g x f n", g=groups, x=2, f=2)
            tt(t1[:, t % 2, :].rearrange("p (g n) -> p g n", g=groups), g, cos, ALU.mult)
            tt(dst5[:, :, :, 0, :], src5[:, :, :, 1, :], sin[0], ALU.mult)
            tt(dst5[:, :, :, 1, :], src5[:, :, :, 0, :], sin[1], ALU.mult)
            dve.drain()
            return tt(rot[:, t % 2, :], t1[:, t % 2, :], t2[:, t % 2, :], ALU.add)

        dve.sem_inc(s("r_took"), 2)
        dve.sem_inc(s("r_masked"), 3)
        dve.wait_ge(s("ld_rope"), 16)
        dve.wait_ge(s("ld_dist"), 16)
        with dve.Fori(0, RH // 2) as i:
            for b in range(2):
                h = 2 * i + b
                lf, lb = dec_l[:, bass.ds(h, 1)], dec_l[:, bass.ds(h + RH, 1)]
                back = aT[:, 0:2, :].rearrange("p a n -> p (a n)")[:, 0:M2W]
                dve.drain()
                ts(mask1, d_neg, lb, None, ALU.mult)
                ts(mask2, c_fwd, lf, None, ALU.mult)
                ts(back, c_bwd, lb, None, ALU.mult)
                dve.drain()
                stt(mask1, d_pos, lf, mask1, ALU.mult, ALU.add).then_inc(s("r_dist"), 1)
                for u in range(NTA + NT):
                    t = u % NTA
                    bank = ps[:, 6 + u % 2, :]
                    if u < NTA:
                        dve.drain()
                        dve.wait_ge(s("r_proj"), 10 * h + u + 1)
                        if u < NT:
                            rotate(t, bank[:, 0:2 * RDK], 2, RDK // 4, 0).then_inc(s("r_took"), 1)
                        else:
                            cp(rot[:, t % 2, P:2 * P], bank[:, P:2 * P]).then_inc(s("r_took"), 1)
                    else:
                        dve.wait_ge(s("r_eg"), NT * h + t + 1)
                        e = eg[:, u % 2, :]
                        ts(e, e, 1.0, None, ALU.add)
                        dve.drain()
                        dve.reciprocal(e, e)
                        dve.drain()
                        tt(sg_sb[:, t, bass.ds(h * RDV, RDV)], bank[:, G1:2 * G1], e, ALU.mult).then_inc(s("r_took"), 1)
                dve.wait_ge(s("r_mask"), 3 * h + 3)
                tt(mask2, mask2, back, ALU.add)
                dve.drain()
                for j in range(NTA):
                    dve.wait_ge(s("r_score"), 6 * h + j + 1)
                    m = mask1[:, (NT - 1 - j) * P:(NT - 1 - j) * P + T] if j < NT else \
                        mask2[:, (NTA - 1 - j) * P:(NTA - 1 - j) * P + T]
                    tt(aT[:, j, :], ps[:, j % 3, :], m, ALU.mult).then_inc(s("r_masked"), 1)
                for t in range(NT):
                    dve.wait_ge(s("r_y"), NT * h + t + 1)
                    stand(dve, "dve")
                    dve.bn_stats(bn6[:, bass.ds((h * NT + t) * 6, 6)], ps[:, 3 + 2 * (t % 2), 0:RDV]).then_inc(s("r_ystat"), 1)

        dve.sem_inc(s("d_row"), 1)

        def take(h, t):
            bank = ps[:, 6 + t % 2, :]
            dve.drain()
            dve.wait_ge(s("d_proj"), 6 * h + t + 1)
            if t < NT:
                rotate(t, bank[:, 0:2 * P], 4, DD // 4, 256).then_inc(s("d_took"), 1)
            else:
                cp(rot[:, t % 2, P:2 * P], bank[:, P:2 * P]).then_inc(s("d_took"), 1)

        def fill_d(h, step):
            for kind, u in FILL[step]:
                if kind == "p":
                    take(h, u)
                elif kind == "m":
                    dve.wait_ge(s("mod_used"), 2 * h + u + 1)
                    cp(mod_row[:, u * G1:(u + 1) * G1], ps[0:2, 7 - u, 0:G1]).then_inc(s("d_row"), 1)

        def head_d(h, ahead):
            for t in range(NT):
                for a in range(2):
                    q = 2 * (t % 2) + a
                    dve.wait_ge(s("d_score"), 2 * (NT * h + t) + a + 1)
                    dve.tensor_reduce(rmx[:, q:q + 1], ps[:, 2 * a:2 * a + 2, :].rearrange("p b n -> p (b n)")[:, 0:TA],
                                      AX.X, ALU.max)
                    dve.drain()
                    ts(nbias[:, q:q + 1], rmx[:, q:q + 1], -(DD ** -0.5), None, ALU.mult).then_inc(s("d_max"), 1)
                dve.wait_ge(s("d_exp"), 2 * (NT * h + t) + 4)
                q = 2 * (t % 2)
                dve.reciprocal(rinv[:, q:q + 2], rsum[:, q:q + 2])
                dve.drain()
                stt(cfac[:, 0:1], rsum[:, q:q + 1], rinv[:, q + 1:q + 2], nlam, ALU.mult, ALU.mult)
                dve.drain()
                stt(prob[:, t % 2, 0, :], prob[:, t % 2, 1, :], cfac[:, 0:1], prob[:, t % 2, 0, :], ALU.mult, ALU.add)\
                    .then_inc(s("d_comb"), 1)
                if ahead:
                    fill_d(h + 1, t)

        for step in range(NT):
            fill_d(0, step)
        with dve.Fori(0, DH // 2 - 1) as i:
            for b in range(2):
                head_d(2 * i + b, True)
        head_d(DH - 2, True)
        head_d(DH - 1, False)

        for n in range(RH * NT):
            dve.bn_aggr(mv[:, 2 * n:2 * n + 2], bn6[:, 6 * n:6 * n + 6])
        sqr = tables[:, 0:2 * D].rearrange("p (b n) -> p b n", b=2)
        dve.wait_ge(s("d_ofree"), NT * DH + 1)
        for t in range(NT):
            tt(sqr[:, t % 2, :], o_sb[:, t, :], o_sb[:, t, :], ALU.mult)
            dve.drain()
            dve.tensor_reduce(ssq[:, 16 + t * DH:16 + (t + 1) * DH], sqr[:, t % 2, :].rearrange("p (h n) -> p h n", n=P), AX.X, ALU.add)
        dve.drain()
        dve.sem_inc(s("q_sq"), 1)
        vbias = vT[:, B_MOD + 16:B_MOD + 48]
        mod2 = modps[:, 16:48, 0]
        for v, (col, gain) in enumerate(((24, POST_FFN), (0, POST_MIX), (16, PRE_FFN), (8, None))):
            tt(colv[:, v, :], mod2[:, col:col + 8], vbias[:, col:col + 8], ALU.add)
            dve.drain()
            if gain is not None:
                stt(colv[:, v, :], colv[:, v, :], 1.0 if v == 2 else 0.0, vT[:, gain:gain + 8], ALU.add, ALU.mult)
                dve.drain()
        dve.wait_ge(s("br_rms"), 2)
        dve.reciprocal(rq[:, 0:48], rmsq[:, 0:48])
        dve.drain()
        mv3 = mv.rearrange("p (h t j) -> p h t j", h=RH, t=NT)
        rq_r = rq[:, 0:16].rearrange("p (h t) -> p h t", h=RH)
        for t in range(NT):
            y3 = y_sb[:, t, :].rearrange("p (h n) -> p h n", h=RH)
            tt(y3, y3, mv3[:, :, t, 0:1].to_broadcast([P, RH, RDV]), ALU.subtract)
            dve.drain()
            tt(y3, y3, rq_r[:, :, t:t + 1].to_broadcast([P, RH, RDV]), ALU.mult)
            dve.drain()
            tt(y_sb[:, t, :], y_sb[:, t, :], sg_sb[:, t, :], ALU.mult).then_inc(s("branch_normed"), 1)
        for t in range(NT):
            o3 = o_sb[:, t, :].rearrange("p (h n) -> p h n", h=DH)
            tt(o3, o3, rq[:, 16 + t * DH:16 + (t + 1) * DH].unsqueeze(2).to_broadcast([P, DH, P]), ALU.mult)\
                .then_inc(s("branch_normed"), 1)
        for n in range(32):
            if n >= 4:
                dve.wait_ge(s("row_mm"), n - 3)
            k = n % 4
            ts(row_diag[:, k, :], ident, colv[:, n // 8, n % 8:n % 8 + 1], None, ALU.mult).then_inc(s("diag8"), 1)
        dve.wait_ge(s("branch_normed"), 2 * NT)
        dve.wait_ge(s("gate_split"), 8)
        for n in range(2 * NT):
            t, dst, gain = n % NT, (zT if n < NT else onT), (RET_GN if n < NT else DIFF_GN)
            dve.wait_ge(s("branch_turned"), n + 1)
            bank = 4 + 2 * (n % 2)
            tt(dst[:, :, t * P:(t + 1) * P], ps[:, bank:bank + 2, :].rearrange("p b (k n) -> p (b k) n", n=P),
               vT[:, gain:gain + 8].unsqueeze(2).to_broadcast([P, KT, P]), ALU.mult).then_inc(s("branch_copied"), 1)
        dve.sem_inc(s("br_free"), 8)
        dve.wait_ge(s("g_free"), 32 + 4)
        with dve.Fori(0, 2) as n:
            for b in range(2):
                for t in range(NT):
                    dve.wait_ge(s("br_proj"), 8 * n + 4 * b + t + 1)
                    g = gate[:, bass.ds(n + 2 * b, 1), t, :].rearrange("p o c -> p (o c)")
                    tt(g, ps[:, 4 * b + t, :], g, ALU.mult).then_inc(s("br_free"), 1)
                    if b == 1:
                        g0 = gate[:, bass.ds(n, 1), t, :].rearrange("p o c -> p (o c)")
                        dve.wait_ge(s("br_free"), 8 * n + 4 * b + t + 9)
                        tt(m_sb[:, t, bass.ds(n * 512, 512)], g0, g, ALU.add).then_inc(s("m_ready"), 1)
        dve.wait_ge(s("row_copied"), 8)
        dve.wait_ge(s("ld_x2"), 16)

        def residual(t):
            dve.wait_ge(s("mix_rms"), t + 1)
            dve.reciprocal(rstd[:, t:t + 1], rms[:, t:t + 1])
            dve.drain()
            stt(f_sb[:, t, :], f_sb[:, t, :], rstd[:, t:t + 1], row_ga, ALU.mult, ALU.mult)
            dve.drain()
            tt(x1[:, t, :], x1[:, t, :], f_sb[:, t, :], ALU.add).then_inc(s("x1_ready"), 1)
            dve.wait_ge(s("x1_rms"), t + 1)
            dve.reciprocal(rstd[:, 4 + t:5 + t], rms[:, 4 + t:5 + t])
            dve.drain()
            stt(f_sb[:, t, :], x1[:, t, :], rstd[:, 4 + t:5 + t], row_af, ALU.mult, ALU.mult)
            dve.drain()
            tt(f_sb[:, t, :], f_sb[:, t, :], row_bf, ALU.add).then_inc(s("f_ready"), 1)

        def topk(h, t, first=False):
            m = NT * h + t
            dve.drain()
            if first:
                dve.wait_ge(s("scored"), t + 1)
            else:
                if t == 0:
                    dve.wait_ge(s("scored"), h + NT)
                elif t == 2:
                    dve.wait_ge(s("scored"), NT)
                dve.wait_ge(s("v_used"), TOPK * (m - 3) + V_CREDIT)
            stand(dve, "dve")
            sc = [ps[:, 6 + a, t * P:(t + 1) * P] for a in range(2)]
            for a in range(2):
                dve.max(top_v[:, a, 0:8], sc[a])
            dve.drain()
            for a in range(2):
                dve.max_index(top_i[:, a, 0:8], top_v[:, a, 0:8], sc[a])
                dve.match_replace(left[:, a, :], top_v[:, a, 0:8], sc[a], NEG)
            dve.drain()
            for a in range(2):
                dve.max(top_v[:, a, 8:16], left[:, a, :])
            dve.drain()
            for a in range(2):
                dve.max_index(top_i[:, a, 8:16], top_v[:, a, 8:16], left[:, a, :])
            tt(cand.rearrange("p (i j) -> p i j", i=TOPK), top_v[:, 0, :].unsqueeze(2).to_broadcast([P, TOPK, TOPK]),
               top_v[:, 1, :].unsqueeze(1).to_broadcast([P, TOPK, TOPK]), ALU.add)
            dve.drain()
            dve.sem_inc(s("topk_done"), 1)
            cp(top_f, top_i)
            dve.max(fin_v[:, 0:8], cand)
            dve.drain()
            dve.max_index(pos[:, 0:8], fin_v[:, 0:8], cand)
            dve.match_replace(cand2, fin_v[:, 0:8], cand, NEG)
            dve.drain()
            dve.max(fin_v[:, 8:16], cand2)
            dve.drain()
            dve.max_index(pos[:, 8:16], fin_v[:, 8:16], cand2)
            ts(logit[:, t, :], fin_v, fin_v[:, 0:1], None, ALU.subtract)
            dve.drain()
            ts(ab_i[:, 0, :], pos, 4, None, ALU.logical_shift_right)
            ts(ab_i[:, 1, :], pos, 15, None, ALU.bitwise_and)
            dve.drain()
            cp(ab_f, ab_i.rearrange("p a n -> p (a n)"))
            dve.drain()
            hot3 = hot.rearrange("p (m j) -> p m j", j=TOPK)
            hot4 = hot.rearrange("p (a m j) -> p a m j", a=2, j=TOPK)
            tt(hot3, ab_f.unsqueeze(2).to_broadcast([P, 32, TOPK]), iota16.unsqueeze(1).to_broadcast([P, 32, TOPK]), ALU.is_equal)
            dve.drain()
            tt(hot4, hot4, top_f.unsqueeze(2).to_broadcast([P, 2, TOPK, TOPK]), ALU.mult)
            dve.drain()
            dve.tensor_reduce(ij.rearrange("p a n -> p (a n)"), hot3, AX.X, ALU.add)
            dve.drain()
            stt(idxs[:, t, :], ij[:, 0, :], float(PK), ij[:, 1, :], ALU.mult, ALU.add).then_inc(s("idx_ready"), 1)

        def dot_products(h, t, half):
            n, b = NT * h + t, t % 2
            dve.drain()
            for e in range(half * USLOTS, (half + 1) * USLOTS):
                dve.wait_ge(s(f"u_in_{e % USLOTS}"), 32 * n + 16 * (e // USLOTS) + 16)
                dve.tensor_tensor_reduce(uslot[:, e % USLOTS, :], uslot[:, e % USLOTS, :], f_sb[:, t, :], 1.0, 0.0,
                                         ALU.mult, ALU.add, dots[:, b, e:e + 1]).then_inc(s("u_used"), 1)

        def unit(h, t, ahead=True, halves=(0, 1)):
            n, b = NT * h + t, t % 2
            for half in halves:
                dot_products(h, t, half)
            if ahead:
                topk(h + (t + 2) // NT, (t + 2) % NT)
            dve.wait_ge(s("v_used"), TOPK * (n - 1) + V_CREDIT)
            accumulate(t + 2)
            dve.wait_ge(s("gelu_done"), n + 1)
            dve.reciprocal(sinv[:, b:b + 1], ssum[:, b:b + 1])
            dve.drain()
            stt(wgt[:, b, :], gel[:, b, :], sinv[:, b:b + 1], soft[:, b, :], ALU.mult, ALU.mult).then_inc(s("w_ready"), 1)

        def accumulate(t):
            a3 = acc[:, t % NT, :].rearrange("p (b n) -> p b n", b=2)
            return tt(a3, a3, ps[:, 2 * (t % 2):2 * (t % 2) + 2, :], ALU.add).then_inc(s("acc_added"), 1)

        dve.drain()
        dve.sem_inc(s("u_used"), USLOTS)
        residual(0)
        residual(1)
        topk(0, 0, first=True)
        residual(2)
        topk(0, 1, first=True)
        dot_products(0, 0, 0)
        residual(3)
        dot_products(0, 0, 1)
        dve.memset(acc, 0.0)
        dve.wait_ge(s("q_copied"), 2 * NT)
        dve.memset(ps[:, 0:4, :], 0.0)
        for t in range(NT):
            unit(0, t, halves=(0, 1) if t else ())
        with dve.Fori(1, PH - 1) as h:
            for t in range(NT):
                unit(h, t)

        def finish(t):
            dve.wait_ge(s("y_rms"), t + 1)
            dve.reciprocal(rstd[:, t:t + 1], rms[:, t:t + 1])
            dve.drain()
            stt(acc[:, t, :], acc[:, t, :], rstd[:, t:t + 1], row_gf, ALU.mult, ALU.mult)
            dve.drain()
            tt(acc[:, t, :], acc[:, t, :], x1[:, t, :], ALU.add).then_inc(s("y_ready"), 1)

        for t in range(NT):
            unit(PH - 1, t, ahead=t < 2)
        finish(0)
        finish(1)
        for t in range(2):
            dve.wait_ge(s("v_used"), TOPK * (NT * PH - 1 + t) + V_CREDIT)
            accumulate(t + 2)
            finish(t + 2)

    @block.gpsimd
    def _(pool):
        def rows_of(table, dst, n, t, half, kind, need):
            for k in range(USLOTS):
                e = half * USLOTS + k
                pool.wait_ge(s(kind + "_used"), TOPK * n + e + 1 + need)
                stand(pool, "pool")
                pool.indirect_dma_start(out=dst[:, k, :], out_offset=None, in_=table,
                                        in_offset=bass.IndirectOffsetOnAxis(ap=idxs[:, t, e:e + 1], axis=0))\
                    .then_inc(s(f"{kind}_in_{k}"), 16)

        def u_rows(n, t, half):
            if half == 0:
                pool.wait_ge(s("idx_ready"), n + 1)
                stand(pool, "pool")
            rows_of(peer_u[:, :], uslot, n, t, half, "u", 0)

        def v_rows(n, t, half):
            rows_of(peer_v[:, :], vslot, n, t, half, "v", V_CREDIT - VSLOTS)

        def split(raw, hi, lo, name):
            stand(pool, "pool")
            for h, r in zip(hi, raw):
                pool.tensor_copy(h, r)
            pool.drain()
            for n, (h, r) in enumerate(zip(hi, raw)):
                last = pool.tensor_tensor(lo[n], r, h.bitcast(F32), ALU.subtract)
            last.then_inc(s(name), 1)

        def in_halves(ap):
            return [ap[:, 0:KT // 2, :], ap[:, KT // 2:KT, :]]

        with pool.Fori(0, RH) as h:
            for j, (raw, lo, hi) in enumerate(slots):
                pool.wait_ge(s(f"ret_w_{j}"), (32 if j == 0 else 16) * (h + 1))
                split([raw], [hi], [lo], "ret_split")
        with pool.Fori(0, DH // 2) as i:
            for b in range(2):
                pool.wait_ge(s(f"diff_w_{b}"), 48 * (i + 1))
                split(in_halves(d_raw[b]), d_hi[b], in_halves(d_lo[b]), "diff_split")
        pool.wait_ge(s("gate_w_0"), 16)
        split([gate_raw[0]], [slots[0][2]], [slots[0][1]], "gate_split")
        for n in range(1, 8):
            pool.wait_ge(s("gate_hi"), n)
            pool.tensor_tensor(slots[n % 2][1], gate_raw[n % 2], slots[n % 2][2].bitcast(F32), ALU.subtract)\
                .then_inc(s("gate_split"), 1)
        u_rows(0, 0, 0)
        v_rows(0, 0, 0)
        u_rows(0, 0, 1)
        u_rows(1, 1, 0)
        v_rows(0, 0, 1)
        u_rows(1, 1, 1)
        with pool.Fori(0, PH - 1) as h:
            for t in range(1, NT + 1):
                for half in range(2):
                    u_rows(NT * h + t + 1, (t + 1) % NT, half)
                    v_rows(NT * h + t, t % NT, half)
        for t in range(1, NT):
            n = NT * (PH - 1) + t
            for half in range(2):
                if t + 1 < NT:
                    u_rows(n + 1, t + 1, half)
                v_rows(n, t, half)

    es.close()


def kernel(**inputs):
    import concourse.bacc as bacc
    from concourse.bass_utils import run_bass_kernel_spmd

    nc = bacc.Bacc("TRN2", target_bir_lowering=False, num_devices=1)
    a = {k: np.asarray(v) for k, v in inputs.items()}
    small, dist, rope = shape_constants()
    blocks = [a[k][0].reshape(-1, P) for k in ("b_mod", "pre_mix_g", "post_mix_g", "pre_ffn_g", "post_ffn_g",
                                               "ret_gn_g", "diff_gn_g")]
    given = {
        "x": a["x"][0], "ctx": a["ctx"][0], "c_pair": np.stack([a["c"][0], a["c_ctx"]], axis=-1),
        "w_mod": a["w_mod"][0], "rows": np.concatenate(blocks, axis=0), "w_in": a["w_in"][0],
        "decays": np.concatenate([a["ret_decay_fwd"][0], a["ret_decay_bwd"][0]]),
        "lam": a["diff_lambda"][0].reshape(-1), "w_br_ret": a["w_br_ret"][0], "w_br_diff": a["w_br_diff"][0],
        "w_out": a["w_out"][0], "w_q": a["peer_w_q"][0], "keys": a["peer_sub_keys"][0],
        "peer_u": a["peer_u"][0], "peer_v": a["peer_v"][0], "small": small, "dist": dist, "rope": rope,
    }
    arrays, args = {}, {}
    for name, value in given.items():
        arrays["in_" + name] = np.ascontiguousarray(value)
        args[name] = nc.dram_tensor("in_" + name, value.shape, mybir.dt.from_np(value.dtype), kind="ExternalInput").ap()
    out = nc.dram_tensor("out_y", (T, D), F32, kind="ExternalOutput").ap()
    build(nc, out=out, **args)
    result = run_bass_kernel_spmd(nc, [arrays], core_ids=[0])
    return result.results[0]["out_y"].reshape(1, T, D)
```

```python
import math
from contextlib import ExitStack

import numpy as np

import concourse.bass as bass
from concourse import mybir

F32 = mybir.dt.float32
F32R = mybir.dt.float32r
U32 = mybir.dt.uint32
ACT = mybir.ActivationFunctionType
ALU = mybir.AluOpType
AX = mybir.AxisListType

P = 128
D = 1024
KT = D // P
T = 512
TC = 256
TA = T + TC
NT = T // P
NTA = TA // P
GRID_W = 64
EPS = 1e-6
LAM_INIT = 0.8 - 0.6 * math.exp(0.0)

RH, RDK, RDV = 4, 128, 256
DH, DD = 8, 64
RQ0, RK0 = 0, RH * RDK
RV0 = RK0 + RH * RDK
RG0 = RV0 + RH * RDV
DQ0 = RG0 + RH * RDV
DK0 = DQ0 + DH * 2 * DD
DV0 = DK0 + DH * 2 * DD
GR0 = DV0 + DH * 2 * DD

PH, PK, TOPK = 8, 128, 16
PDK = 256
USLOTS = VSLOTS = 8
NDIAG = 4
V_CREDIT = 32

LAG_W = (NT - 1) * P
M1W = 2 * NT * P - P
M2W = T + TC - P
G1 = 256
ROPE_W = 384
NEG = -3.0e38

B_MOD, PRE_MIX, POST_MIX, PRE_FFN, POST_FFN, RET_GN, DIFF_GN, NROWS = 0, 48, 56, 64, 72, 80, 88, 96


RET_BANK = (0, 1, 2, 4, 0, 1)

FILL = ((("p", 0), ("p", 1), ("t", 0)), (("p", 2), ("t", 1)),
        (("t", 2), ("m", 0), ("p", 3), ("p", 4), ("t", 3)), (("t", 4), ("p", 5), ("m", 1)))


def shape_constants():
    p = np.arange(P, dtype=np.float32)[:, None]
    d1 = np.arange(M1W, dtype=np.float32)[None, :] - LAG_W - p
    d2 = np.arange(M2W, dtype=np.float32)[None, :] - (TC - P) - p
    dist = np.concatenate([np.maximum(d1, 0), np.maximum(-d1, 0), d2 + TC, T - d2], axis=1)
    small = np.concatenate([np.eye(P, dtype=np.float32), np.tile(np.arange(16, dtype=np.float32), (P, 1))], axis=1)
    tok = np.arange(T)
    pos = np.stack([tok // GRID_W, tok % GRID_W], axis=1).astype(np.float32)

    def table(half):
        inv = np.power(np.float32(10000.0), -(np.arange(half, dtype=np.float32) / np.float32(half))).astype(np.float32)
        ang = (pos[:, :, None] * inv).astype(np.float32)
        cos, sin = np.cos(ang), np.sin(ang)
        both = np.stack([cos, cos], axis=2).reshape(T, 4 * half)
        return [both, (-sin).reshape(T, 2 * half), sin.reshape(T, 2 * half)]

    rope = np.concatenate(table(RDK // 4) + table(DD // 4), axis=1)
    return small.astype(np.float32), dist.astype(np.float32), rope.astype(np.float32)


def build(nc, x, ctx, c_pair, w_mod, rows, w_in, decays, lam, w_br_ret, w_br_diff, w_out,
          w_q, keys, peer_u, peer_v, small, dist, rope, out, debug=None):
    es = ExitStack()

    place = {}

    def sb(name, width, dt=F32):
        t = es.enter_context(nc.sbuf_tensor(name, [P, width], dt))
        place[name] = nc.sbuf_base - 4 * width
        return t

    def half_of(name, region, first, width):
        return nc.alloc_sbuf_tensor_at(name, [P, width], F32R, offset=place[region] + 4 * first)

    ps = es.enter_context(nc.psum_tensor("ps", [P, 8, 512], F32))
    wring = sb("wring", 14336)
    region_y = sb("region_ab", 2 * NT * D)
    region_o = sb("region_o", NT * D)
    region_z = sb("region_z", NT * D)
    region_u = sb("region_u", KT * TA)
    work = sb("work", 8 * D)
    tables = sb("tables", 2 * M1W + 3 * M2W + M1W)
    rope_t = sb("rope_t", NT * ROPE_W)
    small_t = sb("small_t", P + 16)
    vT = sb("vT", NROWS)
    stat = sb("stat", 672)
    ones = sb("ones", P)

    def ks(ap, k=KT):
        return ap.rearrange("p (k n) -> p k n", k=k)

    UW = KT * TA
    u_raw = ks(wring[:, 0:UW])
    u_lo, u_hi = ks(half_of("u_lo", "wring", 0, UW)[:, :]), ks(half_of("u_hi", "region_u", 0, UW)[:, :])
    GW = KT * G1
    slots = []
    for n, (region, name, first) in enumerate(((wring, "wring", UW), (wring, "wring", UW + 2 * GW), (region_o, "region_o", 0))):
        slots.append((ks(region[:, first:first + GW]), ks(half_of(f"w_lo_{n}", name, first, GW)[:, :]),
                      ks(half_of(f"w_hi_{n}", name, first + GW, GW)[:, :])))
    gate1_hi = ks(half_of("gate1_hi", "tables", 2 * D, GW)[:, :])
    gate_raw = [ks(region_z[:, b * GW:(b + 1) * GW]) for b in range(2)]
    branch_raw = [ks(region_y[:, b * GW:(b + 1) * GW]) for b in range(2)]
    TW = KT * T
    branch_hi = [ks(half_of("z_hi", "region_u", 0, TW)[:, :]), ks(half_of("on_hi", "wring", 0, TW)[:, :])]
    branch_lo = [ks(half_of("z_lo", "region_z", 0, TW)[:, :]), ks(half_of("on_lo", "region_ab", TW, TW)[:, :])]
    DW, DHALF = KT * 3 * P, KT // 2 * 3 * P
    d_raw = [ks(wring[:, UW:UW + DW]), ks(tables[:, 0:DW])]
    d_lo = [ks(half_of("d_lo_0", "wring", UW, DW)[:, :]), ks(half_of("d_lo_1", "tables", 0, DW)[:, :])]
    d_hi_0 = half_of("d_hi_0", "wring", UW + DW, DW)
    d_hi = [[ks(d_hi_0[:, j * DHALF:(j + 1) * DHALF], KT // 2) for j in range(2)],
            [ks(half_of("d_hi_1a", "tables", DW, DHALF)[:, :], KT // 2),
             ks(half_of("d_hi_1b", "region_z", 0, DHALF)[:, :], KT // 2)]]
    mod_w = ks(region_z[:, DHALF:DHALF + GW])
    mod_row = region_z[0:2, DHALF + GW:DHALF + GW + 512]
    WC = [r[:, 0:KT * 512].rearrange("p (k n) -> p k n", k=KT)
          for r in (wring[:, UW:UW + KT * 512], wring[:, UW + KT * 512:], region_z, region_u)]
    ident, iota16 = small_t[:, 0:P], small_t[:, P:P + 16]
    mT = fT = region_u[:, 0:KT * T].rearrange("p (k t) -> p k t", k=KT)
    y_sb = region_y[:, 0:NT * D].rearrange("p (t n) -> p t n", t=NT)
    sg_sb = region_y[:, NT * D:].rearrange("p (t n) -> p t n", t=NT)
    onT = region_y[:, NT * D:].rearrange("p (k t) -> p k t", k=KT)
    x_in = region_y[:, 0:NTA * D].rearrange("p (t n) -> p t n", t=NTA)
    o_sb = region_o[:, :].rearrange("p (t n) -> p t n", t=NT)
    x1 = o_sb
    zT = region_z[:, :].rearrange("p (k t) -> p k t", k=KT)
    f_sb = region_z[:, :].rearrange("p (t n) -> p t n", t=NT)
    gate = work[:, :].rearrange("p (n t c) -> p n t c", n=4, t=NT)
    uslot = work[:, :].rearrange("p (s n) -> p s n", s=USLOTS)
    vslot = region_y[:, :].rearrange("p (s n) -> p s n", s=VSLOTS)
    d_pos, d_neg = tables[:, 0:M1W], tables[:, M1W:2 * M1W]
    c_fwd, c_bwd = tables[:, 2 * M1W:2 * M1W + M2W], tables[:, 2 * M1W + M2W:2 * M1W + 2 * M2W]
    mask1 = tables[:, 2 * M1W + 2 * M2W:3 * M1W + 2 * M2W]
    mask2 = tables[:, 3 * M1W + 2 * M2W:3 * M1W + 3 * M2W]
    row_gf, row_ga, row_af, row_bf = (tables[:, i * D:(i + 1) * D] for i in range(4))
    ropes = rope_t[:, :].rearrange("p (t n) -> p t n", t=NT)

    at = [0]

    def piece(region, n, dt=None):
        a = region[:, at[0]:at[0] + n]
        at[0] += n
        return a if dt is None else a.bitcast(dt)

    at[0] = 0
    qT, kT = piece(work, T), piece(work, TA)
    v_sb = piece(work, NTA * RDV).rearrange("p (t n) -> p t n", t=NTA)
    rot = piece(work, 512).rearrange("p (b n) -> p b n", b=2)
    t1 = piece(work, 512).rearrange("p (b n) -> p b n", b=2)
    t2 = piece(work, 512).rearrange("p (b n) -> p b n", b=2)
    shared = at[0]
    aT = piece(work, NTA * T).rearrange("p (j n) -> p j n", j=NTA)
    eg = piece(work, 2 * RDV).rearrange("p (b n) -> p b n", b=2)
    at[0] = shared
    prob = piece(work, 4 * TA).rearrange("p (b a n) -> p b a n", b=2, a=2)
    dT = piece(work, TA)
    assert at[0] <= 8 * D
    at[0] = 0
    second = wring[:, UW + 2 * DW:]
    qTd = [qT, piece(second, T)]
    kTd = [kT, piece(second, TA)]
    v_d = [v_sb[:, :, 0:P], piece(second, NTA * P).rearrange("p (t n) -> p t n", t=NTA)]
    mod_row1 = work[0:2, 2048:4096]
    at[0] = 0
    cin = piece(stat, 2 * KT)
    csig = piece(stat, 2 * KT)
    csil = piece(stat, 2 * KT).rearrange("p (k j) -> p k j", j=2)
    eps_t = piece(stat, 1)
    ss, rms, rstd = piece(stat, 8), piece(stat, 8), piece(stat, 8)
    modv = piece(stat, 32).rearrange("p (k j) -> p k j", j=2)
    scaleA = piece(stat, 2 * KT).rearrange("p (k j) -> p k j", j=2)
    dec, dec_e, dec_y, dec_l, dec_r = (piece(stat, 2 * RH) for _ in range(5))
    lsum, lexp, nlam = piece(stat, 2), piece(stat, 2), piece(stat, 1)
    bn6 = piece(stat, RH * NT * 6)
    mv = piece(stat, RH * NT * 2)
    rmx, nbias, rsum, rinv, cfac = (piece(stat, 4) for _ in range(5))
    colv = piece(stat, 4 * KT).rearrange("p (v k) -> p v k", v=4)
    ssq, rmsq, rq = (piece(stat, 2 * NT * DH) for _ in range(3))
    assert at[0] <= 672, at[0]
    rowsT = work[:, 0:P]
    lamb = work[:, P:P + 256]
    lamp = work[:, P + 256:P + 384]
    row_diag = tables[:, 4 * D:4 * D + 512].rearrange("p (b n) -> p b n", b=4)
    square_u = region_y[:, NTA * D:].rearrange("p (b n) -> p b n", b=2)
    beside = [wring[:, 0:UW // 2], wring[:, UW // 2:UW]]
    peer_t = beside[0][:, 0:2560]
    at[0] = 0
    top_v = piece(peer_t, 32).rearrange("p (a n) -> p a n", a=2)
    top_i = piece(peer_t, 32, U32).rearrange("p (a n) -> p a n", a=2)
    top_f = piece(peer_t, 32).rearrange("p (a n) -> p a n", a=2)
    left = piece(peer_t, 256).rearrange("p (a n) -> p a n", a=2)
    cand = piece(peer_t, 256)
    cand2 = piece(peer_t, 256)
    fin_v = piece(peer_t, 16)
    pos = piece(peer_t, 16, U32)
    ab_i = piece(peer_t, 32, U32).rearrange("p (a n) -> p a n", a=2)
    ab_f = piece(peer_t, 32)
    hot = piece(peer_t, 512)
    ij = piece(peer_t, 32).rearrange("p (a n) -> p a n", a=2)
    idxs = piece(peer_t, NT * 16, U32).rearrange("p (t n) -> p t n", t=NT)
    logit = piece(peer_t, NT * 16).rearrange("p (t n) -> p t n", t=NT)
    dots = piece(peer_t, 32).rearrange("p (b n) -> p b n", b=2)
    gel = piece(peer_t, 32).rearrange("p (b n) -> p b n", b=2)
    soft = piece(peer_t, 32).rearrange("p (b n) -> p b n", b=2)
    ssum, sinv = piece(peer_t, 2), piece(peer_t, 2)
    wgt = piece(peer_t, 32).rearrange("p (b n) -> p b n", b=2)
    diag = piece(peer_t, NDIAG * P).rearrange("p (b n) -> p b n", b=NDIAG)
    assert at[0] <= 2560, at[0]
    keys_t = beside[0][:, 2560:2816].rearrange("p (a n) -> p a n", a=2)
    keysT = beside[0][:, 2816:3072].rearrange("p (a n) -> p a n", a=2)
    wq_t = beside[1][:, 0:KT * PDK].rearrange("p (k n) -> p k n", k=KT)
    pqT = beside[1][:, KT * PDK:KT * PDK + 1024].rearrange("p (a n) -> p a n", a=2)
    acc = wring[:, UW:UW + NT * D].rearrange("p (t n) -> p t n", t=NT)
    square_b = rope_t[:, 0:D]
    modps = ps[:, 5, 416:512].rearrange("p (c j) -> p c j", j=2)

    made = {}

    def s(name):
        if name not in made:
            made[name] = es.enter_context(nc.semaphore(name))
        return made[name]

    def stand(eng, name):
        eng.sem_inc(s("stood_" + name), 1)

    w_in_v = w_in.rearrange("(k p) n -> p k n", p=P)
    w_mod_v = w_mod.rearrange("(p k) n -> p k n", k=KT)
    br_v = [w.rearrange("(k p) n -> p k n", p=P) for w in (w_br_ret, w_br_diff, w_out)]
    w_q_v = w_q.rearrange("(k p) n -> p k n", p=P)
    x_v = x.rearrange("(t p) n -> p t n", p=P)
    ctx_v = ctx.rearrange("(t p) n -> p t n", p=P)
    out_v = out.rearrange("(t p) n -> p t n", p=P)
    C1 = 512

    block = es.enter_context(nc.Block())

    @block.sync
    def _(sp):
        def load(dst, src, name):
            return sp.dma_start(dst, src).then_inc(s(name), 16)

        load(cin, c_pair.rearrange("(p k) j -> p (k j)", k=KT), "ld_c")
        load(small_t[:, :], small, "ld_small")
        load(rowsT[0:NROWS, :], rows, "ld_rows")
        load(x_in[:, 0:NT, :], x_v, "ld_x")
        load(x_in[:, NT:NTA, :], ctx_v, "ld_ctx")
        load(dec, decays.partition_broadcast(P), "ld_dec")
        load(lamb, lam.partition_broadcast(P), "ld_lam")
        for n in range(4):
            load(WC[n], w_mod_v[:, :, n * C1:(n + 1) * C1], f"w_mod1_{n}")

        def ret_load(h, j):
            for dst, base, width in (((0, RQ0, RDK), (RDK, RK0, RDK)), ((0, RV0, RDV),), ((0, RG0, RDV),))[j]:
                load(slots[j][0][:, :, dst:dst + width], w_in_v[:, :, bass.ds(h * width + base, width)], f"ret_w_{j}")

        def diff_load(h, b):
            for j, base in enumerate((DQ0, DK0, DV0)):
                load(d_raw[b][:, :, j * P:(j + 1) * P], w_in_v[:, :, bass.ds(h * P + base, P)], f"diff_w_{b}")

        def mod_load(h, j):
            load(mod_w, w_mod_v[:, :, bass.ds(h * C1 + 4 * C1 + j * G1, G1)], "mod_w")

        sp.wait_ge(s("mod1_used"), 1)
        ret_load(0, 0)
        sp.wait_ge(s("mod1_used"), 2)
        ret_load(0, 1)
        load(rope_t[:, :].rearrange("p (t n) -> p t n", t=NT), rope.rearrange("(t p) n -> p t n", p=P), "ld_rope")
        load(tables[:, 0:2 * M1W + 2 * M2W], dist, "ld_dist")
        ret_load(0, 2)
        with sp.Fori(1, RH) as h:
            sp.wait_ge(s("r_proj"), 10 * h - 4)
            ret_load(h, 0)
            ret_load(h, 1)
            sp.wait_ge(s("r_proj"), 10 * h)
            ret_load(h, 2)
        sp.wait_ge(s("r_proj"), 10 * RH - 4)
        diff_load(0, 0)
        mod_load(0, 0)
        sp.wait_ge(s("r_masked"), 6 * RH)
        diff_load(1, 1)
        sp.wait_ge(s("mod_used"), 1)
        mod_load(0, 1)

        def diff_step(h, b, ahead=True):
            sp.wait_ge(s("mod_used"), 2 * h)
            mod_load(h, 0)
            if ahead:
                sp.wait_ge(s("d_proj"), 6 * h)
                diff_load(h + 1, b)
            sp.wait_ge(s("mod_used"), 2 * h + 1)
            mod_load(h, 1)

        with sp.Fori(0, DH // 2 - 1) as i:
            diff_step(2 * i + 1, 0)
            diff_step(2 * i + 2, 1)
        diff_step(DH - 1, 0, ahead=False)
        for n in range(8):
            if n == 0:
                sp.wait_ge(s("mod_used"), 2 * DH)
            elif n == 1:
                sp.wait_ge(s("d_aturned"), NT * (DH - 1) + 1)
            else:
                sp.wait_ge(s("gate_split"), n - 1)
            load(gate_raw[n % 2], w_in_v[:, :, n * G1 + GR0:(n + 1) * G1 + GR0], f"gate_w_{n % 2}")
        for n in range(8):
            if n < 2:
                sp.wait_ge(s("branch_turned"), NT)
            else:
                sp.wait_ge(s("br_split"), n - 1)
            load(branch_raw[n % 2], br_v[n % 2][:, :, n // 2 * G1:(n // 2 + 1) * G1], f"br_w_{n % 2}")
        load(x1, x_v, "ld_x2")
        for b in range(2):
            sp.wait_ge(s("br_proj"), 4 * (7 + b))
            load(WC[b], br_v[2][:, :, b * C1:(b + 1) * C1], f"out_w_{b}")
        load(wq_t, w_q_v[:, :, 0:PDK], "ld_wq")
        load(keys_t, keys[0].rearrange("a k d -> k a d"), "ld_wq")
        with sp.Fori(0, PH - 1) as h:
            sp.wait_ge(s("q_proj"), 2 * h + 2 * NT)
            load(wq_t, w_q_v[:, :, bass.ds(h * PDK + PDK, PDK)], "ld_wq")
            load(keys_t, keys[bass.ds(h + 1, 1)].rearrange("o a k d -> k (o a) d"), "ld_wq")
        for t in range(NT):
            sp.wait_ge(s("y_ready"), t + 1)
            load(out_v[:, t, :], acc[:, t, :], "stored")
        sp.wait_ge(s("stored"), NT * 16)

    @block.tensor
    def _(pe):
        def product(out_ap, lhs, rhs, n=KT):
            for k in range(n):
                last = pe.matmul(out_ap, lhs(k), rhs(k), start=(k == 0), stop=(k == n - 1))
            return last

        def product3(out_ap, t, hi, lo, src=(u_hi, u_lo)):
            tile = slice(t * P, (t + 1) * P)
            for k in range(KT):
                pe.matmul(out_ap, src[0][:, k, tile], hi(k), start=(k == 0), stop=False)
                pe.matmul(out_ap, src[0][:, k, tile], lo(k), start=False, stop=False)
                last = pe.matmul(out_ap, src[1][:, k, tile], hi(k), start=False, stop=(k == KT - 1))
            return last

        def slot_product(out_ap, t, n, src=(u_hi, u_lo)):
            return product3(out_ap, t, lambda k: slots[n][2][:, k, :], lambda k: slots[n][1][:, k, :], src)

        pe.wait_ge(s("ld_small"), 16)
        for t in range(NTA):
            pe.wait_ge(s("xn_ready"), t + 1)
            if t >= 2:
                pe.wait_ge(s("xt_act"), t - 1)
                pe.wait_ge(s("xt_dve"), t - 1)
            for k in range(KT):
                last = pe.transpose(ps[:, 2 * (t % 2) + k // 4, (k % 4) * P:(k % 4 + 1) * P],
                                    x_in[:, t, k * P:(k + 1) * P], ident)
            last.then_inc(s("x_turned"), 1)

        pe.wait_ge(s("csil_ready"), 1)
        def turn_mod1(n):
            pe.wait_ge(s("mod1_row"), n + 1)
            for j in range(4):
                last = pe.transpose(modps[:, n * 4 + j, :], mod_row1[:, (4 * n + j) * P:(4 * n + j + 1) * P], ident[0:2, 0:2])
            last.then_inc(s("mod1_turned"), 1)

        for n in range(4):
            pe.wait_ge(s(f"w_mod1_{n}"), 16)
            product(ps[0:2, 6 + n % 2, :], lambda k: csil[:, k, :], lambda k: WC[n][:, k, :]).then_inc(s("mod1_used"), 1)
            if n >= 1:
                turn_mod1(n - 1)
        turn_mod1(3)
        pe.wait_ge(s("ld_rows"), 16)
        pe.transpose(ps[:, 4, 0:NROWS], rowsT[0:NROWS, :], small_t[0:NROWS, 0:NROWS]).then_inc(s("rows_turned"), 1)
        with pe.Fori(0, RH // 2) as i:
            for b in range(2):
                h = 2 * i + b

                def turn(t):
                    pe.wait_ge(s("r_took"), 10 * h + t + 3)
                    pe.wait_ge(s("r_tfree"), 6 * h + t + 1)
                    if t == 1:
                        pe.wait_ge(s("r_yfree"), NT * h + 2)
                    if t < NT:
                        pe.transpose(ps[:, 4 - t % 2, 0:P], rot[:, t % 2, 0:P], ident)
                    pe.transpose(ps[:, 4 - t % 2, P:2 * P], rot[:, t % 2, P:2 * P], ident).then_inc(s("r_turned"), 1)

                for u in range(NTA + NT):
                    if u in (0, 2, 4):
                        pe.wait_ge(s("ut_split"), u // 2 + 1)
                    if u == 0:
                        pe.wait_ge(s("ret_split_0"), h + 1)
                        pe.wait_ge(s("ret_split_1"), h + 1)
                    elif u == NTA:
                        pe.wait_ge(s("ret_split_2"), h + 1)
                    if 2 <= u < NTA + 2:
                        pe.wait_ge(s("r_vcopied"), 6 * h + u - 1)
                    pe.wait_ge(s("r_took"), 10 * h + u + 1)
                    t = u % NTA
                    if u < NTA:
                        slot_product(ps[:, 6 + u % 2, 0:G1], t, 0)
                    slot_product(ps[:, 6 + u % 2, G1:2 * G1], t, 1 if u < NTA else 2).then_inc(s("r_proj"), 1)
                    if 1 <= u <= NTA:
                        turn(u - 1)
                pe.wait_ge(s("r_tfree"), 6 * h + NTA + 2)
                for j in range(NTA):
                    if j >= 4:
                        pe.wait_ge(s("r_masked"), 6 * h + j - 3)
                    mm = pe.matmul(ps[:, RET_BANK[j], :], kT[:, j * P:(j + 1) * P], qT[:, :], start=True, stop=True)
                    mm.then_inc(s("r_score"), 1)
                for t in range(NT):
                    if t == 0:
                        pe.wait_ge(s("r_masked"), 6 * h + NTA)
                    pe.wait_ge(s("r_yfree"), NT * h + t + 1)
                    product(ps[:, 3 + 2 * (t % 2), 0:RDV], lambda j: aT[:, j, t * P:(t + 1) * P],
                            lambda j: v_sb[:, j, :], NTA).then_inc(s("r_y"), 1)

        def project(h, b, t):
            pe.wait_ge(s("d_tfree"), 6 * h + t + 1)
            if t in (0, 3):
                pe.wait_ge(s("d_row"), 2 * h + 1 + (1 if t else 0))
            lo = 0 if t < NT else P
            product3(ps[:, 6 + t % 2, lo:3 * P], t, lambda k: d_hi[b][k // 4][:, k % 4, lo:3 * P],
                     lambda k: d_lo[b][:, k, lo:3 * P]).then_inc(s("d_proj"), 1)

        def turn_d(h, t):
            pe.wait_ge(s("d_took"), 6 * h + t + 1)
            pe.wait_ge(s("d_vcopied"), 6 * h + t + 1)
            for a in range(0 if t < NT else 1, 2):
                last = pe.transpose(ps[:, 6 + t % 2, a * P:(a + 1) * P], rot[:, t % 2, a * P:(a + 1) * P], ident)
            last.then_inc(s("d_turned"), 1)

        def mod(h, u):
            pe.wait_ge(s("mod_w"), 32 * h + 16 * u + 16)
            pe.wait_ge(s("d_tfree"), 6 * h + 3 * u + 4)
            product(ps[0:2, 7 - u, 0:G1], lambda k: csil[:, k, :], lambda k: mod_w[:, k, :])\
                .then_inc(s("mod_used"), 1)

        def turn_mod(h):
            pe.wait_ge(s("d_row"), 2 * h + 3)
            for j in range(4):
                pe.matmul(modps[:, bass.ds(h * 4 + 16 + j, 1), :].rearrange("p c j -> p (c j)"),
                          mod_row[:, j * P:(j + 1) * P], ident[0:2, 0:2], start=True, stop=True)

        def fill(h, b, step):
            for kind, u in FILL[step]:
                if kind == "p":
                    project(h, b, u)
                elif kind == "t":
                    turn_d(h, u)
                else:
                    mod(h, u)

        def scores(h, b, t):
            for a in range(2):
                pe.wait_ge(s("d_exp"), 2 * (NT * h + t) + a + 1)
                for lo, hi in ((0, 512), (512, TA)):
                    mm = pe.matmul(ps[:, 2 * a + lo // 512, 0:hi - lo], qTd[b][a * DD:(a + 1) * DD, t * P:(t + 1) * P],
                                   kTd[b][a * DD:(a + 1) * DD, lo:hi], start=True, stop=True)
                mm.then_inc(s("d_score"), 1)

        def first_scores(h, b):
            pe.wait_ge(s("d_tfree"), 6 * h + NTA + 2)
            scores(h, b, 0)

        def gate_first(t):
            pe.wait_ge(s("gate_split"), 1)
            slot_product(ps[:, 6 + t // 2, (t % 2) * G1:(t % 2 + 1) * G1], t, 0).then_inc(s("g_proj"), 1)

        def head(h, b, ahead):
            for t in range(NT):
                if ahead:
                    if t == 0:
                        pe.wait_ge(s("diff_split"), h + 2)
                    fill(h + 1, 1 - b, t)
                pe.wait_ge(s("d_ofree"), NT * h + t + 1)
                if not ahead and t >= 1:
                    gate_first(t - 1)
                if t == 0:
                    turn_mod(h)
                pe.wait_ge(s("d_comb"), NT * h + t + 1)
                for j in range(NTA):
                    mm = pe.transpose(ps[:, 4 + j // 4, (j % 4) * P:(j % 4 + 1) * P],
                                      prob[:, t % 2, 0, j * P:(j + 1) * P], ident)
                mm.then_inc(s("d_aturned"), 1)
                if t + 1 < NT:
                    scores(h, b, t + 1)
                elif ahead:
                    turn_d(h + 1, NTA - 1)
                pe.wait_ge(s("d_acopied"), NT * h + t + 1)
                product(ps[:, 5, 256:384], lambda j: dT[:, j * P:(j + 1) * P],
                        lambda j: v_d[b][:, j, :], NTA).then_inc(s("d_o"), 1)
            if ahead:
                first_scores(h + 1, 1 - b)
            else:
                gate_first(NT - 1)

        pe.wait_ge(s("r_took"), 10 * RH + 2)
        pe.wait_ge(s("diff_split"), 1)
        for step in range(NT):
            fill(0, 0, step)
        turn_d(0, NTA - 1)
        first_scores(0, 0)
        with pe.Fori(0, DH // 2 - 1) as i:
            head(2 * i, 0, True)
            head(2 * i + 1, 1, True)
        head(DH - 2, 0, True)
        head(DH - 1, 1, False)

        def gate_piece(n, b, between=None, hi=None):
            pe.wait_ge(s("gate_split"), n + 1)
            for t in range(NT):
                if hi is None:
                    pe.wait_ge(s("g_free"), 4 * n + t + 1)
                    slot_product(ps[:, t, 0:G1], t, b).then_inc(s("g_proj"), 1)
                else:
                    pe.wait_ge(s("g_free"), 4)
                    product3(ps[:, t, 0:G1], t, lambda k: hi[:, k, :], lambda k: slots[b][1][:, k, :])\
                        .then_inc(s("g_proj"), 1)
                if between is not None:
                    between(2 * t)
                    between(2 * t + 1)

        def row_half(n):
            if n >= 2:
                pe.wait_ge(s("row_copied"), n - 1)
            for k in range(4):
                pe.wait_ge(s("diag8"), 4 * n + k + 1)
                pe.matmul(ps[:, 6 + n % 2, k * P:(k + 1) * P], ones[:, :], row_diag[:, k, :],
                          start=True, stop=True).then_inc(s("row_mm"), 1)

        def turn_branch(n):
            t, src = n % NT, (y_sb if n < NT else o_sb)
            pe.wait_ge(s("branch_normed"), n + 1)
            if n >= 2:
                pe.wait_ge(s("branch_copied"), n - 1)
            elif n == 1:
                pe.wait_ge(s("row_copied"), 8)
            for k in range(KT):
                last = pe.transpose(ps[:, 4 + 2 * (n % 2) + k // 4, (k % 4) * P:(k % 4 + 1) * P],
                                    src[:, t, k * P:(k + 1) * P], ident)
            last.then_inc(s("branch_turned"), 1)

        gate_piece(1, 1, hi=gate1_hi)
        with pe.Fori(1, 3) as i:
            for b in range(2):
                gate_piece(2 * i + b, b)
        gate_piece(6, 0, row_half)
        gate_piece(7, 1, turn_branch)
        pe.wait_ge(s("branch_copied"), 2 * NT)
        pe.wait_ge(s("g_free"), 32 + 4)
        with pe.Fori(0, 2) as n:
            for c in range(2):
                for b in range(2):
                    pe.wait_ge(s("br_split"), 4 * n + 2 * c + b + 1)
                    for t in range(NT):
                        if c == 0:
                            pe.wait_ge(s("branch_split"), NT * b + t + 1)
                        pe.wait_ge(s("br_free"), 16 * n + 8 * c + 4 * b + t + 1)
                        slot_product(ps[:, 4 * b + t, 0:G1], t, b, (branch_hi[b], branch_lo[b])).then_inc(s("br_proj"), 1)
        for t in range(NT):
            pe.wait_ge(s("m_ready"), 3 * NT + t + 1)
            if t >= 2:
                pe.wait_ge(s("m_copied"), t - 1)
            for k in range(KT):
                last = pe.transpose(ps[:, 2 * (t % 2) + k // 4, (k % 4) * P:(k % 4 + 1) * P],
                                    gate[:, k // 4, t, (k % 4) * P:(k % 4 + 1) * P], ident)
            last.then_inc(s("m_turned"), 1)

        def keys_of(h, bank):
            pe.wait_ge(s("ld_wq"), 32 * h + 32)
            for a in range(2):
                last = pe.transpose(ps[:, bank, a * P:(a + 1) * P], keys_t[:, a, :], ident)
            last.then_inc(s("keys_turned"), 1)

        def queries_of_tile(t):
            pe.wait_ge(s("f_ready"), t + 1)
            for k in range(KT):
                last = pe.transpose(ps[:, k // 4, (k % 4) * P:(k % 4 + 1) * P], f_sb[:, t, k * P:(k + 1) * P], ident)
            last.then_inc(s("f_turned"), 1)
            pe.wait_ge(s("f_copied"), t + 1)
            if t == 0:
                pe.wait_ge(s("keys_copied"), 1)
            for a in range(2):
                product(ps[:, 2 + a, 0:P], lambda k: wq_t[:, k, a * P:(a + 1) * P],
                        lambda k: fT[:, k, t * P:(t + 1) * P]).then_inc(s("q_proj"), 1)
            if t in (1, 2):
                pe.wait_ge(s("topk_done"), t)
            for a in range(2):
                pe.wait_ge(s("q_copied"), 2 * t + a + 1)
                last = pe.matmul(ps[:, 6 + a, t * P:(t + 1) * P], pqT[:, a, t * P:(t + 1) * P], keysT[:, a, :],
                                 start=True, stop=True)
            last.then_inc(s("scored"), 1)

        pe.wait_ge(s("m_copied"), NT)
        pe.sem_inc(s("v_used"), V_CREDIT)
        for t in range(NT):
            pe.wait_ge(s("m_copied"), t + 1)
            for n in range(2):
                if t >= 1:
                    pe.wait_ge(s("mix_out"), 2 * (t - 1) + n + 1)
                else:
                    pe.wait_ge(s(f"out_w_{n}"), 16)
                product(ps[:, 4 + n, :], lambda k: mT[:, k, t * P:(t + 1) * P],
                        lambda k: WC[n][:, k, :]).then_inc(s("mix"), 1)
            if t == 1:
                keys_of(0, 6)
            if t >= 1:
                queries_of_tile(t - 1)
        queries_of_tile(NT - 1)

        def query_product(h, a):
            if a == 0:
                keys_of(h, 4)
            else:
                pe.wait_ge(s("q_copied"), 2 * (h + NT - 1) + 1)
            product(ps[:, 5, :], lambda k: wq_t[:, k, a * P:(a + 1) * P], lambda k: fT[:, k, :]).then_inc(s("q_proj"), 1)

        def key_scores(h):
            pe.wait_ge(s("topk_done"), NT * h)
            for a in range(2):
                pe.wait_ge(s("q_copied"), 2 * (h + NT - 1) + a + 1)
                if a == 0:
                    pe.wait_ge(s("keys_copied"), h + 1)
                for t in range(NT):
                    last = pe.matmul(ps[:, 6 + a, t * P:(t + 1) * P], pqT[:, a, t * P:(t + 1) * P], keysT[:, a, :],
                                     start=True, stop=True)
            last.then_inc(s("scored"), 1)

        def weighted_sum(h, t, ahead=False):
            n = NT * h + t
            pe.wait_ge(s("acc_added"), n + 1)
            for e in range(TOPK):
                pe.wait_ge(s(f"v_in_{e % VSLOTS}"), 32 * n + 16 * (e // VSLOTS) + 16)
                pe.wait_ge(s("diag_ready"), TOPK * n + e + 1)
                for half in range(2):
                    last = pe.matmul(ps[:, 2 * (t % 2) + half, :], diag[:, e % NDIAG, :],
                                     vslot[:, e % VSLOTS, half * 512:(half + 1) * 512],
                                     start=(e == 0), stop=(e == TOPK - 1))
                last.then_inc(s("v_used"), 1)
                if ahead and t == 0 and e in (5, 11):
                    query_product(h + 1, e // 6)
                elif ahead and t == 1 and e == 5:
                    key_scores(h + 1)

        pe.wait_ge(s("mix_out"), 2 * NT)
        with pe.Fori(0, PH - 1) as h:
            for t in range(NT):
                weighted_sum(h, t, ahead=True)
        for t in range(NT):
            weighted_sum(PH - 1, t)

    @block.scalar
    def _(act):
        def do(out_ap, in_ap, func=ACT.Copy, **kw):
            return act.activation(out_ap, in_ap, func, **kw)

        act.wait_ge(s("ld_c"), 16)
        do(csig, cin, ACT.Sigmoid).then_inc(s("csig"), 1)
        act.wait_ge(s("eps_set"), 1)
        for t in range(NTA):
            if t in (0, NT):
                act.wait_ge(s("ld_x" if t == 0 else "ld_ctx"), 16)
            if t >= 2:
                act.drain()
            do(square_u[:, t % 2, :], x_in[:, t, :], ACT.Square, accum_out=ss[:, t:t + 1])
            if t in (NT - 1, NTA - 1):
                first = 0 if t < NT else NT
                act.drain()
                do(rms[:, first:t + 1], ss[:, first:t + 1], ACT.Sqrt, scale=1.0 / D, bias=eps_t).then_inc(s("x_rms"), 1)
        for t in range(NTA):
            act.wait_ge(s("x_turned"), t + 1)
            do(u_raw[:, 0:4, t * P:(t + 1) * P], ps[:, 2 * (t % 2), :].rearrange("p (k n) -> p k n", k=4))\
                .then_inc(s("xt_act"), 1)
        act.wait_ge(s("ld_dec"), 16)
        do(dec_e, dec, ACT.Exp, scale=math.log(2.0)).then_inc(s("dec_e"), 1)
        act.wait_ge(s("lam_sums"), 1)
        do(lexp, lsum, ACT.Exp).then_inc(s("lam_exp"), 1)
        act.wait_ge(s("dec_y"), 1)
        do(dec_l, dec_y, ACT.Ln).then_inc(s("dec_ln"), 1)
        act.wait_ge(s("ret_w_1"), 16)
        do(slots[1][2], slots[1][0]).then_inc(s("ret_v_hi"), 1)
        act.wait_ge(s("mod_ready"), 1)
        for g in range(NTA // 2):
            j, two = (0 if 2 * g < NT else 1), slice(2 * g * P, 2 * (g + 1) * P)
            act.drain()
            for k in range(4):
                do(u_raw[:, k, two], u_raw[:, k, two], ACT.Identity, scale=scaleA[:, k, j:j + 1], bias=modv[:, k, j:j + 1])
            act.drain()
            do(u_hi[:, 0:4, two], u_raw[:, 0:4, two]).then_inc(s("ut_hi"), 1)

        act.sem_inc(s("r_tfree"), 2)
        act.sem_inc(s("r_yfree"), 2)
        act.wait_ge(s("ld_dist"), 16)
        act.wait_ge(s("dec_ready"), 1)
        with act.Fori(0, RH // 2) as i:
            for b in range(2):
                h = 2 * i + b
                act.wait_ge(s("r_dist"), h + 1)
                do(mask1, mask1, ACT.Exp).then_inc(s("r_mask"), 1)
                do(mask2, mask2, ACT.Exp).then_inc(s("r_mask"), 1)
                do(aT[:, 0:2, :].rearrange("p a n -> p (a n)")[:, 0:M2W],
                   aT[:, 0:2, :].rearrange("p a n -> p (a n)")[:, 0:M2W], ACT.Exp).then_inc(s("r_mask"), 1)

                def copy_t(t):
                    act.wait_ge(s("r_turned"), 6 * h + t + 1)
                    if t < NT:
                        do(qT[:, t * P:(t + 1) * P], ps[:, 4 - t % 2, 0:P], scale=RDK ** -0.5)
                    last = do(kT[:, t * P:(t + 1) * P], ps[:, 4 - t % 2, P:2 * P])
                    last.then_inc(s("r_tfree"), 1)

                for u in range(NTA + NT):
                    act.wait_ge(s("r_proj"), 10 * h + u + 1)
                    if u < NTA:
                        act.wait_ge(s("r_took"), 10 * h + u + 3)
                        do(v_sb[:, u, :], ps[:, 6 + u % 2, G1:2 * G1]).then_inc(s("r_vcopied"), 1)
                    else:
                        if u >= NTA + 2:
                            act.wait_ge(s("r_took"), 10 * h + u + 1)
                        do(eg[:, u % 2, :], ps[:, 6 + u % 2, G1:2 * G1], ACT.Exp, scale=-1.0).then_inc(s("r_eg"), 1)
                    if 1 <= u <= NTA:
                        copy_t(u - 1)
                for t in range(NT):
                    act.wait_ge(s("r_ystat"), NT * h + t + 1)
                    stand(act, "act")
                    do(y_sb[:, t, bass.ds(h * RDV, RDV)], ps[:, 3 + 2 * (t % 2), 0:RDV]).then_inc(s("r_yfree"), 1)

        act.sem_inc(s("d_tfree"), 2)
        act.sem_inc(s("d_exp"), 2)
        act.sem_inc(s("d_ofree"), 1)

        def copy_v(h, b, u):
            act.wait_ge(s("d_took"), 6 * h + u + 1)
            do(v_d[b][:, u, :], ps[:, 6 + u % 2, 2 * P:3 * P]).then_inc(s("d_vcopied"), 1)

        def copy_qk(h, b, t):
            act.wait_ge(s("d_turned"), 6 * h + t + 1)
            if t < NT:
                do(qTd[b][:, t * P:(t + 1) * P], ps[:, 6 + t % 2, 0:P])
            do(kTd[b][:, t * P:(t + 1) * P], ps[:, 6 + t % 2, P:2 * P]).then_inc(s("d_tfree"), 1)

        def fill(h, b, step):
            for kind, u in FILL[step]:
                if kind == "t":
                    copy_qk(h, b, u)
                elif kind == "p":
                    copy_v(h, b, u)

        def exps(h, t):
            for a in range(2):
                act.wait_ge(s("d_max"), 2 * (NT * h + t) + a + 1)
                table = ps[:, 2 * a:2 * a + 2, :].rearrange("p b n -> p (b n)")[:, 0:TA]
                do(prob[:, t % 2, a, :], table, ACT.Exp, scale=DD ** -0.5,
                   bias=nbias[:, 2 * (t % 2) + a:2 * (t % 2) + a + 1],
                   accum_out=rsum[:, 2 * (t % 2) + a:2 * (t % 2) + a + 1]).then_inc(s("d_exp"), 1)

        def head(h, b, ahead):
            exps(h, 0)
            for t in range(NT):
                if ahead:
                    fill(h + 1, 1 - b, t)
                act.wait_ge(s("d_aturned"), NT * h + t + 1)
                do(dT[:, :], ps[:, 4:6, :].rearrange("p b n -> p (b n)")[:, 0:TA]).then_inc(s("d_acopied"), 1)
                if t + 1 < NT:
                    exps(h, t + 1)
                elif ahead:
                    copy_qk(h + 1, 1 - b, NTA - 1)
                act.wait_ge(s("d_o"), NT * h + t + 1)
                stand(act, "act")
                do(o_sb[:, t, bass.ds(h * P, P)], ps[:, 5, 256:384], scale=rinv[:, 2 * (t % 2):2 * (t % 2) + 1])\
                    .then_inc(s("d_ofree"), 1)

        for step in range(NT):
            fill(0, 0, step)
        copy_qk(0, 0, NTA - 1)
        with act.Fori(0, DH // 2 - 1) as i:
            for b in range(2):
                head(2 * i + b, b, True)
        head(DH - 2, 0, True)
        head(DH - 1, 1, False)

        def gate_hi(n, b):
            act.wait_ge(s(f"gate_w_{b}"), 8 * (n - b) + 16)
            stand(act, "act")
            do(slots[b][2], gate_raw[b]).then_inc(s("gate_hi"), 1)

        act.sem_inc(s("g_free"), 4)
        act.wait_ge(s("q_sq"), 1)
        do(rmsq[:, 0:16], mv.rearrange("p (n j) -> p n j", j=2)[:, :, 1], ACT.Sqrt, bias=eps_t).then_inc(s("br_rms"), 1)
        do(rmsq[:, 16:48], ssq[:, 16:48], ACT.Sqrt, scale=1.0 / P, bias=eps_t).then_inc(s("br_rms"), 1)
        def sigmoids(n, i, b, between=None, first=False):
            for t in range(NT):
                act.wait_ge(s("g_proj"), NT if first else 4 * n + t + 1)
                stand(act, "act")
                bank = ps[:, 6 + t // 2, (t % 2) * G1:(t % 2 + 1) * G1] if first else ps[:, t, 0:G1]
                do(gate[:, bass.ds(i, 1), t, b * G1:(b + 1) * G1].rearrange("p o c -> p (o c)"), bank, ACT.Sigmoid)\
                    .then_inc(s("g_free"), 1)
                if between is not None:
                    between(2 * t)
                    between(2 * t + 1)

        def row_half(n):
            act.wait_ge(s("row_mm"), 4 * n + 4)
            dst = (row_gf, row_ga, row_af, row_bf)[n // 2]
            do(dst[:, (n % 2) * 512:(n % 2 + 1) * 512], ps[:, 6 + n % 2, :]).then_inc(s("row_copied"), 1)

        for b in range(2):
            sigmoids(b, 0, b, first=(b == 0))
            gate_hi(b + 2, b)
        with act.Fori(1, 3) as i:
            for b in range(2):
                sigmoids(2 * i + b, i, b)
                gate_hi(2 * i + b + 2, b)
        sigmoids(6, 3, 0, row_half)
        def branch_w_hi(n):
            b = n % 2
            act.wait_ge(s(f"br_w_{b}"), 8 * (n - b) + 16)
            if n < 2:
                act.wait_ge(s("g_proj"), 4 * (7 + b))
            else:
                act.wait_ge(s("br_proj"), 4 * (n - 1))
            do(slots[b][2], branch_raw[b]).then_inc(s("br_hi"), 1)

        sigmoids(7, 3, 1, lambda n: branch_w_hi(0) if n == 4 else None)
        for n in range(2 * NT):
            b, tile = n // NT, slice(n % NT * P, (n % NT + 1) * P)
            act.wait_ge(s("branch_copied"), n + 1)
            do(branch_hi[b][:, :, tile], (zT, onT)[b][:, :, tile]).then_inc(s("branch_hi"), 1)
            if n == 1:
                branch_w_hi(1)
        for n in range(2, 8):
            branch_w_hi(n)
        for t in range(NT):
            act.wait_ge(s("m_turned"), t + 1)
            do(mT[:, :, t * P:(t + 1) * P], ps[:, 2 * (t % 2):2 * (t % 2) + 2, :].rearrange("p b (k n) -> p (b k) n", n=P))\
                .then_inc(s("m_copied"), 1)

        def copy_tile(t):
            act.wait_ge(s("f_turned"), t + 1)
            do(fT[:, :, t * P:(t + 1) * P], ps[:, 0:2, :].rearrange("p b (k n) -> p (b k) n", n=P)).then_inc(s("f_copied"), 1)
            for a in range(2):
                act.wait_ge(s("q_proj"), 2 * t + a + 1)
                do(pqT[:, a, t * P:(t + 1) * P], ps[:, 2 + a, 0:P]).then_inc(s("q_copied"), 1)

        for t in range(NT):
            for n in range(2):
                act.wait_ge(s("mix"), 2 * t + n + 1)
                do(f_sb[:, t, n * 512:(n + 1) * 512], ps[:, 4 + n, :]).then_inc(s("mix_out"), 1)
            act.drain()
            do(square_b, f_sb[:, t, :], ACT.Square, accum_out=ss[:, t:t + 1])
            act.drain()
            do(rms[:, t:t + 1], ss[:, t:t + 1], ACT.Sqrt, scale=1.0 / D, bias=eps_t).then_inc(s("mix_rms"), 1)
            if t == 1:
                act.wait_ge(s("keys_turned"), 1)
                do(keysT, ps[:, 6, 0:256].rearrange("p (a n) -> p a n", a=2)).then_inc(s("keys_copied"), 1)
            if 1 <= t < NT - 1:
                copy_tile(t - 1)
                act.drain()
            act.wait_ge(s("x1_ready"), t + 1)
            do(square_b, x1[:, t, :], ACT.Square, accum_out=ss[:, 4 + t:5 + t])
            act.drain()
            do(rms[:, 4 + t:5 + t], ss[:, 4 + t:5 + t], ACT.Sqrt, scale=1.0 / D, bias=eps_t).then_inc(s("x1_rms"), 1)
        copy_tile(NT - 2)
        copy_tile(NT - 1)

        def copy_queries(h, a):
            if a == 0:
                act.wait_ge(s("keys_turned"), h + 1)
                do(keysT, ps[:, 4, 0:256].rearrange("p (a n) -> p a n", a=2)).then_inc(s("keys_copied"), 1)
            act.wait_ge(s("q_proj"), 2 * (h + NT - 1) + a + 1)
            do(pqT[:, a, :], ps[:, 5, :]).then_inc(s("q_copied"), 1)

        def square_sum(t):
            act.wait_ge(s("acc_added"), NT * PH - 1 + t)
            act.drain()
            do(square_b, acc[:, t, :], ACT.Square, accum_out=ss[:, t:t + 1])
            act.drain()
            do(rms[:, t:t + 1], ss[:, t:t + 1], ACT.Sqrt, scale=1.0 / D, bias=eps_t).then_inc(s("y_rms"), 1)

        def unit(h, t, last=False, ahead=False):
            n, b = NT * h + t, t % 2
            act.wait_ge(s("u_used"), TOPK * n + TOPK + USLOTS)
            do(soft[:, b, :], logit[:, t, :], ACT.Exp, accum_out=ssum[:, b:b + 1])
            do(gel[:, b, :], dots[:, b, :], ACT.Gelu)
            act.drain()
            act.sem_inc(s("gelu_done"), 1)
            act.wait_ge(s("w_ready"), n + 1)
            for e in range(TOPK):
                if ahead and e == 10:
                    copy_queries(h + 1, 0)
                if last and e == USLOTS:
                    square_sum(0)
                    square_sum(1)
                act.wait_ge(s("v_used"), TOPK * n + e + 1 - NDIAG + V_CREDIT)
                do(diag[:, e % NDIAG, :], ident, scale=wgt[:, b, e:e + 1]).then_inc(s("diag_ready"), 1)

        with act.Fori(0, PH - 1) as h:
            for t in range(NT):
                unit(h, t, ahead=(t == 0))
                if t == 0:
                    copy_queries(h + 1, 1)
        for t in range(NT):
            unit(PH - 1, t, last=(t == NT - 1))
        square_sum(2)
        square_sum(3)

    @block.vector
    def _(dve):
        tt, ts, stt, cp = dve.tensor_tensor, dve.tensor_scalar, dve.scalar_tensor_tensor, dve.tensor_copy

        dve.memset(eps_t, EPS).then_inc(s("eps_set"), 1)
        dve.memset(ones[:, :], 1.0)
        dve.wait_ge(s("csig"), 1)
        tt(csil, cin.rearrange("p (k j) -> p k j", j=2), csig.rearrange("p (k j) -> p k j", j=2), ALU.mult)\
            .then_inc(s("csil_ready"), 1)
        dve.wait_ge(s("ld_lam"), 16)
        lam4 = lamb.rearrange("p (a b n) -> p a b n", a=2, b=2)
        tt(lamp.rearrange("p (a n) -> p a n", a=2), lam4[:, :, 0, :], lam4[:, :, 1, :], ALU.mult)
        dve.drain()
        dve.tensor_reduce(lsum, lamp.rearrange("p (a n) -> p a n", a=2), AX.X, ALU.add).then_inc(s("lam_sums"), 1)
        for first, end in ((0, NT), (NT, NTA)):
            dve.wait_ge(s("x_rms"), 1 if first == 0 else 2)
            dve.reciprocal(rstd[:, first:end], rms[:, first:end])
            dve.drain()
            for t in range(first, end):
                ts(x_in[:, t, :], x_in[:, t, :], rstd[:, t:t + 1], None, ALU.mult).then_inc(s("xn_ready"), 1)
        for t in range(NTA):
            dve.wait_ge(s("x_turned"), t + 1)
            cp(u_raw[:, 4:KT, t * P:(t + 1) * P], ps[:, 2 * (t % 2) + 1, :].rearrange("p (k n) -> p k n", k=4))\
                .then_inc(s("xt_dve"), 1)
        dve.wait_ge(s("dec_e"), 1)
        ts(dec_y, dec_e, -1.0, 1.0, ALU.mult, ALU.add).then_inc(s("dec_y"), 1)
        dve.drain()
        ts(dec_r, dec_y, -1.0, 1.0, ALU.mult, ALU.add)
        dve.drain()
        ts(dec_r, dec_r, 1e-30, None, ALU.max)
        dve.drain()
        dve.reciprocal(dec_r, dec_r)
        dve.drain()
        tt(dec_r, dec_r, dec_e, ALU.mult)
        dve.drain()
        dve.wait_ge(s("dec_ln"), 1)
        tt(dec_l, dec_l, dec_r, ALU.mult).then_inc(s("dec_ready"), 1)
        dve.wait_ge(s("lam_exp"), 1)
        tt(nlam, lexp[:, 1:2], lexp[:, 0:1], ALU.subtract)
        dve.drain()
        ts(nlam, nlam, -LAM_INIT, None, ALU.add)
        for n in range(4):
            if n == 3:
                dve.wait_ge(s("ret_v_hi"), 1)
                tt(slots[1][1], slots[1][0], slots[1][2].bitcast(F32), ALU.subtract).then_inc(s("ret_split_1"), 1)
            dve.wait_ge(s("mod1_used"), n + 1)
            cp(mod_row1[:, n * C1:(n + 1) * C1], ps[0:2, 6 + n % 2, :]).then_inc(s("mod1_row"), 1)
        dve.wait_ge(s("rows_turned"), 1)
        cp(vT[:, :], ps[:, 4, 0:NROWS])
        dve.drain()
        dve.wait_ge(s("mod1_turned"), 4)
        tt(modv, modps[:, 0:16, :], vT[:, B_MOD:B_MOD + 16].unsqueeze(2).to_broadcast([P, 16, 2]), ALU.add)
        dve.drain()
        stt(scaleA, modv[:, 8:16, :], 1.0, vT[:, PRE_MIX:PRE_MIX + 8].unsqueeze(2).to_broadcast([P, 8, 2]),
            ALU.add, ALU.mult).then_inc(s("mod_ready"), 1)
        ts(vT[:, DIFF_GN:DIFF_GN + 8], vT[:, DIFF_GN:DIFF_GN + 8], 1.0 - LAM_INIT, None, ALU.mult)
        dve.drain()
        dve.sem_inc(s("r_took"), 2)
        for g in range(NTA // 2):
            j, two = (0 if 2 * g < NT else 1), slice(2 * g * P, 2 * (g + 1) * P)
            for k in range(4, KT):
                ts(u_raw[:, k, two], u_raw[:, k, two], scaleA[:, k, j:j + 1], modv[:, k, j:j + 1], ALU.mult, ALU.add)
            dve.drain()
            cp(u_hi[:, 4:KT, two], u_raw[:, 4:KT, two])
            dve.drain()
            dve.wait_ge(s("ut_hi"), g + 1)
            tt(u_lo[:, :, two], u_raw[:, :, two], u_hi[:, :, two].bitcast(F32), ALU.subtract).then_inc(s("ut_split"), 1)

        def rotate(t, src, groups, half, table):
            w = 4 * half
            cos = ropes[:, t, table:table + w].unsqueeze(1).to_broadcast([P, groups, w])
            g = src.rearrange("p (g n) -> p g n", g=groups)
            sin = [ropes[:, t, table + w + i * 2 * half:table + w + (i + 1) * 2 * half]
                   .rearrange("p (x n) -> p x n", x=2).unsqueeze(1).to_broadcast([P, groups, 2, half]) for i in range(2)]
            src5 = src.rearrange("p (g x f n) -> p g x f n", g=groups, x=2, f=2)
            dst5 = t2[:, t % 2, :].rearrange("p (g x f n) -> p g x f n", g=groups, x=2, f=2)
            tt(t1[:, t % 2, :].rearrange("p (g n) -> p g n", g=groups), g, cos, ALU.mult)
            tt(dst5[:, :, :, 0, :], src5[:, :, :, 1, :], sin[0], ALU.mult)
            tt(dst5[:, :, :, 1, :], src5[:, :, :, 0, :], sin[1], ALU.mult)
            dve.drain()
            return tt(rot[:, t % 2, :], t1[:, t % 2, :], t2[:, t % 2, :], ALU.add)

        dve.wait_ge(s("ld_rope"), 16)
        dve.wait_ge(s("ld_dist"), 16)
        with dve.Fori(0, RH // 2) as i:
            for b in range(2):
                h = 2 * i + b
                lf, lb = dec_l[:, bass.ds(h, 1)], dec_l[:, bass.ds(h + RH, 1)]
                back = aT[:, 0:2, :].rearrange("p a n -> p (a n)")[:, 0:M2W]
                dve.drain()
                ts(mask1, d_neg, lb, None, ALU.mult)
                ts(mask2, c_fwd, lf, None, ALU.mult)
                ts(back, c_bwd, lb, None, ALU.mult)
                dve.drain()
                stt(mask1, d_pos, lf, mask1, ALU.mult, ALU.add).then_inc(s("r_dist"), 1)
                for u in range(NTA + NT):
                    t = u % NTA
                    bank = ps[:, 6 + u % 2, :]
                    if u == NTA:
                        dve.wait_ge(s("r_mask"), 3 * h + 3)
                        tt(mask2, mask2, back, ALU.add)
                    if u < NTA:
                        dve.drain()
                        dve.wait_ge(s("r_proj"), 10 * h + u + 1)
                        if u < NT:
                            rotate(t, bank[:, 0:2 * RDK], 2, RDK // 4, 0).then_inc(s("r_took"), 1)
                        else:
                            cp(rot[:, t % 2, P:2 * P], bank[:, P:2 * P]).then_inc(s("r_took"), 1)
                    else:
                        dve.wait_ge(s("r_eg"), NT * h + t + 1)
                        e = eg[:, u % 2, :]
                        ts(e, e, 1.0, None, ALU.add)
                        dve.drain()
                        dve.reciprocal(e, e)
                        dve.drain()
                        tt(sg_sb[:, t, bass.ds(h * RDV, RDV)], bank[:, G1:2 * G1], e, ALU.mult).then_inc(s("r_took"), 1)
                dve.drain()
                for j in range(NTA):
                    dve.wait_ge(s("r_score"), 6 * h + j + 1)
                    m = mask1[:, (NT - 1 - j) * P:(NT - 1 - j) * P + T] if j < NT else \
                        mask2[:, (NTA - 1 - j) * P:(NTA - 1 - j) * P + T]
                    tt(aT[:, j, :], ps[:, RET_BANK[j], :], m, ALU.mult).then_inc(s("r_masked"), 1)
                for t in range(NT):
                    dve.wait_ge(s("r_y"), NT * h + t + 1)
                    stand(dve, "dve")
                    dve.bn_stats(bn6[:, bass.ds((h * NT + t) * 6, 6)], ps[:, 3 + 2 * (t % 2), 0:RDV]).then_inc(s("r_ystat"), 1)

        dve.sem_inc(s("d_row"), 1)

        def take(h, t):
            bank = ps[:, 6 + t % 2, :]
            dve.drain()
            dve.wait_ge(s("d_proj"), 6 * h + t + 1)
            if t < NT:
                rotate(t, bank[:, 0:2 * P], 4, DD // 4, 256).then_inc(s("d_took"), 1)
            else:
                cp(rot[:, t % 2, P:2 * P], bank[:, P:2 * P]).then_inc(s("d_took"), 1)

        def fill_d(h, step):
            for kind, u in FILL[step]:
                if kind == "p":
                    take(h, u)
                elif kind == "m":
                    dve.wait_ge(s("mod_used"), 2 * h + u + 1)
                    cp(mod_row[:, u * G1:(u + 1) * G1], ps[0:2, 7 - u, 0:G1]).then_inc(s("d_row"), 1)

        def head_d(h, ahead):
            for t in range(NT):
                for a in range(2):
                    q = 2 * (t % 2) + a
                    dve.wait_ge(s("d_score"), 2 * (NT * h + t) + a + 1)
                    dve.tensor_reduce(rmx[:, q:q + 1], ps[:, 2 * a:2 * a + 2, :].rearrange("p b n -> p (b n)")[:, 0:TA],
                                      AX.X, ALU.max)
                    dve.drain()
                    ts(nbias[:, q:q + 1], rmx[:, q:q + 1], -(DD ** -0.5), None, ALU.mult).then_inc(s("d_max"), 1)
                dve.wait_ge(s("d_exp"), 2 * (NT * h + t) + 4)
                q = 2 * (t % 2)
                dve.reciprocal(rinv[:, q:q + 2], rsum[:, q:q + 2])
                dve.drain()
                stt(cfac[:, 0:1], rsum[:, q:q + 1], rinv[:, q + 1:q + 2], nlam, ALU.mult, ALU.mult)
                dve.drain()
                stt(prob[:, t % 2, 0, :], prob[:, t % 2, 1, :], cfac[:, 0:1], prob[:, t % 2, 0, :], ALU.mult, ALU.add)\
                    .then_inc(s("d_comb"), 1)
                if ahead:
                    fill_d(h + 1, t)

        for step in range(NT):
            fill_d(0, step)
        with dve.Fori(0, DH // 2 - 1) as i:
            for b in range(2):
                head_d(2 * i + b, True)
        head_d(DH - 2, True)
        head_d(DH - 1, False)

        for n in range(RH * NT):
            dve.bn_aggr(mv[:, 2 * n:2 * n + 2], bn6[:, 6 * n:6 * n + 6])
        sqr = tables[:, 0:2 * D].rearrange("p (b n) -> p b n", b=2)
        dve.wait_ge(s("d_ofree"), NT * DH + 1)
        for t in range(NT):
            tt(sqr[:, t % 2, :], o_sb[:, t, :], o_sb[:, t, :], ALU.mult)
            dve.drain()
            dve.tensor_reduce(ssq[:, 16 + t * DH:16 + (t + 1) * DH], sqr[:, t % 2, :].rearrange("p (h n) -> p h n", n=P), AX.X, ALU.add)
        dve.drain()
        dve.sem_inc(s("q_sq"), 1)
        vbias = vT[:, B_MOD + 16:B_MOD + 48]
        mod2 = modps[:, 16:48, 0]
        for v, (col, gain) in enumerate(((24, POST_FFN), (0, POST_MIX), (16, PRE_FFN), (8, None))):
            tt(colv[:, v, :], mod2[:, col:col + 8], vbias[:, col:col + 8], ALU.add)
            dve.drain()
            if gain is not None:
                stt(colv[:, v, :], colv[:, v, :], 1.0 if v == 2 else 0.0, vT[:, gain:gain + 8], ALU.add, ALU.mult)
                dve.drain()
        dve.wait_ge(s("br_rms"), 2)
        dve.reciprocal(rq[:, 0:48], rmsq[:, 0:48])
        dve.drain()
        mv3 = mv.rearrange("p (h t j) -> p h t j", h=RH, t=NT)
        rq_r = rq[:, 0:16].rearrange("p (h t) -> p h t", h=RH)
        for t in range(NT):
            y3 = y_sb[:, t, :].rearrange("p (h n) -> p h n", h=RH)
            tt(y3, y3, mv3[:, :, t, 0:1].to_broadcast([P, RH, RDV]), ALU.subtract)
            dve.drain()
            tt(y3, y3, rq_r[:, :, t:t + 1].to_broadcast([P, RH, RDV]), ALU.mult)
            dve.drain()
            tt(y_sb[:, t, :], y_sb[:, t, :], sg_sb[:, t, :], ALU.mult).then_inc(s("branch_normed"), 1)
        for t in range(NT):
            o3 = o_sb[:, t, :].rearrange("p (h n) -> p h n", h=DH)
            tt(o3, o3, rq[:, 16 + t * DH:16 + (t + 1) * DH].unsqueeze(2).to_broadcast([P, DH, P]), ALU.mult)\
                .then_inc(s("branch_normed"), 1)
        for n in range(32):
            if n >= 4:
                dve.wait_ge(s("row_mm"), n - 3)
            k = n % 4
            ts(row_diag[:, k, :], ident, colv[:, n // 8, n % 8:n % 8 + 1], None, ALU.mult).then_inc(s("diag8"), 1)
        dve.sem_inc(s("br_free"), 8)
        dve.wait_ge(s("branch_normed"), 2 * NT)
        dve.wait_ge(s("gate_split"), 8)
        for n in range(2 * NT):
            t, dst, gain = n % NT, (zT if n < NT else onT), (RET_GN if n < NT else DIFF_GN)
            dve.wait_ge(s("branch_turned"), n + 1)
            bank = 4 + 2 * (n % 2)
            tt(dst[:, :, t * P:(t + 1) * P], ps[:, bank:bank + 2, :].rearrange("p b (k n) -> p (b k) n", n=P),
               vT[:, gain:gain + 8].unsqueeze(2).to_broadcast([P, KT, P]), ALU.mult).then_inc(s("branch_copied"), 1)
        for n in range(2 * NT):
            b, tile = n // NT, slice(n % NT * P, (n % NT + 1) * P)
            dve.wait_ge(s("branch_hi"), n + 1)
            tt(branch_lo[b][:, :, tile], (zT, onT)[b][:, :, tile], branch_hi[b][:, :, tile].bitcast(F32), ALU.subtract)\
                .then_inc(s("branch_split"), 1)
        dve.wait_ge(s("g_free"), 32 + 4)
        with dve.Fori(0, 2) as n:
            for c in range(2):
                cols = slice(c * G1, (c + 1) * G1)
                for b in range(2):
                    for t in range(NT):
                        done = 16 * n + 8 * c + 4 * b + t + 1
                        dve.wait_ge(s("br_proj"), done)
                        g = gate[:, bass.ds(n + 2 * b, 1), t, cols].rearrange("p o c -> p (o c)")
                        tt(g, ps[:, 4 * b + t, 0:G1], g, ALU.mult).then_inc(s("br_free"), 1)
                        if b == 1:
                            g0 = gate[:, bass.ds(n, 1), t, cols].rearrange("p o c -> p (o c)")
                            dve.wait_ge(s("br_free"), done + 8)
                            tt(g0, g0, g, ALU.add).then_inc(s("m_ready"), 1)
        dve.wait_ge(s("row_copied"), 8)
        dve.wait_ge(s("ld_x2"), 16)

        def residual(t):
            dve.wait_ge(s("mix_rms"), t + 1)
            dve.reciprocal(rstd[:, t:t + 1], rms[:, t:t + 1])
            dve.drain()
            stt(f_sb[:, t, :], f_sb[:, t, :], rstd[:, t:t + 1], row_ga, ALU.mult, ALU.mult)
            dve.drain()
            tt(x1[:, t, :], x1[:, t, :], f_sb[:, t, :], ALU.add).then_inc(s("x1_ready"), 1)
            dve.wait_ge(s("x1_rms"), t + 1)
            dve.reciprocal(rstd[:, 4 + t:5 + t], rms[:, 4 + t:5 + t])
            dve.drain()
            stt(f_sb[:, t, :], x1[:, t, :], rstd[:, 4 + t:5 + t], row_af, ALU.mult, ALU.mult)
            dve.drain()
            tt(f_sb[:, t, :], f_sb[:, t, :], row_bf, ALU.add).then_inc(s("f_ready"), 1)

        def topk(h, t, first=False):
            m = NT * h + t
            dve.drain()
            if first:
                dve.wait_ge(s("scored"), t + 1)
            else:
                if t == 0:
                    dve.wait_ge(s("scored"), h + NT)
                elif t == 2:
                    dve.wait_ge(s("scored"), NT)
                dve.wait_ge(s("v_used"), TOPK * (m - 3) + V_CREDIT)
            stand(dve, "dve")
            sc = [ps[:, 6 + a, t * P:(t + 1) * P] for a in range(2)]
            for a in range(2):
                dve.max(top_v[:, a, 0:8], sc[a])
            dve.drain()
            for a in range(2):
                dve.max_index(top_i[:, a, 0:8], top_v[:, a, 0:8], sc[a])
                dve.match_replace(left[:, a, :], top_v[:, a, 0:8], sc[a], NEG)
            dve.drain()
            for a in range(2):
                dve.max(top_v[:, a, 8:16], left[:, a, :])
            dve.drain()
            for a in range(2):
                dve.max_index(top_i[:, a, 8:16], top_v[:, a, 8:16], left[:, a, :])
            tt(cand.rearrange("p (i j) -> p i j", i=TOPK), top_v[:, 0, :].unsqueeze(2).to_broadcast([P, TOPK, TOPK]),
               top_v[:, 1, :].unsqueeze(1).to_broadcast([P, TOPK, TOPK]), ALU.add)
            dve.drain()
            dve.sem_inc(s("topk_done"), 1)
            cp(top_f, top_i)
            dve.max(fin_v[:, 0:8], cand)
            dve.drain()
            dve.max_index(pos[:, 0:8], fin_v[:, 0:8], cand)
            dve.match_replace(cand2, fin_v[:, 0:8], cand, NEG)
            dve.drain()
            dve.max(fin_v[:, 8:16], cand2)
            dve.drain()
            dve.max_index(pos[:, 8:16], fin_v[:, 8:16], cand2)
            ts(logit[:, t, :], fin_v, fin_v[:, 0:1], None, ALU.subtract)
            dve.drain()
            ts(ab_i[:, 0, :], pos, 4, None, ALU.logical_shift_right)
            ts(ab_i[:, 1, :], pos, 15, None, ALU.bitwise_and)
            dve.drain()
            cp(ab_f, ab_i.rearrange("p a n -> p (a n)"))
            dve.drain()
            hot3 = hot.rearrange("p (m j) -> p m j", j=TOPK)
            hot4 = hot.rearrange("p (a m j) -> p a m j", a=2, j=TOPK)
            tt(hot3, ab_f.unsqueeze(2).to_broadcast([P, 32, TOPK]), iota16.unsqueeze(1).to_broadcast([P, 32, TOPK]), ALU.is_equal)
            dve.drain()
            tt(hot4, hot4, top_f.unsqueeze(2).to_broadcast([P, 2, TOPK, TOPK]), ALU.mult)
            dve.drain()
            dve.tensor_reduce(ij.rearrange("p a n -> p (a n)"), hot3, AX.X, ALU.add)
            dve.drain()
            stt(idxs[:, t, :], ij[:, 0, :], float(PK), ij[:, 1, :], ALU.mult, ALU.add).then_inc(s("idx_ready"), 1)

        def dot_products(h, t, half):
            n, b = NT * h + t, t % 2
            dve.drain()
            for e in range(half * USLOTS, (half + 1) * USLOTS):
                dve.wait_ge(s(f"u_in_{e % USLOTS}"), 32 * n + 16 * (e // USLOTS) + 16)
                dve.tensor_tensor_reduce(uslot[:, e % USLOTS, :], uslot[:, e % USLOTS, :], f_sb[:, t, :], 1.0, 0.0,
                                         ALU.mult, ALU.add, dots[:, b, e:e + 1]).then_inc(s("u_used"), 1)

        def weights(h, t):
            n, b = NT * h + t, t % 2
            dve.wait_ge(s("gelu_done"), n + 1)
            dve.reciprocal(sinv[:, b:b + 1], ssum[:, b:b + 1])
            dve.drain()
            stt(wgt[:, b, :], gel[:, b, :], sinv[:, b:b + 1], soft[:, b, :], ALU.mult, ALU.mult).then_inc(s("w_ready"), 1)

        def unit(h, t, ahead=True, add=True):
            n = NT * h + t
            for half in range(2):
                dot_products(h, t, half)
            if ahead:
                topk(h + (t + 2) // NT, (t + 2) % NT)
            if add:
                dve.wait_ge(s("v_used"), TOPK * (n - 1) + V_CREDIT)
                accumulate(t + 2)
            weights(h, t)

        def accumulate(t):
            a3 = acc[:, t % NT, :].rearrange("p (b n) -> p b n", b=2)
            return tt(a3, a3, ps[:, 2 * (t % 2):2 * (t % 2) + 2, :], ALU.add).then_inc(s("acc_added"), 1)

        dve.drain()
        dve.wait_ge(s("m_copied"), NT)
        dve.sem_inc(s("u_used"), USLOTS)
        residual(0)
        residual(1)
        topk(0, 0, first=True)
        residual(2)
        topk(0, 1, first=True)
        dot_products(0, 0, 0)
        residual(3)
        dot_products(0, 0, 1)
        dve.sem_inc(s("acc_added"), 2)
        weights(0, 0)
        topk(0, 2)
        dve.memset(acc, 0.0)
        unit(0, 1, add=False)
        unit(0, 2)
        unit(0, 3)
        with dve.Fori(1, PH - 1) as h:
            for t in range(NT):
                unit(h, t)

        def finish(t):
            dve.wait_ge(s("y_rms"), t + 1)
            dve.reciprocal(rstd[:, t:t + 1], rms[:, t:t + 1])
            dve.drain()
            stt(acc[:, t, :], acc[:, t, :], rstd[:, t:t + 1], row_gf, ALU.mult, ALU.mult)
            dve.drain()
            tt(acc[:, t, :], acc[:, t, :], x1[:, t, :], ALU.add).then_inc(s("y_ready"), 1)

        for t in range(NT):
            unit(PH - 1, t, ahead=t < 2)
        finish(0)
        finish(1)
        for t in range(2):
            dve.wait_ge(s("v_used"), TOPK * (NT * PH - 1 + t) + V_CREDIT)
            accumulate(t + 2)
            finish(t + 2)

    @block.gpsimd
    def _(pool):
        def rows_of(table, dst, n, t, half, kind, need):
            for k in range(USLOTS):
                e = half * USLOTS + k
                pool.wait_ge(s(kind + "_used"), TOPK * n + e + 1 + need)
                stand(pool, "pool")
                pool.indirect_dma_start(out=dst[:, k, :], out_offset=None, in_=table,
                                        in_offset=bass.IndirectOffsetOnAxis(ap=idxs[:, t, e:e + 1], axis=0))\
                    .then_inc(s(f"{kind}_in_{k}"), 16)

        def u_rows(n, t, half):
            if half == 0:
                pool.wait_ge(s("idx_ready"), n + 1)
                stand(pool, "pool")
            rows_of(peer_u[:, :], uslot, n, t, half, "u", 0)

        def v_rows(n, t, half):
            rows_of(peer_v[:, :], vslot, n, t, half, "v", V_CREDIT - VSLOTS)

        def split(raw, hi, lo, name):
            stand(pool, "pool")
            for h, r in zip(hi, raw):
                pool.tensor_copy(h, r)
            pool.drain()
            for n, (h, r) in enumerate(zip(hi, raw)):
                last = pool.tensor_tensor(lo[n], r, h.bitcast(F32), ALU.subtract)
            last.then_inc(s(name), 1)

        def in_halves(ap):
            return [ap[:, 0:KT // 2, :], ap[:, KT // 2:KT, :]]

        def ret_split(h, j):
            raw, lo, hi = slots[j]
            pool.wait_ge(s(f"ret_w_{j}"), (32 if j == 0 else 16) * (h + 1))
            split([raw], [hi], [lo], f"ret_split_{j}")

        ret_split(0, 0)
        ret_split(0, 2)
        with pool.Fori(1, RH) as h:
            for j in range(3):
                ret_split(h, j)
        with pool.Fori(0, DH // 2) as i:
            for b in range(2):
                pool.wait_ge(s(f"diff_w_{b}"), 48 * (i + 1))
                split(in_halves(d_raw[b]), d_hi[b], in_halves(d_lo[b]), "diff_split")
        for b, hi in enumerate((slots[0][2], gate1_hi)):
            pool.wait_ge(s(f"gate_w_{b}"), 16)
            split([gate_raw[b]], [hi], [slots[b][1]], "gate_split")
        for n in range(2, 8):
            pool.wait_ge(s("gate_hi"), n - 1)
            pool.tensor_tensor(slots[n % 2][1], gate_raw[n % 2], slots[n % 2][2].bitcast(F32), ALU.subtract)\
                .then_inc(s("gate_split"), 1)
        for n in range(8):
            pool.wait_ge(s("br_hi"), n + 1)
            pool.tensor_tensor(slots[n % 2][1], branch_raw[n % 2], slots[n % 2][2].bitcast(F32), ALU.subtract)\
                .then_inc(s("br_split"), 1)
        u_rows(0, 0, 0)
        v_rows(0, 0, 0)
        u_rows(0, 0, 1)
        u_rows(1, 1, 0)
        v_rows(0, 0, 1)
        u_rows(1, 1, 1)
        with pool.Fori(0, PH - 1) as h:
            for t in range(1, NT + 1):
                for half in range(2):
                    u_rows(NT * h + t + 1, (t + 1) % NT, half)
                    v_rows(NT * h + t, t % NT, half)
        for t in range(1, NT):
            n = NT * (PH - 1) + t
            for half in range(2):
                if t + 1 < NT:
                    u_rows(n + 1, t + 1, half)
                v_rows(n, t, half)

    es.close()


def kernel(**inputs):
    import concourse.bacc as bacc
    from concourse.bass_utils import run_bass_kernel_spmd

    nc = bacc.Bacc("TRN2", target_bir_lowering=False, num_devices=1)
    a = {k: np.asarray(v) for k, v in inputs.items()}
    small, dist, rope = shape_constants()
    blocks = [a[k][0].reshape(-1, P) for k in ("b_mod", "pre_mix_g", "post_mix_g", "pre_ffn_g", "post_ffn_g",
                                               "ret_gn_g", "diff_gn_g")]
    given = {
        "x": a["x"][0], "ctx": a["ctx"][0], "c_pair": np.stack([a["c"][0], a["c_ctx"]], axis=-1),
        "w_mod": a["w_mod"][0], "rows": np.concatenate(blocks, axis=0), "w_in": a["w_in"][0],
        "decays": np.concatenate([a["ret_decay_fwd"][0], a["ret_decay_bwd"][0]]),
        "lam": a["diff_lambda"][0].reshape(-1), "w_br_ret": a["w_br_ret"][0], "w_br_diff": a["w_br_diff"][0],
        "w_out": a["w_out"][0], "w_q": a["peer_w_q"][0], "keys": a["peer_sub_keys"][0],
        "peer_u": a["peer_u"][0], "peer_v": a["peer_v"][0], "small": small, "dist": dist, "rope": rope,
    }
    arrays, args = {}, {}
    for name, value in given.items():
        arrays["in_" + name] = np.ascontiguousarray(value)
        args[name] = nc.dram_tensor("in_" + name, value.shape, mybir.dt.from_np(value.dtype), kind="ExternalInput").ap()
    out = nc.dram_tensor("out_y", (T, D), F32, kind="ExternalOutput").ap()
    build(nc, out=out, **args)
    result = run_bass_kernel_spmd(nc, [arrays], core_ids=[0])
    return result.results[0]["out_y"].reshape(1, T, D)
```
